# Optimizing a Trainium2 kernel written in Bass

```python
import jax, jax.numpy as jnp
from jax import lax
import numpy as np

D_MODEL = 1024
BATCH = 1
SEQ = 256
DEPTH = 1

N_META = 16
EPS = 1e-6
N_BRANCH = 4
POOL_WINDOWS = (2, 4, 8, 16)
POOL_GROUP = 64
POOL_W = POOL_GROUP * 4
MLA_HEADS = 8
QK_NOPE = 64
QK_ROPE = 32
V_DIM = 64
Q_RANK = 256
KV_RANK = 128
ROPE_THETA = 10000.0
MLA_W = MLA_HEADS * V_DIM
Q_BLOCK = 128
CONF_W = 256
CONF_K = 31
SC_W = 256
SC_K = 3

IN_SPLITS = (POOL_W, POOL_W,
             Q_RANK, KV_RANK, QK_ROPE, MLA_W,
             2 * CONF_W, CONF_W,
             3 * SC_W, SC_W,
             N_BRANCH * D_MODEL)
IN_W = sum(IN_SPLITS)


def rms_norm(x, g):
    xf = x.astype(jnp.float32)
    y = xf * lax.rsqrt(jnp.mean(xf * xf, axis=-1, keepdims=True) + EPS)
    return (y * g.astype(jnp.float32)).astype(x.dtype)

def layer_norm(x, g, b):
    xf = x.astype(jnp.float32)
    mu = jnp.mean(xf, axis=-1, keepdims=True)
    var = jnp.mean(jnp.square(xf - mu), axis=-1, keepdims=True)
    y = (xf - mu) * lax.rsqrt(var + EPS)
    return (y * g.astype(jnp.float32) + b.astype(jnp.float32)).astype(x.dtype)

def split_cols(z):
    idx = [int(i) for i in np.cumsum(IN_SPLITS)[:-1]]
    return jnp.split(z, idx, axis=-1)

def causal_dwconv(u, w):
    width, c = w.shape
    up = jnp.pad(u, ((0, 0), (width - 1, 0), (0, 0)))
    return lax.conv_general_dilated(up, w[:, None, :].astype(u.dtype), window_strides=(1,),
                                    padding='VALID', dimension_numbers=('NWC', 'WIO', 'NWC'),
                                    feature_group_count=c)

def rope_tables(n_pos, dim, dtype):
    inv = 1.0 / (ROPE_THETA ** (jnp.arange(0, dim, 2, dtype=jnp.float32) / dim))
    ang = jnp.arange(n_pos, dtype=jnp.float32)[:, None] * inv[None, :]
    return jnp.cos(ang).astype(dtype), jnp.sin(ang).astype(dtype)

def apply_rope(t, cos, sin):
    t1, t2 = jnp.split(t, 2, axis=-1)
    return jnp.concatenate([t1 * cos - t2 * sin, t1 * sin + t2 * cos], axis=-1)

def pool_mixer(v, w_group, scale):
    b_, l_, _ = v.shape
    vf = v.astype(jnp.float32)
    groups = jnp.split(vf, len(POOL_WINDOWS), axis=-1)
    pos = jnp.arange(l_)
    outs = []
    for g, w in zip(groups, POOL_WINDOWS):
        cs = jnp.cumsum(g, axis=1)
        lag = jnp.pad(cs, ((0, 0), (w, 0), (0, 0)))[:, :l_]
        cnt = jnp.minimum(pos + 1, w).astype(jnp.float32)[None, :, None]
        outs.append((cs - lag) / cnt - g)
    p = jnp.stack(outs, axis=2).astype(v.dtype)
    y = jnp.einsum('blgc,gcd->blgd', p, w_group).reshape(b_, l_, POOL_W)
    return y * scale

def mla_attention(c_q, c_kv, k_rope, q_norm_g, w_uq, kv_norm_g, w_ukv, cos, sin):
    b_, l_, _ = c_q.shape
    q = (rms_norm(c_q, q_norm_g) @ w_uq).reshape(b_, l_, MLA_HEADS, QK_NOPE + QK_ROPE)
    q_nope, q_rope = jnp.split(q, [QK_NOPE], axis=-1)
    q_rope = apply_rope(q_rope, cos[:, None, :], sin[:, None, :])
    kv = (rms_norm(c_kv, kv_norm_g) @ w_ukv).reshape(b_, l_, MLA_HEADS, QK_NOPE + V_DIM)
    k_nope, v = jnp.split(kv, [QK_NOPE], axis=-1)
    k_rope = apply_rope(k_rope, cos, sin)
    k = jnp.concatenate([k_nope, jnp.broadcast_to(k_rope[:, :, None, :], (b_, l_, MLA_HEADS, QK_ROPE))], axis=-1)
    qf = jnp.concatenate([q_nope, q_rope], axis=-1) * ((QK_NOPE + QK_ROPE) ** -0.5)
    n_blk = -(-l_ // Q_BLOCK)
    lp = n_blk * Q_BLOCK
    pad = ((0, 0), (0, lp - l_), (0, 0), (0, 0))
    qf, k, v = jnp.pad(qf, pad), jnp.pad(k, pad), jnp.pad(v, pad)
    k_pos = jnp.arange(lp)
    q_blocks = qf.reshape(b_, n_blk, Q_BLOCK, MLA_HEADS, QK_NOPE + QK_ROPE).transpose(1, 0, 2, 3, 4)

    def attend(args):
        qb, i = args
        s = jnp.einsum('bqhd,bkhd->bhqk', qb, k).astype(jnp.float32)
        q_pos = i * Q_BLOCK + jnp.arange(Q_BLOCK)
        s = jnp.where(k_pos[None, :] <= q_pos[:, None], s, -jnp.inf)
        p = jax.nn.softmax(s, axis=-1).astype(v.dtype)
        return jnp.einsum('bhqk,bkhd->bqhd', p, v)

    o = lax.map(attend, (q_blocks, jnp.arange(n_blk)))
    return o.transpose(1, 0, 2, 3, 4).reshape(b_, lp, MLA_W)[:, :l_]

def conformer_conv(u, w_dw, b_dw, ln_g, ln_b):
    a, gate = jnp.split(u, 2, axis=-1)
    z = a * jax.nn.sigmoid(gate)
    z = causal_dwconv(z, w_dw) + b_dw
    z = layer_norm(z, ln_g, ln_b)
    return jax.nn.silu(z)

def short_conv(bcx, w_dw):
    bg, cg, xv = jnp.split(bcx, 3, axis=-1)
    return bg * causal_dwconv(cg * xv, w_dw)

def first_inputs(seed: int = 0) -> dict:
    key = jax.random.key(seed)
    ks = jax.random.split(key, 24)
    f32 = jnp.float32

    def nrm(k, shape, fan_in):
        return jax.random.normal(k, shape, f32) * (fan_in ** -0.5)

    def gain(k, shape):
        return 1.0 + 0.05 * jax.random.normal(k, shape, f32)

    def bias(k, shape):
        return 0.02 * jax.random.normal(k, shape, f32)

    return {
        "x": jax.random.normal(ks[0], (BATCH, SEQ, D_MODEL), f32),
        "meta_tokens": jax.random.normal(ks[1], (N_META, D_MODEL), f32),
        "pre_norm_g": gain(ks[2], (DEPTH, D_MODEL)),
        "w_in": nrm(ks[3], (DEPTH, D_MODEL, IN_W), D_MODEL),
        "gate_bias": bias(ks[4], (DEPTH, N_BRANCH * D_MODEL)),
        "pool_w": nrm(ks[5], (DEPTH, 4, POOL_GROUP, POOL_GROUP), POOL_GROUP),
        "pool_scale": gain(ks[6], (DEPTH, POOL_W)),
        "w_out_pool": nrm(ks[7], (DEPTH, POOL_W, D_MODEL), POOL_W),
        "q_norm_g": gain(ks[8], (DEPTH, Q_RANK)),
        "w_uq": nrm(ks[9], (DEPTH, Q_RANK, MLA_HEADS * (QK_NOPE + QK_ROPE)), Q_RANK),
        "kv_norm_g": gain(ks[10], (DEPTH, KV_RANK)),
        "w_ukv": nrm(ks[11], (DEPTH, KV_RANK, MLA_HEADS * (QK_NOPE + V_DIM)), KV_RANK),
        "w_out_mla": nrm(ks[12], (DEPTH, MLA_W, D_MODEL), MLA_W),
        "conf_dw_w": nrm(ks[13], (DEPTH, CONF_K, CONF_W), CONF_K),
        "conf_dw_b": bias(ks[14], (DEPTH, CONF_W)),
        "conf_ln_g": gain(ks[15], (DEPTH, CONF_W)),
        "conf_ln_b": bias(ks[16], (DEPTH, CONF_W)),
        "w_out_conf": nrm(ks[17], (DEPTH, CONF_W, D_MODEL), CONF_W),
        "sc_dw_w": nrm(ks[18], (DEPTH, SC_K, SC_W), SC_K),
        "w_out_sc": nrm(ks[19], (DEPTH, SC_W, D_MODEL), SC_W),
        "w_o": nrm(ks[20], (DEPTH, D_MODEL, D_MODEL), D_MODEL),
        "post_norm_g": gain(ks[21], (DEPTH, D_MODEL)),
    }

def first_block(x, meta_tokens, pre_norm_g, w_in, gate_bias, pool_w, pool_scale, w_out_pool,
              q_norm_g, w_uq, kv_norm_g, w_ukv, w_out_mla, conf_dw_w, conf_dw_b, conf_ln_g,
              conf_ln_b, w_out_conf, sc_dw_w, w_out_sc, w_o, post_norm_g):
    b_ = x.shape[0]
    meta = jnp.broadcast_to(meta_tokens[None].astype(x.dtype), (b_, N_META, D_MODEL))
    h_res = jnp.concatenate([meta, x], axis=1)
    l_ = h_res.shape[1]
    cos, sin = rope_tables(l_, QK_ROPE, x.dtype)

    for i in range(DEPTH):
        h = rms_norm(h_res, pre_norm_g[i])
        z = h @ w_in[i]
        (pv, pg, cq, ckv, kr, mg, cu, cg, sbcx, sg, gl) = split_cols(z)

        y_a = (pool_mixer(pv, pool_w[i], pool_scale[i]) * jax.nn.silu(pg)) @ w_out_pool[i]
        y_b = (mla_attention(cq, ckv, kr, q_norm_g[i], w_uq[i], kv_norm_g[i], w_ukv[i], cos, sin)
               * jax.nn.silu(mg)) @ w_out_mla[i]
        y_c = (conformer_conv(cu, conf_dw_w[i], conf_dw_b[i], conf_ln_g[i], conf_ln_b[i])
               * jax.nn.silu(cg)) @ w_out_conf[i]
        y_d = (short_conv(sbcx, sc_dw_w[i]) * jax.nn.silu(sg)) @ w_out_sc[i]

        gts = jax.nn.sigmoid(gl + gate_bias[i]).reshape(b_, l_, N_BRANCH, D_MODEL)
        m = (gts[:, :, 0] * y_a + gts[:, :, 1] * y_b + gts[:, :, 2] * y_c + gts[:, :, 3] * y_d)
        h_res = h_res + rms_norm(m @ w_o[i], post_norm_g[i])

    return h_res[:, N_META:]


DEPTH_2 = 2

N_MIXERS = 4
HEAD_DIM = 128
CHUNK = 64
GLA_HEADS = 4
GLA_DK = D_MODEL // 2 // GLA_HEADS
GLA_DV = D_MODEL // GLA_HEADS
GLA_GATE_RANK = 16
GLA_GATE_NORMALIZER = 16.0
GLA_COLS = (GLA_HEADS * GLA_DK, GLA_HEADS * GLA_DK, GLA_HEADS * GLA_DV, GLA_HEADS * GLA_DV, GLA_GATE_RANK)
MOBA_HEADS = D_MODEL // HEAD_DIM
MOBA_BLOCK = 256
MOBA_TOPK = 3
MOBA_QCHUNK = 16
MOBA_COLS = (D_MODEL, D_MODEL, D_MODEL)
ROPE_THETA_2 = 500000.0
ROPE_DIM = HEAD_DIM // 4
NEG_INF = -1e30
GDN_HEADS = D_MODEL // HEAD_DIM
GDN_DK = HEAD_DIM
GDN_WIDTH = GDN_HEADS * GDN_DK
GDN_CONV = 4
GDN_COLS = (3 * GDN_WIDTH, GDN_WIDTH, GDN_HEADS, GDN_HEADS)
HGRN_HEADS = 8
HGRN_F_DIM = 128
HGRN_F = HGRN_HEADS * HGRN_F_DIM
HGRN_COLS = (HGRN_F, HGRN_F, D_MODEL, D_MODEL)
FFN_HIDDEN = -(-8 * D_MODEL // (3 * 256)) * 256
DEEPNORM_ALPHA = (2.0 * DEPTH_2) ** 0.25
DEEPNORM_BETA = (8.0 * DEPTH_2) ** -0.25
N_GLA = len(range(0, DEPTH_2, N_MIXERS))
N_MOBA = len(range(1, DEPTH_2, N_MIXERS))
N_GDN = len(range(2, DEPTH_2, N_MIXERS))
N_HGRN = len(range(3, DEPTH_2, N_MIXERS))


def split_cols_2(x, cols):
    return jnp.split(x, [int(c) for c in np.cumsum(cols)[:-1]], axis=-1)

def to_heads(x, h):
    b, s, _ = x.shape
    return x.reshape(b, s, h, -1).transpose(0, 2, 1, 3)

def from_heads(x):
    b, h, s, d = x.shape
    return x.transpose(0, 2, 1, 3).reshape(b, s, h * d)

def layer_norm_2(x, g, b, eps=1e-5):
    xf = x.astype(jnp.float32)
    mu = jnp.mean(xf, -1, keepdims=True)
    var = jnp.mean(jnp.square(xf - mu), -1, keepdims=True)
    return ((xf - mu) * lax.rsqrt(var + eps) * g + b).astype(x.dtype)

def rms_norm_2(x, g, eps=1e-6):
    xf = x.astype(jnp.float32)
    return (xf * lax.rsqrt(jnp.mean(xf * xf, -1, keepdims=True) + eps) * g).astype(x.dtype)

def l2_normalize(x, eps=1e-6):
    xf = x.astype(jnp.float32)
    return (xf * lax.rsqrt(jnp.sum(xf * xf, -1, keepdims=True) + eps)).astype(x.dtype)

def partial_rope(x, positions):
    inv_freq = ROPE_THETA_2 ** (-jnp.arange(0, ROPE_DIM, 2, dtype=jnp.float32) / ROPE_DIM)
    ang = positions.astype(jnp.float32)[:, None, :, None] * inv_freq
    cos, sin = jnp.cos(ang), jnp.sin(ang)
    xr = x[..., :ROPE_DIM].astype(jnp.float32)
    x1, x2 = xr[..., :ROPE_DIM // 2], xr[..., ROPE_DIM // 2:]
    rot = jnp.concatenate([x1 * cos - x2 * sin, x2 * cos + x1 * sin], -1).astype(x.dtype)
    return jnp.concatenate([rot, x[..., ROPE_DIM:]], -1)

def causal_depthwise_conv(x, w):
    k, c = w.shape
    return lax.conv_general_dilated(x, w.reshape(k, 1, c).astype(x.dtype), window_strides=(1,),
                                    padding=((k - 1, 0),), dimension_numbers=("NWC", "WIO", "NWC"),
                                    feature_group_count=c)

def swiglu_ffn(x, w_gu, w_down):
    gate, up = jnp.split(x @ w_gu, 2, axis=-1)
    return (jax.nn.silu(gate) * up) @ w_down

def chunk_gla(q, k, v, log_g):
    b, h, s, dk = q.shape
    dv = v.shape[-1]
    n = s // CHUNK
    f32 = jnp.float32
    q, k, log_g = (t.astype(f32).reshape(b, h, n, CHUNK, dk) for t in (q, k, log_g))
    v = v.astype(f32).reshape(b, h, n, CHUNK, dv)
    cum = jnp.cumsum(log_g, axis=3)
    last = cum[:, :, :, -1:, :]
    q_dec = q * jnp.exp(cum)
    k_inv = k * jnp.exp(-cum)
    k_to_end = k * jnp.exp(last - cum)
    causal = jnp.tril(jnp.ones((CHUNK, CHUNK), bool))
    scores = jnp.where(causal, jnp.einsum("bhnik,bhnjk->bhnij", q_dec, k_inv), 0.0)
    o_intra = jnp.einsum("bhnij,bhnjv->bhniv", scores, v)
    upd = jnp.einsum("bhnjk,bhnjv->bhnkv", k_to_end, v)
    decay = jnp.exp(last[:, :, :, 0, :])

    def step(state, inp):
        dec, u = inp
        return state * dec[..., None] + u, state

    _, states = lax.scan(step, jnp.zeros((b, h, dk, dv), f32),
                         (jnp.moveaxis(decay, 2, 0), jnp.moveaxis(upd, 2, 0)))
    states = jnp.moveaxis(states, 0, 2)
    o_inter = jnp.einsum("bhnik,bhnkv->bhniv", q_dec, states)
    return (o_intra + o_inter).reshape(b, h, s, dv)

def chunk_gated_delta(q, k, v, g, beta):
    b, h, s, dk = q.shape
    dv = v.shape[-1]
    n = s // CHUNK
    f32 = jnp.float32
    q = q.astype(f32).reshape(b, h, n, CHUNK, dk)
    k = k.astype(f32).reshape(b, h, n, CHUNK, dk)
    v = v.astype(f32).reshape(b, h, n, CHUNK, dv)
    g = g.astype(f32).reshape(b, h, n, CHUNK)
    beta = beta.astype(f32).reshape(b, h, n, CHUNK)
    cum = jnp.cumsum(g, axis=-1)
    incl = jnp.tril(jnp.ones((CHUNK, CHUNK), bool))
    strict = jnp.tril(jnp.ones((CHUNK, CHUNK), bool), -1)
    diff = cum[..., :, None] - cum[..., None, :]
    decay = jnp.where(incl, jnp.exp(jnp.where(incl, diff, 0.0)), 0.0)
    k_beta = k * beta[..., None]
    lower = jnp.where(strict, jnp.einsum("bhnid,bhnjd->bhnij", k_beta, k) * decay, 0.0)
    eye = jnp.eye(CHUNK, dtype=f32)
    rhs = jnp.concatenate([v * beta[..., None], k_beta * jnp.exp(cum)[..., None]], axis=-1)
    sol = lax.linalg.triangular_solve(lower + eye, rhs, left_side=True, lower=True)
    u, w = sol[..., :dv], sol[..., dv:]
    qk = jnp.einsum("bhnid,bhnjd->bhnij", q, k) * decay
    q_dec = q * jnp.exp(cum)[..., None]
    k_end = k * jnp.exp(cum[..., -1:] - cum)[..., None]
    chunk_decay = jnp.exp(cum[..., -1])

    def step(state, inp):
        u_c, w_c, qk_c, qd_c, ke_c, dec_c = inp
        v_new = u_c - jnp.einsum("bhck,bhkv->bhcv", w_c, state)
        o_c = jnp.einsum("bhck,bhkv->bhcv", qd_c, state) + jnp.einsum("bhij,bhjv->bhiv", qk_c, v_new)
        state = state * dec_c[..., None, None] + jnp.einsum("bhck,bhcv->bhkv", ke_c, v_new)
        return state, o_c

    xs = tuple(jnp.moveaxis(t, 2, 0) for t in (u, w, qk, q_dec, k_end, chunk_decay))
    _, o = lax.scan(step, jnp.zeros((b, h, dk, dv), f32), xs)
    return jnp.moveaxis(o, 0, 2).reshape(b, h, s, dv)

def moba_attention(q, k, v):
    b, h, s, d = q.shape
    nb = -(-s // MOBA_BLOCK)
    s_pad = nb * MOBA_BLOCK
    pad = ((0, 0), (0, 0), (0, s_pad - s), (0, 0))
    q, k, v = (jnp.pad(t, pad) for t in (q, k, v))
    scale = HEAD_DIM ** -0.5
    k_blocks = k.reshape(b, h, nb, MOBA_BLOCK, d)
    v_blocks = v.reshape(b, h, nb, MOBA_BLOCK, d)
    k_mean = jnp.mean(k_blocks.astype(jnp.float32), axis=3)
    gate = jnp.einsum("bhsd,bhnd->bhsn", q.astype(jnp.float32), k_mean)
    q_block = jnp.arange(s_pad) // MOBA_BLOCK
    past = jnp.arange(nb)[None, :] < q_block[:, None]
    gate = jnp.where(past, gate, NEG_INF)
    n_sel = min(MOBA_TOPK, nb)
    _, sel = lax.top_k(gate, n_sel)
    bi = jnp.arange(b)[:, None, None, None]
    hi = jnp.arange(h)[None, :, None, None]

    def chunk_fn(ci):
        q0 = ci * MOBA_QCHUNK
        blk = q0 // MOBA_BLOCK
        q_c = lax.dynamic_slice_in_dim(q, q0, MOBA_QCHUNK, axis=2)
        k_own = lax.dynamic_slice_in_dim(k, blk * MOBA_BLOCK, MOBA_BLOCK, axis=2)
        v_own = lax.dynamic_slice_in_dim(v, blk * MOBA_BLOCK, MOBA_BLOCK, axis=2)
        sel_c = lax.dynamic_slice_in_dim(sel, q0, MOBA_QCHUNK, axis=2)
        k_sel = k_blocks[bi, hi, sel_c]
        v_sel = v_blocks[bi, hi, sel_c]
        own = jnp.einsum("bhqd,bhkd->bhqk", q_c, k_own, preferred_element_type=jnp.float32) * scale
        q_pos = q0 + jnp.arange(MOBA_QCHUNK)
        k_pos = blk * MOBA_BLOCK + jnp.arange(MOBA_BLOCK)
        own = jnp.where(k_pos[None, :] <= q_pos[:, None], own, NEG_INF)
        far = jnp.einsum("bhqd,bhqnkd->bhqnk", q_c, k_sel, preferred_element_type=jnp.float32) * scale
        far = jnp.where((jnp.arange(n_sel) < blk)[:, None], far, NEG_INF)
        logits = jnp.concatenate([own, far.reshape(b, h, MOBA_QCHUNK, n_sel * MOBA_BLOCK)], axis=-1)
        p = jax.nn.softmax(logits, axis=-1).astype(v.dtype)
        p_own = p[..., :MOBA_BLOCK]
        p_far = p[..., MOBA_BLOCK:].reshape(b, h, MOBA_QCHUNK, n_sel, MOBA_BLOCK)
        return (jnp.einsum("bhqk,bhkd->bhqd", p_own, v_own)
                + jnp.einsum("bhqnk,bhqnkd->bhqd", p_far, v_sel))

    out = lax.map(chunk_fn, jnp.arange(s_pad // MOBA_QCHUNK))
    out = jnp.moveaxis(out, 0, 2).reshape(b, h, s_pad, d)
    return out[:, :, :s]

def gla_mixer(x, w_in, w_gk, b_gk, norm_g, w_out):
    q, k, v, g, gk_low = split_cols_2(x @ w_in, GLA_COLS)
    log_a = jax.nn.log_sigmoid((gk_low @ w_gk + b_gk).astype(jnp.float32)) / GLA_GATE_NORMALIZER
    q = to_heads(q, GLA_HEADS) * (GLA_DK ** -0.5)
    o = chunk_gla(q, to_heads(k, GLA_HEADS), to_heads(v, GLA_HEADS), to_heads(log_a, GLA_HEADS))
    o = from_heads(rms_norm_2(o.astype(x.dtype), norm_g)) * jax.nn.silu(g)
    return o @ w_out

def moba_mixer(x, positions, w_in, w_out):
    q, k, v = split_cols_2(x @ w_in, MOBA_COLS)
    q = partial_rope(to_heads(q, MOBA_HEADS), positions)
    k = partial_rope(to_heads(k, MOBA_HEADS), positions)
    o = moba_attention(q, k, to_heads(v, MOBA_HEADS))
    return from_heads(o) @ w_out

def gdn_mixer(x, w_in, conv_w, a_log, dt_bias, norm_g, w_out):
    qkv, z, a, b_logit = split_cols_2(x @ w_in, GDN_COLS)
    qkv = jax.nn.silu(causal_depthwise_conv(qkv, conv_w))
    q, k, v = jnp.split(qkv, 3, axis=-1)
    q = l2_normalize(to_heads(q, GDN_HEADS)) * (GDN_DK ** -0.5)
    k = l2_normalize(to_heads(k, GDN_HEADS))
    v = to_heads(v, GDN_HEADS)
    beta = jax.nn.sigmoid(b_logit.astype(jnp.float32)).transpose(0, 2, 1)
    g = (-jnp.exp(a_log.astype(jnp.float32))
         * jax.nn.softplus(a.astype(jnp.float32) + dt_bias)).transpose(0, 2, 1)
    o = chunk_gated_delta(q, k, v, g, beta).astype(x.dtype)
    o = from_heads(rms_norm_2(o, norm_g)) * jax.nn.silu(z)
    return o @ w_out

def hgrn2_mixer(x, lb, w_in, norm_g, w_out):
    q, f_logit, i, g = split_cols_2(x @ w_in, HGRN_COLS)
    f_logit = f_logit.astype(jnp.float32)
    forget = lb + (1.0 - lb) * jax.nn.sigmoid(f_logit)
    k_in = (1.0 - lb) * jax.nn.sigmoid(-f_logit)
    o = chunk_gla(to_heads(q, HGRN_HEADS), to_heads(k_in, HGRN_HEADS), to_heads(i, HGRN_HEADS),
                  to_heads(jnp.log(forget), HGRN_HEADS))
    o = from_heads(rms_norm_2(o.astype(x.dtype), norm_g)) * jax.nn.silu(g)
    return o @ w_out

def second_inputs(seed: int = 0) -> dict:
    key = jax.random.key(seed)
    ks = iter(jax.random.split(key, 32))
    f32 = jnp.float32

    def normal(shape):
        return jax.random.normal(next(ks), shape, f32)

    def dense(shape, fan_in, scale=1.0):
        return normal(shape) * (scale * fan_in ** -0.5)

    def gain(shape):
        return 1.0 + 0.02 * normal(shape)

    def small(shape):
        return 0.02 * normal(shape)

    x = normal((BATCH, SEQ, D_MODEL))
    offset = jax.random.randint(next(ks), (BATCH,), 0, 4096, dtype=jnp.int32)
    positions = offset[:, None] + jnp.arange(SEQ, dtype=jnp.int32)[None, :]
    a_init = jax.random.uniform(next(ks), (N_GDN, GDN_HEADS), f32, 1.0, 16.0)
    dt = jnp.exp(jax.random.uniform(next(ks), (N_GDN, GDN_HEADS), f32, float(np.log(1e-3)), float(np.log(1e-1))))
    return {
        "x": x,
        "positions": positions,
        "gla_w_in": dense((N_GLA, D_MODEL, sum(GLA_COLS)), D_MODEL),
        "gla_w_gk": dense((N_GLA, GLA_GATE_RANK, GLA_HEADS * GLA_DK), GLA_GATE_RANK),
        "gla_b_gk": small((N_GLA, GLA_HEADS * GLA_DK)),
        "gla_norm_g": gain((N_GLA, GLA_DV)),
        "gla_w_out": dense((N_GLA, GLA_HEADS * GLA_DV, D_MODEL), GLA_HEADS * GLA_DV, DEEPNORM_BETA),
        "moba_w_in": dense((N_MOBA, D_MODEL, sum(MOBA_COLS)), D_MODEL),
        "moba_w_out": dense((N_MOBA, D_MODEL, D_MODEL), D_MODEL, DEEPNORM_BETA),
        "gdn_w_in": dense((N_GDN, D_MODEL, sum(GDN_COLS)), D_MODEL),
        "gdn_conv_w": dense((N_GDN, GDN_CONV, 3 * GDN_WIDTH), GDN_CONV),
        "gdn_a_log": jnp.log(a_init),
        "gdn_dt_bias": dt + jnp.log(-jnp.expm1(-dt)),
        "gdn_norm_g": gain((N_GDN, GDN_DK)),
        "gdn_w_out": dense((N_GDN, GDN_WIDTH, D_MODEL), GDN_WIDTH, DEEPNORM_BETA),
        "hgrn_lower_bounds": small((DEPTH_2, HGRN_F)),
        "hgrn_w_in": dense((N_HGRN, D_MODEL, sum(HGRN_COLS)), D_MODEL),
        "hgrn_norm_g": gain((N_HGRN, D_MODEL // HGRN_HEADS)),
        "hgrn_w_out": dense((N_HGRN, D_MODEL, D_MODEL), D_MODEL, DEEPNORM_BETA),
        "ffn_w_gu": dense((DEPTH_2, D_MODEL, 2 * FFN_HIDDEN), D_MODEL),
        "ffn_w_down": dense((DEPTH_2, FFN_HIDDEN, D_MODEL), FFN_HIDDEN, DEEPNORM_BETA),
        "ln_g": gain((DEPTH_2, 2, D_MODEL)),
        "ln_b": small((DEPTH_2, 2, D_MODEL)),
    }

def second_block(x, positions, gla_w_in, gla_w_gk, gla_b_gk, gla_norm_g, gla_w_out, moba_w_in, moba_w_out,
              gdn_w_in, gdn_conv_w, gdn_a_log, gdn_dt_bias, gdn_norm_g, gdn_w_out, hgrn_lower_bounds,
              hgrn_w_in, hgrn_norm_g, hgrn_w_out, ffn_w_gu, ffn_w_down, ln_g, ln_b):
    lb_soft = jax.nn.softmax(hgrn_lower_bounds.astype(jnp.float32), axis=0)
    lower_bounds = jnp.cumsum(lb_soft, axis=0) - lb_soft[0]
    for i in range(DEPTH_2):
        kind, j = i % N_MIXERS, i // N_MIXERS
        if kind == 0:
            y = gla_mixer(x, gla_w_in[j], gla_w_gk[j], gla_b_gk[j], gla_norm_g[j], gla_w_out[j])
        elif kind == 1:
            y = moba_mixer(x, positions, moba_w_in[j], moba_w_out[j])
        elif kind == 2:
            y = gdn_mixer(x, gdn_w_in[j], gdn_conv_w[j], gdn_a_log[j], gdn_dt_bias[j], gdn_norm_g[j], gdn_w_out[j])
        else:
            y = hgrn2_mixer(x, lower_bounds[i], hgrn_w_in[j], hgrn_norm_g[j], hgrn_w_out[j])
        x = layer_norm_2(DEEPNORM_ALPHA * x + y, ln_g[i, 0], ln_b[i, 0])
        x = layer_norm_2(DEEPNORM_ALPHA * x + swiglu_ffn(x, ffn_w_gu[i], ffn_w_down[i]), ln_g[i, 1], ln_b[i, 1])
    return x


def setup_inputs(seed=0):
    out = dict(first_inputs(seed))
    for name, value in second_inputs(seed + 1).items():
        if name != "x":
            out[name + "_2"] = value
    return out


def reference(
    x, meta_tokens, pre_norm_g, w_in, gate_bias, pool_w, pool_scale, w_out_pool, q_norm_g, w_uq,
    kv_norm_g, w_ukv, w_out_mla, conf_dw_w, conf_dw_b, conf_ln_g, conf_ln_b, w_out_conf,
    sc_dw_w, w_out_sc, w_o, post_norm_g, positions_2, gla_w_in_2, gla_w_gk_2, gla_b_gk_2,
    gla_norm_g_2, gla_w_out_2, moba_w_in_2, moba_w_out_2, gdn_w_in_2, gdn_conv_w_2, gdn_a_log_2,
    gdn_dt_bias_2, gdn_norm_g_2, gdn_w_out_2, hgrn_lower_bounds_2, hgrn_w_in_2, hgrn_norm_g_2,
    hgrn_w_out_2, ffn_w_gu_2, ffn_w_down_2, ln_g_2, ln_b_2,
):
    x = first_block(
        x, meta_tokens, pre_norm_g, w_in, gate_bias, pool_w, pool_scale, w_out_pool, q_norm_g,
        w_uq, kv_norm_g, w_ukv, w_out_mla, conf_dw_w, conf_dw_b, conf_ln_g, conf_ln_b,
        w_out_conf, sc_dw_w, w_out_sc, w_o, post_norm_g,
    )
    return second_block(
        x, positions_2, gla_w_in_2, gla_w_gk_2, gla_b_gk_2, gla_norm_g_2, gla_w_out_2,
        moba_w_in_2, moba_w_out_2, gdn_w_in_2, gdn_conv_w_2, gdn_a_log_2, gdn_dt_bias_2,
        gdn_norm_g_2, gdn_w_out_2, hgrn_lower_bounds_2, hgrn_w_in_2, hgrn_norm_g_2,
        hgrn_w_out_2, ffn_w_gu_2, ffn_w_down_2, ln_g_2, ln_b_2,
    )


_drawn_inputs = setup_inputs


def setup_inputs(seed=0):
    import zlib

    import numpy as np

    out = dict(_drawn_inputs(seed))
    spreads = {}
    factors = {'gate_bias': 8.0,
     'q_norm_g': 8.0,
     'kv_norm_g': 7.212,
     'conf_dw_b': 4.417,
     'conf_ln_g': 9.215,
     'conf_ln_b': 20.518,
     'gla_b_gk_2': 8.0,
     'gla_norm_g_2': 26.012,
     'pool_scale': 6.572}
    for name, (base, spread) in spreads.items():
        noise = np.random.default_rng([zlib.crc32(name.encode()), seed]).standard_normal(out[name].shape)
        drawn = base * np.exp(spread * noise) if base else spread * noise
        out[name] = __import__('jax').numpy.asarray(drawn.astype(out[name].dtype))
    for name, factor in factors.items():
        out[name] = (out[name] * factor).astype(out[name].dtype)
    return out
```

```python
from contextlib import ExitStack

import numpy as np

import concourse.bass as bass
import concourse.mybir as mybir

F32 = mybir.dt.float32
F32R = mybir.dt.float32r
I32 = mybir.dt.int32
ALU = mybir.AluOpType
ACT = mybir.ActivationFunctionType
AX = mybir.AxisListType

P = 128
ROWS, META, DM = 256, 16, 1024
KEYS = ROWS + META
TILES, KC = ROWS // P, DM // P
EPS, LN_EPS = 1e-6, 1e-5
ALPHA = (2.0 * 2) ** 0.25
SLOT, RING, LEAD = 1024, 4, 3
HEADS, NOPE, ROPE, VD = 8, 64, 32, 64
QK = NOPE + ROPE
CONF_K, SC_K = 31, 3
GLA_H, DK, DV, CH = 4, 128, 256, 64
NCH = ROWS // CH
FFN = 2816
FCH = FFN // P
HD = 128
NEG = -1e30

Z_BLOCKS = [("ckv_kr", 768), ("cq", 512), ("pool_v", 0), ("conf_a", 1440), ("conf_g", 1696), ("sc_c", 2464),
            ("sc_x", 2720), ("sc_b", 2208), ("sc_gate", 2976), ("pool_gate", 256), ("conf_gate", 1952),
            ("mla_gate0", 928), ("mla_gate1", 1184)]
GATE_COL0 = 3232
BRANCH = {"pool": 0, "mla": 1, "conf": 2, "sc": 3}

STAGES = [("z", 26), ("gate_sc", 8), ("y_sc", 2), ("gate_pool", 8), ("y_pool", 2), ("gate_conf", 8), ("y_conf", 2),
          ("gate_mla", 8), ("y_mla", 4), ("w_o", 8), ("gla_gk", 2), ("gla_q", 4), ("gla_k", 4), ("gla_v", 8),
          ("gla_g", 8), ("gla_out", 8), ("gu0", 44), ("down0", 22), ("moba_q", 8), ("moba_k", 8), ("moba_v", 8),
          ("moba_out", 8), ("gu1", 44), ("down1", 22)]
FIRST, COUNT, TOTAL = {}, {}, 0
for _name, _n in STAGES:
    FIRST[_name], COUNT[_name] = TOTAL, _n
    TOTAL += _n

OUTS = ["z%d" % _i for _i in range(13)]
for _b in ("sc", "pool", "conf"):
    OUTS += ["gate_%s%d" % (_b, _i) for _i in range(4)] + ["y_%s%d" % (_b, _i) for _i in range(4)]
OUTS += ["gate_mla0", "gate_mla1", "heads0", "gate_mla2", "heads1", "gate_mla3", "heads2", "heads3"]
OUTS += ["y_mla%d" % _i for _i in range(4)] + ["w_o0", "w_o1", "gla_gk", "gla_q0", "gla_q1", "gla_k0", "gla_k1",
                                              "gla_v0", "gla_v1", "gla_g0", "gla_g1", "gla_out0", "gla_out1"]
OUTS += ["gu0_%d" % _i for _i in range(22)] + ["down0_0", "down0_1"]
OUTS += ["moba_q%d" % _i for _i in range(4)] + ["moba_k%d" % _i for _i in range(4)] + ["moba_v0", "moba_v1"]
OUTS += ["moba_heads%d" % _i for _i in range(4)] + ["moba_out0", "moba_out1"]
OUTS += ["gu1_%d" % _i for _i in range(22)] + ["down1_0", "down1_1"]
OUT = {_n: _i for _i, _n in enumerate(OUTS)}

MISC = ["vec"] + ["x0_%d" % _i for _i in range(KC)] + ["ssq_kv", "ssq_cq"]
MISC += ["uq%d" % _i for _i in range(4)] + ["kn%d" % _i for _i in range(8)] + ["vt%d" % _i for _i in range(3)]
MISC += ["krs", "krc"] + ["qs%d" % _i for _i in range(4)] + ["pool", "conf_mean", "conf_var"]
for _h in range(HEADS):
    MISC += ["s%d" % _h] + (["pt%d" % (_h - 1), "pm%d" % (_h - 1)] if _h else [])
MISC += ["pt7", "pm7"] + ["x1_%d" % _i for _i in range(4)] + ["la0", "la1", "sg0", "sg1", "ke0", "ke1"]
for _h in range(GLA_H):
    MISC += ["upd%da" % _h, "upd%db" % _h]
MISC += ["o%d" % _i for _i in range(4)] + ["ot%d" % _i for _i in range(4)] + ["x2_%d" % _i for _i in range(4)]
MISC += ["x3_%d" % _i for _i in range(4)] + ["rq%d" % _i for _i in range(4)] + ["rk%d" % _i for _i in range(4)]
for _h in range(HEADS):
    MISC += ["ms%d" % _h] + (["mt%d" % (_h - 1)] if _h else [])
MISC += ["mt7"] + ["x4_%d" % _i for _i in range(4)]
BANK = {_n: _i for _i, _n in enumerate(MISC)}

VEC_ROWS = [("pre_norm_g", 8), ("gate_bias", 32), ("pool_scale", 2), ("q_norm_g", 2), ("kv_norm_g", 1),
            ("conf_dw_w", 2 * CONF_K), ("conf_dw_b", 2), ("conf_ln_g", 2), ("conf_ln_b", 2), ("sc_dw_w", 2 * SC_K),
            ("gla_b_gk_2", 4)]
VEC, VEC_N = {}, 0
for _name, _n in VEC_ROWS:
    VEC[_name] = VEC_N
    VEC_N += _n

S0, S1 = META + P, META + ROWS
CONST = {}
CONST_N = 0
for _name, _n in [("ident", P), ("ones", P), ("mask_mla", S0 + S1), ("mask_moba", P + ROWS), ("cos", KEYS),
                  ("sin", KEYS), ("swap", ROPE), ("inv_freq", 1), ("sign", 1)]:
    CONST[_name] = CONST_N
    CONST_N += _n


def constants():
    c = np.zeros((P, CONST_N), np.float32)

    def put(name, rows, block):
        c[rows, CONST[name]:CONST[name] + block.shape[1]] = block

    every = slice(0, P)
    put("ident", every, np.eye(P, dtype=np.float32))
    put("ones", every, np.ones((P, P), np.float32))
    q, k = np.arange(P)[:, None], np.arange(S1)[None, :]
    m0 = np.where(k[:, :S0] <= q + META, 0, NEG)
    m1 = np.where(k <= q + META + P, 0, NEG)
    put("mask_mla", every, np.concatenate([m0, m1], 1).astype(np.float32))
    k = np.arange(ROWS)[None, :]
    put("mask_moba", every, np.concatenate([np.where(k[:, :P] <= q, 0, NEG), np.where(k <= q + P, 0, NEG)], 1)
        .astype(np.float32))
    inv = (1.0 / (np.float32(10000.0) ** (np.arange(0, ROPE, 2, dtype=np.float32) / np.float32(ROPE)))).astype(np.float32)
    ang = (np.arange(KEYS, dtype=np.float32)[None, :] * inv[:, None]).astype(np.float32)
    rope = slice(NOPE, NOPE + ROPE)
    put("cos", rope, np.concatenate([np.cos(ang), np.cos(ang)]).astype(np.float32))
    put("sin", rope, np.concatenate([-np.sin(ang), np.sin(ang)]).astype(np.float32))
    swap = np.roll(np.eye(ROPE, dtype=np.float32), ROPE // 2, axis=1)
    put("swap", slice(0, ROPE), swap)
    put("swap", rope, swap)
    inv2 = np.power(np.float32(500000.0), -np.arange(0, 32, 2, dtype=np.float32) / np.float32(32)).astype(np.float32)
    put("inv_freq", slice(0, 32), np.concatenate([inv2, inv2])[:, None])
    put("sign", slice(0, 32), np.concatenate([-np.ones(16), np.ones(16)]).astype(np.float32)[:, None])
    return c


class Slot:

    def __init__(self, at, index, loop):
        self.at, self.index, self.loop = at, index, loop

    def number(self, ahead=0):
        return self.at + ahead if self.loop is None else self.loop * RING + (self.at + ahead)

    def ring(self, ahead=0):
        return (self.at + ahead) % RING

    def uses(self, ahead=0):
        n = (self.at + ahead) // RING
        return n if self.loop is None else self.loop + n


def over_slots(eng, first, count, loops=None):
    groups = count // RING if loops is None else loops
    done = 0
    if groups >= 2:
        with eng.Fori(0, groups) as g:
            for j in range(RING):
                yield Slot(first + j, j, g)
        done = RING * groups
    for j in range(done, count):
        yield Slot(first + j, j, None)


def hybrid_stack(nc, d, out):
    with ExitStack() as ctx:
        cursor = [(nc.sbuf_base + 63) // 64 * 64]

        def place(name, cols, dt=F32):
            cols = [cols] if isinstance(cols, int) else list(cols)
            t = nc.alloc_sbuf_tensor_at(name, [P] + cols, dt, offset=cursor[0])
            cursor[0] += (int(np.prod(cols)) * 4 + 31) // 32 * 32
            return t

        staged = place("staged", [RING, SLOT])
        w_hi = place("w_hi", [RING, SLOT], F32R)
        w_lo = place("w_lo", [RING, SLOT], F32R)
        const = place("const", CONST_N)
        vec_rows = place("vec_rows", P)
        vec = place("vec", P)
        neg_bias = place("neg_bias", 8)
        x = place("x", [TILES, DM])
        y = place("y", [TILES, DM])
        x_hi = place("x_hi", [KC, KEYS], F32R)
        x_lo = place("x_lo", [KC, KEYS], F32R)
        gain = place("gain", DM)
        shift = place("shift", DM)
        trig = place("trig", [2, ROWS])
        w_gk = place("w_gk", GLA_H * DK)
        head_gain = place("head_gain", DV)
        ssq = place("ssq", 8)
        rs = place("rs", [3, 8])
        mu_var = place("mu_var", [2, 2])
        stats = place("stats", [2, 2, 6])
        nmr = place("nmr", 2)
        half_pi = place("half_pi", 1)
        neg_max = place("neg_max", [2, 2])
        sums = place("sums", [2, 2])
        inv_sum = place("inv_sum", [2, 2])
        region = cursor[0]

        kT = place("kT", [HEADS, KEYS])
        qT = place("qT", [HEADS, ROWS])
        end_qk = cursor[0]
        vt = place("vt", [3, HEADS * VD])
        mla_gate = place("mla_gate", [4, ROWS])
        conv = place("conv", [2, ROWS])
        conf_gate = place("conf_gate", [2, ROWS])
        glu = place("glu", [2, KEYS])
        glu_g = place("glu_g", [2, KEYS])
        gates = place("gates", [KC, ROWS])
        conf_sq = place("conf_sq", [2, ROWS])
        early = cursor[0]
        kv_z = place("kv_z", KEYS)
        kr_z = place("kr_z", KEYS)
        cq_z = place("cq_z", [2, ROWS])
        sq_kv = place("sq_kv", KEYS)
        sq_cq = place("sq_cq", [2, ROWS])
        w_uq = place("w_uq", [2, HEADS * QK])
        w_ukv = place("w_ukv", HEADS * (NOPE + VD))
        early_end = cursor[0]
        cursor[0] = early
        m = place("m", [KC, ROWS])
        y_gated = place("y_gated", [2, 2, ROWS])
        u_pool_hi = place("u_pool_hi", [2, ROWS], F32R)
        u_pool_lo = place("u_pool_lo", [2, ROWS], F32R)
        u_conf_hi = place("u_conf_hi", [2, ROWS], F32R)
        u_conf_lo = place("u_conf_lo", [2, ROWS], F32R)
        cursor[0] = max(cursor[0], early_end)
        u_sc_hi = place("u_sc_hi", [2, ROWS], F32R)
        u_sc_lo = place("u_sc_lo", [2, ROWS], F32R)
        rope_t = place("rope_t", 2 * ROWS)
        kr_t = place("kr_t", KEYS)
        mid = cursor[0]
        pool_v = place("pool_v", [2, KEYS])
        pool_a = place("pool_a", [2, KEYS])
        pool_b = place("pool_b", [2, KEYS])
        pooled = place("pooled", [2, ROWS])
        pool_gate = place("pool_gate", [2, ROWS])
        w_pool = place("w_pool", [2, P])
        sc_c = place("sc_c", [2, KEYS])
        sc_x = place("sc_x", [2, KEYS])
        sc_b = place("sc_b", [2, ROWS])
        sc_gate = place("sc_gate", [2, ROWS])
        sc_acc = place("sc_acc", [2, ROWS])
        mid_end = cursor[0]
        cursor[0] = mid
        scores = place("scores", [2, S0 + S1])
        probs = place("probs", [2, S0 + S1])
        probsT = place("probsT", [2, 3 * P])
        metaT = place("metaT", [2, ROWS])
        u_mla_hi = place("u_mla_hi", [4, ROWS], F32R)
        u_mla_lo = place("u_mla_lo", [4, ROWS], F32R)
        u_mla = place("u_mla", [4, ROWS])
        end1 = max(cursor[0], mid_end)
        cursor[0] = region
        m_hi = place("m_hi", [KC, ROWS], F32R)
        m_lo = place("m_lo", [KC, ROWS], F32R)
        assert cursor[0] <= end_qk

        cursor[0] = region
        gq = place("gq", [GLA_H, ROWS])
        gk = place("gk", [GLA_H, ROWS])
        la = place("la", [GLA_H, ROWS])
        la_e = place("la_e", [GLA_H, ROWS])
        gla_dead = cursor[0]
        gk_low = place("gk_low", ROWS)
        reset = place("reset", [GLA_H, ROWS])
        e_cum = place("e_cum", [GLA_H, ROWS])
        e_inv = place("e_inv", [GLA_H, ROWS])
        e_end = place("e_end", [GLA_H, ROWS])
        qd = place("qd", [GLA_H, ROWS])
        qd_half = place("qd_half", [2, GLA_H, ROWS])
        ki = place("ki", [GLA_H, ROWS])
        ke = place("ke", [GLA_H, ROWS])
        ke_half = place("ke_half", [2, GLA_H * TILES, P])
        gv = place("gv", [TILES, GLA_H * DV])
        gg = place("gg", [TILES, GLA_H * DV])
        state = place("state", [GLA_H, NCH - 1, DV])
        intra = place("intra", [GLA_H * TILES, P])
        end2 = cursor[0]
        cursor[0] = region
        o_hi = place("o_hi", [KC, ROWS], F32R)
        o_lo = place("o_lo", [KC, ROWS], F32R)
        assert cursor[0] <= gla_dead

        cursor[0] = region
        h_hi = place("h_hi", [FCH, ROWS], F32R)
        h_lo = place("h_lo", [FCH, ROWS], F32R)
        h_gate = place("h_gate", [2, ROWS])
        h = place("h", [2, ROWS])
        ffn_end = cursor[0]

        cursor[0] = region
        mo_hi = place("mo_hi", [KC, ROWS], F32R)
        mo_lo = place("mo_lo", [KC, ROWS], F32R)
        mq = place("mq", [HEADS, ROWS])
        mk = place("mk", [HEADS, ROWS])
        mv = place("mv", [TILES, DM])
        mscores = place("mscores", [2, P + ROWS])
        mprobs = place("mprobs", [2, P + ROWS])
        mprobsT = place("mprobsT", [HEADS, P + ROWS])
        mrope = place("mrope", 2 * ROWS)
        end4 = cursor[0]
        assert max(end1, end2, ffn_end, end4) <= nc.sbuf_usable_end, (end1, end2, ffn_end, end4, nc.sbuf_usable_end)

        scratch = y[:].rearrange("p t c -> p (t c)")
        flat_gates = gates[:].rearrange("p c r -> p (c r)")
        m_rows, meta_h = flat_gates[0:META, 0:DM], flat_gates[0:META, DM:2 * DM]
        pos_i = kr_t[0:ROPE, 0:ROWS].bitcast(I32)
        trig_r, trig_abs = rope_t[0:ROPE, 0:ROWS], rope_t[0:ROPE, ROWS:2 * ROWS]
        trig_k, trig_kh = conf_sq[0:ROPE, 0, :], conf_sq[0:ROPE, 1, :]
        kvq_rs = [scratch[:, i * 528:(i + 1) * 528] for i in range(3)]

        acc = ctx.enter_context(nc.psum_tensor("acc", [P, 2, 2, 512], F32))
        misc = ctx.enter_context(nc.psum_tensor("misc", [P, 4, 512], F32))

        def sem(name):
            return ctx.enter_context(nc.semaphore(name))

        landed = [sem("landed%d" % i) for i in range(RING)]
        rounded, split, weights_used = sem("rounded"), sem("split"), sem("weights_used")
        evacuated = [sem("evacuated%d" % i) for i in range(2)]
        bank_full = [sem("bank_full%d" % i) for i in range(4)]
        bank_read = [sem("bank_read%d" % i) for i in range(4)]
        dve_chain, act_chain, pool_chain = sem("dve_chain"), sem("act_chain"), sem("pool_chain")
        s = {n: sem(n) for n in (
            "cleared", "conf_rounded", "conf_sig", "conf_split", "conf_squared", "conf_u",
            "conf_zn", "const_loaded", "conv_done", "cum_ready", "e_ready",
            "end_ready", "exp_done", "gain_loaded", "gg_ready", "gk_loaded", "glu_ready",
            "h_rounded", "h_split", "half_ready", "heads_done", "intra_ready", "k_spread",
            "ke_ready", "ki_ready", "kr_roped", "kv_normed", "la_abs", "la_log",
            "ln_hat", "ln_stats", "m_added", "m_exp", "m_heads_done", "m_max",
            "m_probs", "m_ready", "m_rounded", "m_split", "max_ready", "meta_cleared",
            "mk_roped", "mla_loaded", "mo_rounded", "mq_roped", "neg_bias_ready", "norm_loaded", "normed",
            "o_rounded", "o_ssq", "pool_loaded", "pool_rounded", "pool_split", "pooled_ready",
            "pos_loaded", "probs_ready", "q_roped", "qd_ready", "rstd0", "sc_ready",
            "sc_rounded", "sc_split", "sc_u", "ssq0", "state_ready", "stored",
            "trig_args", "trig_ready", "u_mla_rounded", "u_mla_split", "vec_loaded", "x0_rounded",
            "x_loaded", "x_ready", "x_rounded", "zeroed")}

        def col(name, i=0):
            return vec[:, VEC[name] + i:VEC[name] + i + 1]

        def cst(name, n, rows=slice(0, P)):
            return const[rows, CONST[name]:CONST[name] + n]

        ident, ones = cst("ident", P), cst("ones", P)

        def pair(name):
            return OUT[name] % 2

        def await_out(eng, name):
            eng.wait_ge(evacuated[OUT[name] % 2], OUT[name] // 2 + 1)

        def bank(name):
            return misc[:, BANK[name] % 4, :]

        def await_full(eng, name):
            eng.wait_ge(bank_full[BANK[name] % 4], BANK[name] // 4 + 1)

        def await_read(eng, name):
            eng.wait_ge(bank_read[BANK[name] % 4], BANK[name] // 4 + 1)

        def read_sem(name):
            return bank_read[BANK[name] % 4]

        def slot_done(eng, stage, index):
            eng.wait_ge(weights_used, FIRST[stage] + index + 1)

        block = ctx.enter_context(nc.Block())

        @block.sync
        def _(sp):
            def slot_free(sl):
                if sl.loop is not None or sl.at >= RING:
                    sp.wait_ge(split, sl.number(1 - RING))

            def load(sl, src, cols=None):
                slot_free(sl)
                dst = staged[:, sl.ring(), :]
                if len(src.shape) == 3:
                    dst = dst.rearrange("p (c n) -> p c n", c=src.shape[1])
                if cols is not None:
                    dst = staged[:, sl.ring(), :].rearrange("p (c n) -> p c n", c=src.shape[1])[:, :, 0:cols]
                sp.dma_start(dst, src).then_inc(landed[sl.ring()], 16)

            def k_half(w, half, c0, n=256):
                return w[half * 512:(half + 1) * 512, bass.ds(c0, n)].rearrange("(c p) n -> p c n", p=P)

            def by_columns(stage, w, c0):
                for sl in over_slots(sp, FIRST[stage], COUNT[stage]):
                    block0 = c0 + sl.index // 2 * 256
                    load(sl, k_half(w, sl.index % 2, block0 if sl.loop is None else sl.loop * 512 + block0))

            def by_rows(stage, w, c0=0):
                for sl in over_slots(sp, FIRST[stage], COUNT[stage]):
                    q = sl.index % 4
                    cols = c0 + sl.index // 4 * 512
                    if sl.loop is not None:
                        cols = sl.loop * 512 + cols
                    load(sl, w[q * 256:(q + 1) * 256, bass.ds(cols, 512)].rearrange("(c p) n -> p c n", p=P))

            sp.dma_start(x[:], d["x"][0].rearrange("(t p) c -> p t c", p=P)).then_inc(s["x_loaded"], 16)
            sp.dma_start(m_rows, d["meta_tokens"]).then_inc(s["x_loaded"], 16)
            for name, n in VEC_ROWS:
                src = d[name]
                flat = src.rearrange("a k (c p) -> (a k c) p", p=P) if len(src.shape) == 3 else \
                    src.rearrange("a (c p) -> (a c) p", p=P)
                sp.dma_start(vec_rows[VEC[name]:VEC[name] + n, :], flat).then_inc(s["vec_loaded"], 16)
            sp.dma_start(const[:], d["constants"]).then_inc(s["const_loaded"], 16)
            w_in = d["w_in"][0]

            def z_slots(lo, hi):
                for sl in over_slots(sp, lo, hi - lo, loops=0):
                    load(sl, k_half(w_in, sl.at % 2, Z_BLOCKS[sl.at // 2][1]))

            z_slots(0, RING)
            sp.dma_start(w_uq[:], d["w_uq"][0].rearrange("(c p) n -> p c n", p=P)).then_inc(s["mla_loaded"], 16)
            sp.dma_start(w_ukv[:], d["w_ukv"][0]).then_inc(s["mla_loaded"], 16)
            sp.dma_start(w_gk[0:16, :], d["gla_w_gk_2"][0]).then_inc(s["gk_loaded"], 16)
            sp.dma_start(head_gain[:], d["gla_norm_g_2"][0].partition_broadcast(P)).then_inc(s["gk_loaded"], 16)
            sp.dma_start(gain[:], d["post_norm_g"][0].partition_broadcast(P)).then_inc(s["gain_loaded"], 16)
            sp.dma_start(pos_i, d["positions_2"][0].partition_broadcast(32)).then_inc(s["pos_loaded"], 16)
            z_slots(RING, 2 * RING)
            sp.wait_ge(s["cleared"], 2)
            for g in range(4):
                r = slice(g % 2 * 64, g % 2 * 64 + 64)
                sp.dma_start(w_pool[r, g // 2, r], d["pool_w"][0, g]).then_inc(s["pool_loaded"], 16)
            z_slots(2 * RING, COUNT["z"])
            for b in ("sc", "pool", "conf", "mla"):
                by_columns("gate_" + b, w_in, GATE_COL0 + BRANCH[b] * DM)
                if b == "mla":
                    for sl in over_slots(sp, FIRST["y_mla"], 4, loops=0):
                        load(sl, k_half(d["w_out_mla"][0], 0, sl.index * 256))
                else:
                    for sl in over_slots(sp, FIRST["y_" + b], 2):
                        load(sl, d["w_out_" + b][0][:, sl.index * 512:(sl.index + 1) * 512]
                             .rearrange("(c p) n -> p c n", p=P))
            by_rows("w_o", d["w_o"][0])
            gla = d["gla_w_in_2"][0]
            for sl in over_slots(sp, FIRST["gla_gk"], 2):
                load(sl, k_half(gla, sl.index, 3072, 16), cols=16)
            by_columns("gla_q", gla, 0)
            by_columns("gla_k", gla, 512)
            by_rows("gla_v", gla, 1024)
            by_rows("gla_g", gla, 2048)
            by_rows("gla_out", d["gla_w_out_2"][0])
            for layer in range(2):
                gu = d["ffn_w_gu_2"][layer]
                for sl in over_slots(sp, FIRST["gu%d" % layer], COUNT["gu%d" % layer]):
                    load(sl, k_half(gu, sl.index % 2, sl.loop * 256 + (FFN if sl.index % 4 >= 2 else 0)))
                dn = d["ffn_w_down_2"][layer]
                for sl in over_slots(sp, FIRST["down%d" % layer], COUNT["down%d" % layer]):
                    row = sl.index * P if sl.loop is None else sl.loop * (RING * P) + sl.index * P
                    load(sl, dn[bass.ds(row, P), :])
                if layer == 0:
                    mw = d["moba_w_in_2"][0]
                    by_columns("moba_q", mw, 0)
                    by_columns("moba_k", mw, DM)
                    by_rows("moba_v", mw, 2 * DM)
                    by_rows("moba_out", d["moba_w_out_2"][0])
            sp.wait_ge(s["x_ready"], 10)
            sp.dma_start(out[0].rearrange("(t p) c -> p t c", p=P), x[:]).then_inc(s["stored"], 16)
            sp.wait_ge(s["stored"], 16)

        @block.tensor
        def _(pe):
            def open_out(name_or_index):
                o = OUT[name_or_index]
                if o >= 2:
                    pe.wait_ge(evacuated[o % 2], o // 2)

            def ready(sl):
                pe.wait_ge(split, sl.number(1))

            def exact(dst, st_hi, st_lo, mv_hi, mv_lo, start, stop):
                pe.matmul(dst, st_hi, mv_hi, start=start, stop=False)
                pe.matmul(dst, st_hi, mv_lo, start=False, stop=False)
                return pe.matmul(dst, st_lo, mv_hi, start=False, stop=stop)

            def t_slot(sl, p, half, mv_hi, mv_lo, kcs=4, last=True, halves=2, first=True):
                ready(sl)
                n = mv_hi.shape[-1]
                hi = w_hi[:, sl.ring(), :].rearrange("p (c n) -> p c n", c=4)
                lo = w_lo[:, sl.ring(), :].rearrange("p (c n) -> p c n", c=4)
                for b in range(halves):
                    for c in range(kcs):
                        cols = slice(b * P, b * P + P)
                        mm = exact(acc[:, p, b, 0:n], hi[:, c, cols], lo[:, c, cols],
                                   mv_hi[:, half * 4 + c, :], mv_lo[:, half * 4 + c, :],
                                   start=first and c == 0, stop=last and c == kcs - 1)
                mm.then_inc(weights_used, 1)

            def t_stage(first, count, out0, mv_hi, mv_lo, halves=2):
                for sl in over_slots(pe, first, count):
                    o = out0 + sl.index // 2
                    if sl.index % 2 == 0:
                        if sl.loop is not None:
                            pe.wait_ge(evacuated[o % 2], sl.loop + o // 2)
                        elif o >= 2:
                            pe.wait_ge(evacuated[o % 2], o // 2)
                    t_slot(sl, o % 2, sl.index % 2, mv_hi, mv_lo, halves=halves,
                           first=sl.index % 2 == 0, last=sl.index % 2 == 1)

            def n_slots(stage, names, st_hi, st_lo, lo=0, hi=None):
                for i in range(lo, COUNT[stage] if hi is None else hi):
                    sl = Slot(FIRST[stage] + i, i, None)
                    q, name = i % 4, names[i // 4]
                    if q == 0:
                        open_out(name)
                    ready(sl)
                    for c in range(2):
                        cols = slice(c * 512, c * 512 + 512)
                        for t in range(TILES):
                            rows = slice(t * P, t * P + P)
                            k = q * 2 + c
                            mm = exact_n(acc[:, pair(name), t, :], st_hi[:, k, rows], st_lo[:, k, rows],
                                         w_hi[:, sl.ring(), cols], w_lo[:, sl.ring(), cols],
                                         start=k == 0, stop=k == KC - 1)
                    mm.then_inc(weights_used, 1)

            exact_n = exact

            def open_bank(name):
                u = BANK[name]
                if u >= 4:
                    pe.wait_ge(bank_read[u % 4], u // 4)
                return misc[:, u % 4, :]

            def filled(ins, name):
                ins.then_inc(bank_full[BANK[name] % 4], 1)

            def turn_rows(tag):
                for j in range(4):
                    b = open_bank("%s_%d" % (tag, j))
                    for c in range(2):
                        for t in range(TILES):
                            tr = pe.transpose(b[:, c * ROWS + t * P:c * ROWS + t * P + P],
                                              x[:, t, (2 * j + c) * P:(2 * j + c) * P + P], ident)
                    filled(tr, "%s_%d" % (tag, j))

            xt_hi, xt_lo = x_hi[:, :, 0:ROWS], x_lo[:, :, 0:ROWS]
            xm_hi, xm_lo = x_hi[:, :, META:KEYS], x_lo[:, :, META:KEYS]

            pe.wait_ge(s["const_loaded"], 16)
            pe.wait_ge(s["vec_loaded"], 16 * len(VEC_ROWS))
            filled(pe.transpose(open_bank("vec")[:, 0:VEC_N], vec_rows[0:VEC_N, :], ident[0:VEC_N, 0:VEC_N]), "vec")
            pe.wait_ge(s["normed"], 3)
            for c in range(KC):
                b = open_bank("x0_%d" % c)
                cols = slice(c * P, c * P + P)
                pe.transpose(b[:, 0:META], meta_h[:, cols], ident[0:META, 0:META])
                for t in range(TILES):
                    tr = pe.transpose(b[:, META + t * P:META + t * P + P], y[:, t, cols], ident)
                filled(tr, "x0_%d" % c)
            for c in range(KC - 4, KC):
                await_read(pe, "x0_%d" % c)

            def z(lo, hi):
                t_stage(lo, hi - lo, lo // 2, x_hi, x_lo)

            z(0, 6)
            await_out(pe, "z0")
            filled(pe.matmul(open_bank("ssq_kv")[:, 0:KEYS], ones, sq_kv[:], start=True, stop=True), "ssq_kv")
            await_out(pe, "z1")
            b = open_bank("ssq_cq")
            pe.matmul(b[:, 0:ROWS], ones, sq_cq[:, 0, :], start=True, stop=False)
            filled(pe.matmul(b[:, 0:ROWS], ones, sq_cq[:, 1, :], start=False, stop=True), "ssq_cq")
            z(6, 18)
            pe.wait_ge(s["mla_loaded"], 32)
            pe.wait_ge(s["kv_normed"], 1)
            for j in range(4):
                b = open_bank("uq%d" % j)
                for i in range(2):
                    for c in range(2):
                        mm = pe.matmul(b[0:QK, i * ROWS:(i + 1) * ROWS], w_uq[:, c, (2 * j + i) * QK:(2 * j + i + 1) * QK],
                                       cq_z[:, c, :], start=c == 0, stop=c == 1)
                filled(mm, "uq%d" % j)
            wkv = w_ukv[:].rearrange("p (h e) -> p h e", h=HEADS)
            for i in range(HEADS):
                filled(pe.matmul(open_bank("kn%d" % i)[0:NOPE, 0:KEYS], wkv[:, i, 0:NOPE], kv_z[:], start=True, stop=True),
                       "kn%d" % i)
            for i, (lo, n) in enumerate([(0, META), (META, P), (META + P, P)]):
                filled(pe.matmul(open_bank("vt%d" % i)[0:n, :], kv_z[:, lo:lo + n], wkv[:, :, NOPE:NOPE + VD],
                                 start=True, stop=True), "vt%d" % i)
            rope = slice(NOPE, QK)
            filled(pe.matmul(open_bank("krs")[rope, 0:KEYS], cst("swap", ROPE, slice(0, ROPE)), kr_z[0:ROPE, :],
                             start=True, stop=True), "krs")
            filled(pe.matmul(open_bank("krc")[rope, 0:KEYS], ident[0:ROPE, 0:ROPE], kr_z[0:ROPE, :],
                             start=True, stop=True), "krc")
            for j in range(4):
                await_read(pe, "uq%d" % j)
                filled(pe.matmul(open_bank("qs%d" % j)[rope, :], cst("swap", ROPE, rope), qT[rope, 2 * j:2 * j + 2, :],
                                 start=True, stop=True), "qs%d" % j)
            z(18, 20)
            pe.wait_ge(s["pool_loaded"], 64)
            pe.wait_ge(s["pooled_ready"], 1)
            b = open_bank("pool")
            for c in range(2):
                mm = pe.matmul(b[:, c * ROWS:(c + 1) * ROWS], w_pool[:, c, :], pooled[:, c, :], start=True, stop=True)
            filled(mm, "pool")
            z(20, 26)

            def y_stage(b, u_hi, u_lo):
                for i in range(2):
                    sl = Slot(FIRST["y_" + b] + i, i, None)
                    ready(sl)
                    hi = w_hi[:, sl.ring(), :].rearrange("p (c n) -> p c n", c=2)
                    lo = w_lo[:, sl.ring(), :].rearrange("p (c n) -> p c n", c=2)
                    for q in range(4):
                        name = "y_%s%d" % (b, 2 * i + q // 2)
                        if q % 2 == 0:
                            open_out(name)
                        for c in range(2):
                            cols = slice(q * P, q * P + P)
                            mm = exact(acc[:, pair(name), q % 2, 0:ROWS], hi[:, c, cols], lo[:, c, cols],
                                       u_hi[:, c, :], u_lo[:, c, :], start=c == 0, stop=c == 1)
                    mm.then_inc(weights_used, 1)

            t_stage(FIRST["gate_sc"], 8, OUT["gate_sc0"], xm_hi, xm_lo)
            pe.wait_ge(s["sc_split"], 1)
            y_stage("sc", u_sc_hi, u_sc_lo)
            t_stage(FIRST["gate_pool"], 8, OUT["gate_pool0"], xm_hi, xm_lo)
            pe.wait_ge(s["pool_split"], 1)
            y_stage("pool", u_pool_hi, u_pool_lo)
            pe.wait_ge(s["conv_done"], 1)
            b = open_bank("conf_mean")
            pe.matmul(b[:, 0:ROWS], ones, conv[:, 0, :], start=True, stop=False)
            filled(pe.matmul(b[:, 0:ROWS], ones, conv[:, 1, :], start=False, stop=True), "conf_mean")
            for i in range(2):
                t_stage(FIRST["gate_conf"] + 4 * i, 4, OUT["gate_conf%d" % (2 * i)], xm_hi, xm_lo)
                if i == 0:
                    pe.wait_ge(s["conf_squared"], 1)
                    b = open_bank("conf_var")
                    pe.matmul(b[:, 0:ROWS], ones, conf_sq[:, 0, :], start=True, stop=False)
                    filled(pe.matmul(b[:, 0:ROWS], ones, conf_sq[:, 1, :], start=False, stop=True), "conf_var")
            pe.wait_ge(s["conf_split"], 1)
            y_stage("conf", u_conf_hi, u_conf_lo)

            pe.wait_ge(s["q_roped"], 4)
            pe.wait_ge(s["k_spread"], 1)

            def mla_scores(i):
                b = open_bank("s%d" % i)
                pe.matmul(b[:, 0:S0], qT[0:QK, i, 0:P], kT[0:QK, i, 0:S0], start=True, stop=True)
                filled(pe.matmul(b[:, S0:S0 + S1], qT[0:QK, i, P:ROWS], kT[0:QK, i, :], start=True, stop=True), "s%d" % i)

            def mla_turn(i):
                pe.wait_ge(s["probs_ready"], i + 1)
                pr = probs[:, i % 2, :]
                b = open_bank("pt%d" % i)
                pe.transpose(b[:, 0:P], pr[:, META:S0], ident)
                pe.transpose(b[:, P:2 * P], pr[:, S0 + META:S0 + S0], ident)
                filled(pe.transpose(b[:, 2 * P:3 * P], pr[:, S0 + S0:S0 + S1], ident), "pt%d" % i)
                b = open_bank("pm%d" % i)
                pe.transpose(b[0:META, 0:P], pr[:, 0:META], ident)
                filled(pe.transpose(b[0:META, P:2 * P], pr[:, S0:S0 + META], ident), "pm%d" % i)

            def mla_heads(i):
                name = "heads%d" % (i // 2)
                if i % 2 == 0:
                    open_out(name)
                await_read(pe, "pt%d" % i)
                await_read(pe, "pm%d" % i)
                dst = acc[i % 2 * VD:i % 2 * VD + VD, pair(name), 0, :]
                cols = slice(i * VD, i * VD + VD)
                pe.matmul(dst[:, 0:ROWS], vt[:, 0, cols], metaT[:, i % 2, :], start=True, stop=False)
                pe.matmul(dst[:, 0:ROWS], vt[:, 1, cols], probsT[:, i % 2, 0:ROWS], start=False, stop=False)
                pe.matmul(dst[:, P:ROWS], vt[:, 2, cols], probsT[:, i % 2, ROWS:ROWS + P], start=False,
                          stop=True).then_inc(s["heads_done"], 1)

            for i in range(HEADS):
                name = "gate_mla%d" % (i // 2)
                if i % 2 == 0:
                    open_out(name)
                t_slot(Slot(FIRST["gate_mla"] + i, i, None), pair(name), i % 2, xm_hi, xm_lo,
                       first=i % 2 == 0, last=i % 2 == 1)
                mla_scores(i)
                if i >= 1:
                    mla_turn(i - 1)
                if i >= 2:
                    mla_heads(i - 2)
            mla_turn(HEADS - 1)
            mla_heads(HEADS - 2)
            mla_heads(HEADS - 1)
            pe.wait_ge(s["u_mla_split"], 4)
            for i in range(4):
                open_out("y_mla%d" % i)
                t_slot(Slot(FIRST["y_mla"] + i, i, None), pair("y_mla%d" % i), 0, u_mla_hi, u_mla_lo)
            pe.wait_ge(s["m_split"], 4)
            n_slots("w_o", ["w_o0", "w_o1"], m_hi, m_lo)

            def next_rows(tag, count):
                pe.wait_ge(s["x_ready"], count)
                turn_rows(tag)
                for j in range(4):
                    await_read(pe, "%s_%d" % (tag, j))

            next_rows("x1", 2)
            t_stage(FIRST["gla_gk"], 2, OUT["gla_gk"], xt_hi, xt_lo, halves=1)
            t_stage(FIRST["gla_q"], 4, OUT["gla_q0"], xt_hi, xt_lo)
            pe.wait_ge(s["gk_loaded"], 32)
            await_out(pe, "gla_gk")
            for j in range(2):
                b = open_bank("la%d" % j)
                for i in range(2):
                    c = 2 * j + i
                    mm = pe.matmul(b[:, i * ROWS:(i + 1) * ROWS], w_gk[0:16, c * DK:(c + 1) * DK], gk_low[0:16, :],
                                   start=True, stop=True)
                filled(mm, "la%d" % j)
            t_stage(FIRST["gla_k"], 4, OUT["gla_k0"], xt_hi, xt_lo)
            n_slots("gla_v", ["gla_v0", "gla_v1"], xt_hi, xt_lo)
            pe.wait_ge(s["qd_ready"], 1)
            pe.wait_ge(s["ki_ready"], 1)
            for j in range(2):
                b = open_bank("sg%d" % j)
                for i in range(4):
                    hd, t = 2 * j + i // 2, i % 2
                    rows = slice(t * P, t * P + P)
                    mm = pe.matmul(b[:, i * P:(i + 1) * P], ki[:, hd, rows], qd[:, hd, rows], start=True, stop=True)
                filled(mm, "sg%d" % j)
            pe.wait_ge(s["ke_ready"], 1)
            for j in range(2):
                b = open_bank("ke%d" % j)
                for i in range(4):
                    hd, t = 2 * j + i // 2, i % 2
                    tr = pe.transpose(b[:, i * P:(i + 1) * P], ke[:, hd, t * P:t * P + P], ident)
                filled(tr, "ke%d" % j)
            n_slots("gla_g", ["gla_g0", "gla_g1"], xt_hi, xt_lo, 0, 3)
            await_read(pe, "ke0")
            await_read(pe, "ke1")
            await_out(pe, "gla_v0")
            await_out(pe, "gla_v1")
            for hd in range(GLA_H):
                for half, chunks in (("a", (0, 1)), ("b", (2,))):
                    b = open_bank("upd%d%s" % (hd, half))
                    for n in chunks:
                        mm = pe.matmul(b[:, n % 2 * DV:n % 2 * DV + DV], ke_half[:, n % 2, hd * TILES + n // 2, :],
                                       gv[:, n // 2, hd * DV:(hd + 1) * DV], start=True, stop=True)
                    filled(mm, "upd%d%s" % (hd, half))
            n_slots("gla_g", ["gla_g0", "gla_g1"], xt_hi, xt_lo, 3, 8)
            pe.wait_ge(s["intra_ready"], 2)
            pe.wait_ge(s["half_ready"], 2)
            for hd in range(GLA_H - 2, GLA_H):
                await_read(pe, "upd%da" % hd)
                await_read(pe, "upd%db" % hd)
            for j in range(4):
                b = open_bank("o%d" % j)
                t = j // 2
                for i in range(2):
                    hd = j % 2 * 2 + i
                    dst = b[:, i * DV:(i + 1) * DV]
                    rows = slice(t * P, t * P + P)
                    pe.matmul(dst, intra[:, hd * TILES + t, :], gv[:, t, hd * DV:(hd + 1) * DV], start=True, stop=False)
                    if t == 1:
                        pe.matmul(dst, qd_half[:, 0, hd, rows], state[:, hd, 1, :], start=False, stop=False)
                    mm = pe.matmul(dst, qd_half[:, 1, hd, rows], state[:, hd, 2 * t, :], start=False, stop=True)
                filled(mm, "o%d" % j)
            for j in range(4):
                await_read(pe, "o%d" % j)
            for j in range(4):
                b = open_bank("ot%d" % j)
                for c in range(2):
                    for t in range(TILES):
                        tr = pe.transpose(b[:, c * ROWS + t * P:c * ROWS + t * P + P],
                                          gg[:, t, (2 * j + c) * P:(2 * j + c) * P + P], ident)
                filled(tr, "ot%d" % j)
            for j in range(4):
                await_read(pe, "ot%d" % j)
            n_slots("gla_out", ["gla_out0", "gla_out1"], o_hi, o_lo)

            def swiglu(layer):
                tag = "gu%d" % layer
                t_stage(FIRST[tag], COUNT[tag], OUT[tag + "_0"], xt_hi, xt_lo)
                tag = "down%d" % layer
                names = [tag + "_0", tag + "_1"]
                pe.wait_ge(s["h_split"], (layer + 1) * FCH // 2)
                for n in names:
                    open_out(n)
                for k in range(FCH):
                    sl = Slot(FIRST[tag] + k, k, None)
                    ready(sl)
                    for t in range(TILES):
                        rows = slice(t * P, t * P + P)
                        for hf in range(2):
                            cols = slice(hf * 512, hf * 512 + 512)
                            mm = exact(acc[:, pair(names[hf]), t, :], h_hi[:, k, rows], h_lo[:, k, rows],
                                       w_hi[:, sl.ring(), cols], w_lo[:, sl.ring(), cols], start=k == 0, stop=k == FCH - 1)
                    mm.then_inc(weights_used, 1)

            next_rows("x2", 4)
            swiglu(0)

            next_rows("x3", 6)
            t_stage(FIRST["moba_q"], 8, OUT["moba_q0"], xt_hi, xt_lo)
            r32 = slice(0, ROPE)

            def swap_halves(tag, src, o):
                for j in range(4):
                    await_out(pe, "%s%d" % (o, j))
                    filled(pe.matmul(open_bank("%s%d" % (tag, j))[r32, :], cst("swap", ROPE, r32),
                                     src[r32, 2 * j:2 * j + 2, :], start=True, stop=True), "%s%d" % (tag, j))

            t_stage(FIRST["moba_k"], 4, OUT["moba_k0"], xt_hi, xt_lo)
            swap_halves("rq", mq, "moba_q")
            t_stage(FIRST["moba_k"] + 4, 4, OUT["moba_k2"], xt_hi, xt_lo)
            n_slots("moba_v", ["moba_v0", "moba_v1"], xt_hi, xt_lo, 0, 2)
            swap_halves("rk", mk, "moba_k")
            n_slots("moba_v", ["moba_v0", "moba_v1"], xt_hi, xt_lo, 2, 4)

            def moba_scores(i):
                b = open_bank("ms%d" % i)
                pe.matmul(b[:, 0:P], mq[:, i, 0:P], mk[:, i, 0:P], start=True, stop=True)
                filled(pe.matmul(b[:, P:P + ROWS], mq[:, i, P:ROWS], mk[:, i, :], start=True, stop=True), "ms%d" % i)

            def moba_turn(i):
                pe.wait_ge(s["m_probs"], i + 1)
                b = open_bank("mt%d" % i)
                for c in range(3):
                    tr = pe.transpose(b[:, c * P:(c + 1) * P], mprobs[:, i % 2, c * P:(c + 1) * P], ident)
                filled(tr, "mt%d" % i)

            pe.wait_ge(s["mk_roped"], 4)
            pe.wait_ge(s["mq_roped"], 4)
            for i in range(HEADS):
                if i < 4:
                    n_slots("moba_v", ["moba_v0", "moba_v1"], xt_hi, xt_lo, 4 + i, 5 + i)
                moba_scores(i)
                if i >= 1:
                    moba_turn(i - 1)
            moba_turn(HEADS - 1)
            await_out(pe, "moba_v0")
            await_out(pe, "moba_v1")
            for i in range(HEADS):
                name = "moba_heads%d" % (i // 2)
                if i % 2 == 0:
                    open_out(name)
                await_read(pe, "mt%d" % i)
                dst = acc[:, pair(name), i % 2, :]
                cols = slice(i * HD, (i + 1) * HD)
                pe.matmul(dst[:, 0:ROWS], mv[:, 0, cols], mprobsT[:, i, 0:ROWS], start=True, stop=False)
                pe.matmul(dst[:, P:ROWS], mv[:, 1, cols], mprobsT[:, i, ROWS:ROWS + P], start=False,
                          stop=True).then_inc(s["m_heads_done"], 1)
            for i in range(4):
                await_out(pe, "moba_heads%d" % i)
            n_slots("moba_out", ["moba_out0", "moba_out1"], mo_hi, mo_lo)
            next_rows("x4", 8)
            swiglu(1)

        @block.scalar
        def _(act):
            chained = [0]

            def link(ins):
                chained[0] += 1
                ins.then_inc(act_chain, 1)
                act.wait_ge(act_chain, chained[0])

            def round_slot(sl, ahead):
                k = sl.ring(ahead)
                act.wait_ge(landed[k], (sl.uses(ahead) + 1) * 16)
                if sl.loop is not None or sl.at + ahead >= RING:
                    act.wait_ge(weights_used, sl.number(ahead + 1 - RING))
                nc.scalar.copy(w_hi[:, k, :], staged[:, k, :]).then_inc(rounded, 1)

            def lead(sl):
                if sl.loop is not None or sl.at + LEAD < TOTAL:
                    round_slot(sl, LEAD)

            def copy_out(dst, src, name, func=ACT.Copy, **kw):
                nc.scalar.activation(dst, src, func, **kw).then_inc(evacuated[OUT[name] % 2], 1)

            def out_t(name, n=ROWS, lo=0):
                return acc[:, pair(name), :, lo:lo + n]

            def halves(dst, i):
                return dst[:, 2 * i:2 * i + 2, :]

            act.wait_ge(s["x_loaded"], 32)
            act.wait_ge(s["cleared"], 1)
            for t in range(TILES):
                nc.scalar.activation(y[:, t, :], x[:, t, :], ACT.Square, accum_out=ssq[:, t:t + 1])
            nc.scalar.activation(meta_h, m_rows, ACT.Square, accum_out=ssq[0:META, 2:3]).then_inc(s["ssq0"], 1)
            round_slot(Slot(0, 0, None), 0)
            act.wait_ge(s["rstd0"], 1)
            for t in range(TILES):
                nc.scalar.activation(y[:, t, :], x[:, t, :], ACT.Copy, scale=rs[:, 1, t:t + 1]).then_inc(s["normed"], 1)
            nc.scalar.activation(meta_h, m_rows, ACT.Copy, scale=rs[0:META, 1, 2:3]).then_inc(s["normed"], 1)
            for i in range(1, LEAD):
                round_slot(Slot(i, i, None), 0)
            await_read(act, "vec")
            for c in range(KC):
                await_full(act, "x0_%d" % c)
                nc.scalar.activation(x_hi[:, c, :], bank("x0_%d" % c)[:, 0:KEYS], ACT.Copy,
                                     scale=col("pre_norm_g", c)).then_inc(s["x0_rounded"], 1)

            for sl in over_slots(act, 0, COUNT["z"], loops=0):
                lead(sl)
                if sl.at % 2 == 0:
                    continue
                name = "z%d" % (sl.at // 2)
                what = Z_BLOCKS[sl.at // 2][0]
                slot_done(act, "z", sl.at)
                if what == "ckv_kr":
                    nc.scalar.copy(kv_z[:], acc[:, pair(name), 0, 0:KEYS])
                    nc.scalar.copy(kr_z[0:ROPE, :], acc[0:ROPE, pair(name), 1, 0:KEYS])
                    copy_out(sq_kv[:], acc[:, pair(name), 0, 0:KEYS], name, ACT.Square)
                elif what == "cq":
                    nc.scalar.copy(cq_z[:], out_t(name, ROWS, META))
                    copy_out(sq_cq[:], out_t(name, ROWS, META), name, ACT.Square)
                elif what in ("pool_v", "conf_a", "sc_c", "sc_x"):
                    dst = {"pool_v": pool_v, "conf_a": glu, "sc_c": sc_c, "sc_x": sc_x}[what]
                    copy_out(dst[:], out_t(name, KEYS), name)
                elif what == "conf_g":
                    copy_out(glu_g[:], out_t(name, KEYS), name, ACT.Sigmoid)
                elif what == "sc_b":
                    copy_out(sc_b[:], out_t(name, ROWS, META), name)
                else:
                    dst = {"sc_gate": sc_gate[:], "pool_gate": pool_gate[:], "conf_gate": conf_gate[:],
                           "mla_gate0": halves(mla_gate, 0), "mla_gate1": halves(mla_gate, 1)}[what]
                    copy_out(dst, out_t(name, ROWS, META), name, ACT.Silu)
                if what == "sc_gate":
                    act.wait_ge(s["trig_args"], 1)
                    act.wait_ge(s["cleared"], 3)
                    nc.scalar.activation(trig[0:ROPE, 0, :], trig_abs, ACT.Sin, bias=half_pi[0:ROPE, :], scale=-1.0)
                    nc.scalar.activation(trig[0:ROPE, 1, :], trig_r, ACT.Sin,
                                         scale=cst("sign", 1, slice(0, ROPE))).then_inc(s["trig_ready"], 1)
                    for j in range(4):
                        await_full(act, "uq%d" % j)
                        nc.scalar.copy(qT[0:QK, 2 * j:2 * j + 2, :], bank("uq%d" % j)[0:QK, :]
                                       .rearrange("p (h r) -> p h r", h=2)).then_inc(read_sem("uq%d" % j), 1)
                    for i in range(HEADS):
                        await_full(act, "kn%d" % i)
                        nc.scalar.copy(kT[0:NOPE, i, :], bank("kn%d" % i)[0:NOPE, 0:KEYS]).then_inc(read_sem("kn%d" % i), 1)
                    act.wait_ge(s["cleared"], 4)
                    for i, n in enumerate((META, P, P)):
                        await_full(act, "vt%d" % i)
                        nc.scalar.copy(vt[0:n, i, :], bank("vt%d" % i)[0:n, :]).then_inc(read_sem("vt%d" % i), 1)
                if sl.at == 23:
                    act.wait_ge(s["sc_u"], 1)
                    nc.scalar.copy(u_sc_hi[:], sc_acc[:]).then_inc(s["sc_rounded"], 1)
                if sl.at == 25:
                    await_read(act, "pool")
                    nc.scalar.copy(u_pool_hi[:], pool_gate[:]).then_inc(s["pool_rounded"], 1)

            def gate_bias(b, c):
                return col("gate_bias", BRANCH[b] * KC + c)

            before = None
            for b in ("sc", "pool", "conf"):
                for sl in over_slots(act, FIRST["gate_" + b], 8, loops=0):
                    lead(sl)
                    if b == "conf" and sl.index == 0:
                        await_read(act, "conf_mean")
                        nc.scalar.square(conf_sq[:], conv[:]).then_inc(s["conf_squared"], 1)
                    if b == "conf" and sl.index == 5:
                        act.wait_ge(s["conf_zn"], 1)
                        nc.scalar.activation(conf_sq[:, 0, :], conv[:, 0, :], ACT.Sigmoid, bias=col("conf_ln_b", 0))
                        nc.scalar.activation(conf_sq[:, 1, :], conv[:, 1, :], ACT.Sigmoid,
                                             bias=col("conf_ln_b", 1)).then_inc(s["conf_sig"], 1)
                    if sl.index % 2 == 1:
                        i = sl.index // 2
                        name = "gate_%s%d" % (b, i)
                        slot_done(act, "gate_" + b, sl.index)
                        if before:
                            await_out(act, "y_%s%d" % (before, i))
                        nc.scalar.activation(gates[:, 2 * i, :], acc[:, pair(name), 0, 0:ROWS], ACT.Sigmoid,
                                             bias=gate_bias(b, 2 * i))
                        copy_out(gates[:, 2 * i + 1, :], acc[:, pair(name), 1, 0:ROWS], name, ACT.Sigmoid,
                                 bias=gate_bias(b, 2 * i + 1))
                    if b == "conf" and sl.index == 7:
                        act.wait_ge(s["conf_u"], 1)
                        nc.scalar.copy(u_conf_hi[:], conv[:]).then_inc(s["conf_rounded"], 1)
                for sl in over_slots(act, FIRST["y_" + b], 2):
                    lead(sl)
                before = b

            def mla_probsT(i):
                await_full(act, "pt%d" % i)
                nc.scalar.copy(probsT[:, i % 2, :], bank("pt%d" % i)[:, 0:3 * P]).then_inc(read_sem("pt%d" % i), 1)
                await_full(act, "pm%d" % i)
                nc.scalar.copy(metaT[0:META, i % 2, :], bank("pm%d" % i)[0:META, 0:ROWS]).then_inc(read_sem("pm%d" % i), 1)

            def mla_u_hi(i):
                await_out(act, "heads%d" % i)
                nc.scalar.copy(u_mla_hi[:, i, :], u_mla[:, i, :]).then_inc(s["u_mla_rounded"], 1)

            act.wait_ge(s["meta_cleared"], 1)
            act.wait_ge(s["neg_bias_ready"], 1)
            for i in range(HEADS):
                lead(Slot(FIRST["gate_mla"] + i, i, None))
                act.wait_ge(s["max_ready"], i + 1)
                nc.scalar.activation(probs[:, i % 2, 0:S0], scores[:, i % 2, 0:S0], ACT.Exp, bias=neg_max[:, i % 2, 0:1],
                                     accum_out=sums[:, i % 2, 0:1])
                nc.scalar.activation(probs[:, i % 2, S0:], scores[:, i % 2, S0:], ACT.Exp, bias=neg_max[:, i % 2, 1:2],
                                     accum_out=sums[:, i % 2, 1:2]).then_inc(s["exp_done"], 1)
                if i % 2 == 1:
                    b, name = i // 2, "gate_mla%d" % (i // 2)
                    slot_done(act, "gate_mla", i)
                    await_out(act, "y_conf%d" % b)
                    nc.scalar.activation(gates[:, 2 * b, :], acc[:, pair(name), 0, 0:ROWS], ACT.Exp,
                                         bias=neg_bias[:, 2 * b:2 * b + 1], scale=-1.0)
                    copy_out(gates[:, 2 * b + 1, :], acc[:, pair(name), 1, 0:ROWS], name, ACT.Exp,
                             bias=neg_bias[:, 2 * b + 1:2 * b + 2], scale=-1.0)
                if i >= 1:
                    mla_probsT(i - 1)
                if i in (5, 7):
                    mla_u_hi((i - 5) // 2)
            mla_probsT(HEADS - 1)
            mla_u_hi(2)
            mla_u_hi(3)
            for i in range(4):
                lead(Slot(FIRST["y_mla"] + i, i, None))
                act.wait_ge(s["m_ready"], i + 1)
                nc.scalar.copy(halves(m_hi, i), halves(m, i)).then_inc(s["m_rounded"], 1)
            junk = m[:].rearrange("p c r -> p (c r)")
            for sl in over_slots(act, FIRST["w_o"], 8, loops=0):
                lead(sl)
                if sl.index % 4 == 3:
                    hf = sl.index // 4
                    name = "w_o%d" % hf
                    slot_done(act, "w_o", sl.index)
                    if hf == 0:
                        act.wait_ge(s["m_split"], 4)
                    nc.scalar.copy(y[:, :, hf * 512:(hf + 1) * 512], acc[:, pair(name), :, :])
                    for t in range(TILES):
                        k = 2 * t + hf
                        sq = nc.scalar.activation(junk[:, k * 512:(k + 1) * 512], acc[:, pair(name), t, :], ACT.Square,
                                                  accum_out=ssq[:, k:k + 1])
                    sq.then_inc(evacuated[pair(name)], 1)

            def round_rows(tag):
                for j in range(4):
                    await_full(act, "%s_%d" % (tag, j))
                    nc.scalar.copy(x_hi[:, 2 * j:2 * j + 2, 0:ROWS], bank("%s_%d" % (tag, j))
                                   .rearrange("p (c r) -> p c r", c=2)).then_inc(s["x_rounded"], 1)

            def norm_rows(k):
                act.wait_ge(s["ln_stats"], k + 1)
                for t in range(TILES):
                    nc.scalar.activation(x[:, t, :], y[:, t, :], ACT.Identity, scale=rs[:, 1, t:t + 1],
                                         bias=nmr[:, t:t + 1]).then_inc(s["ln_hat"], 1)

            round_rows("x1")
            for sl in over_slots(act, FIRST["gla_gk"], 2):
                lead(sl)
            slot_done(act, "gla_gk", 1)
            copy_out(gk_low[0:16, :], acc[0:16, pair("gla_gk"), 0, 0:ROWS], "gla_gk")
            for sl in over_slots(act, FIRST["gla_q"], 4, loops=0):
                lead(sl)
                if sl.index % 2 == 1:
                    slot_done(act, "gla_q", sl.index)
                    name = "gla_q%d" % (sl.index // 2)
                    copy_out(halves(gq, sl.index // 2), out_t(name), name, scale=float(DK) ** -0.5)
            for sl in over_slots(act, FIRST["gla_k"], 4, loops=0):
                lead(sl)
                if sl.index == 0:
                    for j in range(2):
                        await_full(act, "la%d" % j)
                        for i in range(2):
                            c = 2 * j + i
                            ab = nc.scalar.activation(la_e[:, c, :], bank("la%d" % j)[:, i * ROWS:(i + 1) * ROWS], ACT.Abs,
                                                      bias=col("gla_b_gk_2", c))
                        ab.then_inc(s["la_abs"], 1)
                    act.wait_ge(s["la_abs"], 2)
                    link(nc.scalar.activation(la_e[:], la_e[:], ACT.Exp, scale=-1.0))
                    nc.scalar.activation(la_e[:], la_e[:], ACT.Ln, bias=1.0).then_inc(s["la_log"], 1)
                if sl.index % 2 == 1:
                    slot_done(act, "gla_k", sl.index)
                    name = "gla_k%d" % (sl.index // 2)
                    copy_out(halves(gk, sl.index // 2), out_t(name), name)
                if sl.index == 2:
                    act.wait_ge(s["cum_ready"], 1)
                    nc.scalar.activation(e_cum[:], la_e[:], ACT.Exp, scale=1.0 / 16.0).then_inc(s["e_ready"], 1)
                    nc.scalar.activation(e_inv[:], la_e[:], ACT.Exp, scale=-1.0 / 16.0).then_inc(s["e_ready"], 1)
                    act.wait_ge(s["end_ready"], 1)
                    nc.scalar.activation(e_end[:], la[:], ACT.Exp, scale=1.0 / 16.0).then_inc(s["e_ready"], 1)
            for sl in over_slots(act, FIRST["gla_v"], 8, loops=0):
                lead(sl)
                if sl.index % 4 == 3:
                    hf = sl.index // 4
                    slot_done(act, "gla_v", sl.index)
                    copy_out(gv[:, :, hf * 512:(hf + 1) * 512], acc[:, pair("gla_v%d" % hf), :, :], "gla_v%d" % hf)
            for sl in over_slots(act, FIRST["gla_g"], 8, loops=0):
                lead(sl)
                if sl.index == 0:
                    act.wait_ge(s["zeroed"], 4)
                    for j in range(2):
                        await_full(act, "sg%d" % j)
                        b = bank("sg%d" % j).rearrange("p (g r) -> p g r", g=4)
                        nc.scalar.copy(intra[0:CH, 4 * j:4 * j + 4, 0:CH], b[0:CH, :, 0:CH])
                        nc.scalar.copy(intra[CH:P, 4 * j:4 * j + 4, CH:P], b[CH:P, :, CH:P]).then_inc(read_sem("sg%d" % j), 1)
                    for j in range(2):
                        await_full(act, "ke%d" % j)
                        b = bank("ke%d" % j).rearrange("p (g r) -> p g r", g=4)
                        nc.scalar.copy(ke_half[0:CH, 0, 4 * j:4 * j + 4, :], b[0:CH])
                        nc.scalar.copy(ke_half[CH:P, 1, 4 * j:4 * j + 4, :], b[CH:P]).then_inc(read_sem("ke%d" % j), 1)
                if sl.index % 4 == 3:
                    hf = sl.index // 4
                    slot_done(act, "gla_g", sl.index)
                    copy_out(gg[:, :, hf * 512:(hf + 1) * 512], acc[:, pair("gla_g%d" % hf), :, :], "gla_g%d" % hf, ACT.Silu)
            junk1 = e_inv[:].rearrange("p h r -> p (h r)")
            junk2 = e_end[:].rearrange("p h r -> p (h r)")
            for j in range(4):
                await_full(act, "o%d" % j)
                for i in range(2):
                    k = 2 * j + i
                    dst = (junk1 if k < 4 else junk2)[:, k % 4 * DV:(k % 4 + 1) * DV]
                    nc.scalar.activation(dst, bank("o%d" % j)[:, i * DV:(i + 1) * DV], ACT.Square,
                                         accum_out=ssq[:, k:k + 1]).then_inc(s["o_ssq"], 1)
            for j in range(4):
                await_full(act, "ot%d" % j)
                nc.scalar.copy(halves(o_hi, j), bank("ot%d" % j).rearrange("p (c r) -> p c r", c=2)).then_inc(s["o_rounded"], 1)
            for sl in over_slots(act, FIRST["gla_out"], 8):
                lead(sl)
            norm_rows(0)

            def swiglu(layer):
                tag = "gu%d" % layer
                for sl in over_slots(act, FIRST[tag], COUNT[tag]):
                    lead(sl)
                    og = OUT[tag + "_0"]
                    if sl.index == 1:
                        act.wait_ge(weights_used, sl.number(1))
                        nc.scalar.activation(h_gate[:], acc[:, og % 2, :, 0:ROWS], ACT.Silu).then_inc(evacuated[og % 2], 1)
                    if sl.index == 3:
                        act.wait_ge(evacuated[(og + 1) % 2], sl.loop + ((og + 1) // 2 + 1))
                        nc.scalar.copy(h_hi[:, bass.ds(sl.loop * 2, 2), :], h[:]).then_inc(s["h_rounded"], 1)
                tag = "down%d" % layer
                for sl in over_slots(act, FIRST[tag], COUNT[tag], loops=5 - layer):
                    lead(sl)

            round_rows("x2")
            swiglu(0)
            norm_rows(1)
            round_rows("x3")
            for tag, dst in (("moba_q", mq), ("moba_k", mk)):
                for sl in over_slots(act, FIRST[tag], 8, loops=0):
                    lead(sl)
                    if sl.index % 2 == 1:
                        slot_done(act, tag, sl.index)
                        name = "%s%d" % (tag, sl.index // 2)
                        copy_out(halves(dst, sl.index // 2), out_t(name), name)

            def moba_v(i):
                lead(Slot(FIRST["moba_v"] + i, i, None))
                if i % 4 == 3:
                    hf = i // 4
                    slot_done(act, "moba_v", i)
                    copy_out(mv[:, :, hf * 512:(hf + 1) * 512], acc[:, pair("moba_v%d" % hf), :, :], "moba_v%d" % hf)

            def moba_probsT(i):
                await_full(act, "mt%d" % i)
                nc.scalar.copy(mprobsT[:, i, :], bank("mt%d" % i)[:, 0:P + ROWS]).then_inc(read_sem("mt%d" % i), 1)

            for i in range(4):
                moba_v(i)
            for i in range(HEADS):
                if i < 4:
                    moba_v(4 + i)
                act.wait_ge(s["m_max"], i + 1)
                nc.scalar.activation(mprobs[:, i % 2, 0:P], mscores[:, i % 2, 0:P], ACT.Exp, bias=neg_max[:, i % 2, 0:1],
                                     accum_out=sums[:, i % 2, 0:1])
                nc.scalar.activation(mprobs[:, i % 2, P:], mscores[:, i % 2, P:], ACT.Exp, bias=neg_max[:, i % 2, 1:2],
                                     accum_out=sums[:, i % 2, 1:2]).then_inc(s["m_exp"], 1)
                if i >= 1:
                    moba_probsT(i - 1)
            moba_probsT(HEADS - 1)
            for i in range(4):
                act.wait_ge(s["m_heads_done"], 2 * i + 2)
                nc.scalar.copy(halves(mo_hi, i), out_t("moba_heads%d" % i)).then_inc(s["mo_rounded"], 1)
            for sl in over_slots(act, FIRST["moba_out"], 8):
                lead(sl)
            norm_rows(2)
            round_rows("x4")
            swiglu(1)
            norm_rows(3)

        @block.vector
        def _(dve):
            chained = [0]

            def count(ins):
                chained[0] += 1
                ins.then_inc(dve_chain, 1)
                return chained[0]

            def link(ins):
                dve.wait_ge(dve_chain, count(ins))

            def split_slot(sl, ahead):
                k = sl.ring(ahead)
                dve.wait_ge(rounded, sl.number(ahead + 1))
                nc.vector.tensor_tensor(w_lo[:, k, :], staged[:, k, :], w_hi[:, k, :].bitcast(F32),
                                        ALU.subtract).then_inc(split, 1)

            def lead(sl):
                if sl.loop is not None or sl.at + LEAD < TOTAL:
                    split_slot(sl, LEAD)

            def rest(dst, src, hi):
                return nc.vector.tensor_tensor(dst, src, hi.bitcast(F32), ALU.subtract)

            def newton(v, r, t):
                link(nc.vector.tensor_scalar(r.bitcast(I32), v.bitcast(I32), 1, None, ALU.logical_shift_right))
                link(nc.vector.tensor_scalar(r.bitcast(I32), r.bitcast(I32), -1.0, float(0x5F3759DF), ALU.mult, ALU.add))
                for step in range(3):
                    link(nc.vector.tensor_tensor(t, r, r, ALU.mult))
                    link(nc.vector.scalar_tensor_tensor(t, t, -0.5, v, ALU.mult, ALU.mult))
                    last = nc.vector.scalar_tensor_tensor(r, t, 1.5, r, ALU.add, ALU.mult)
                    if step < 2:
                        link(last)
                return last

            def mean_eps(dst, src, n, eps):
                return nc.vector.tensor_scalar(dst, src, 1.0 / n, eps, ALU.mult, ALU.add)

            def halves(dst, i):
                return dst[:, 2 * i:2 * i + 2, :]

            def out_t(name):
                return acc[:, pair(name), :, 0:ROWS]

            def taken(ins, name):
                ins.then_inc(evacuated[pair(name)], 1)

            def read(ins, name):
                ins.then_inc(read_sem(name), 1)

            dve.wait_ge(s["ssq0"], 1)
            link(mean_eps(rs[:, 0, 0:3], ssq[:, 0:3], DM, EPS))
            newton(rs[:, 0, 0:3], rs[:, 1, 0:3], rs[:, 2, 0:3]).then_inc(s["rstd0"], 1)
            for i in range(LEAD):
                split_slot(Slot(i, i, None), 0)
            await_full(dve, "vec")
            read(nc.vector.tensor_copy(vec[:, 0:VEC_N], bank("vec")[:, 0:VEC_N]), "vec")
            await_read(dve, "vec")
            nb = VEC["gate_bias"] + BRANCH["mla"] * KC
            nc.vector.tensor_scalar(neg_bias[:], vec[:, nb:nb + KC], -1.0, None, ALU.mult).then_inc(s["neg_bias_ready"], 1)
            for c in range(KC):
                dve.wait_ge(s["x0_rounded"], c + 1)
                read(nc.vector.scalar_tensor_tensor(x_lo[:, c, :], bank("x0_%d" % c)[:, 0:KEYS], col("pre_norm_g", c),
                                                    x_hi[:, c, :].bitcast(F32), ALU.mult, ALU.subtract), "x0_%d" % c)

            def trig_reduce():
                dve.wait_ge(s["pos_loaded"], 16)
                dve.wait_ge(s["const_loaded"], 16)
                link(nc.vector.tensor_scalar(trig_r, pos_i, cst("inv_freq", 1, slice(0, ROPE)), None, ALU.mult))
                magic = 1.5 * 2.0 ** 23
                link(nc.vector.tensor_scalar(trig_k, trig_r, float(1 / (2 * np.pi)), magic, ALU.mult, ALU.add))
                link(nc.vector.tensor_scalar(trig_k, trig_k, -magic, None, ALU.add))
                link(nc.vector.tensor_scalar(trig_kh, trig_k, 1.0 / 2048, magic, ALU.mult, ALU.add))
                link(nc.vector.tensor_scalar(trig_kh, trig_kh, -magic, 2048.0, ALU.add, ALU.mult))
                link(nc.vector.tensor_tensor(trig_k, trig_k, trig_kh, ALU.subtract))
                rest_2pi, parts = 2 * np.pi, []
                for bits in (11, 11, 11):
                    e = np.floor(np.log2(rest_2pi))
                    unit = 2.0 ** (e - bits + 1)
                    parts.append(np.floor(rest_2pi / unit) * unit)
                    rest_2pi -= parts[-1]
                for part in parts + [rest_2pi]:
                    for k in (trig_kh, trig_k):
                        link(nc.vector.scalar_tensor_tensor(trig_r, k, -float(part), trig_r, ALU.mult, ALU.add))
                link(nc.vector.tensor_scalar(trig_r, trig_r, 3.1415925, -3.1415925, ALU.min, ALU.max))
                nc.vector.scalar_tensor_tensor(trig_abs, trig_r, -1.0, trig_r, ALU.mult, ALU.max).then_inc(s["trig_args"], 1)

            def kvq_norm():
                v, r, t = kvq_rs
                await_full(dve, "ssq_kv")
                read(mean_eps(v[:, 0:KEYS], bank("ssq_kv")[:, 0:KEYS], P, EPS), "ssq_kv")
                await_full(dve, "ssq_cq")
                read(mean_eps(v[:, KEYS:], bank("ssq_cq")[:, 0:ROWS], 2 * P, EPS), "ssq_cq")
                await_read(dve, "ssq_kv")
                await_read(dve, "ssq_cq")
                link(newton(v, r, t))
                nc.vector.scalar_tensor_tensor(kv_z[:], kv_z[:], col("kv_norm_g"), r[:, 0:KEYS], ALU.mult, ALU.mult)
                for c in range(2):
                    last = nc.vector.scalar_tensor_tensor(cq_z[:, c, :], cq_z[:, c, :], col("q_norm_g", c), r[:, KEYS:],
                                                          ALU.mult, ALU.mult)
                last.then_inc(s["kv_normed"], 1)

            conv_last = [0, 0]

            def conv_taps(lo, hi):
                for j in range(lo, hi):
                    k = CONF_K - 1 - j
                    for c in range(2):
                        w = col("conf_dw_w", 2 * k + c)
                        if j == 0:
                            ins = nc.vector.tensor_scalar(conv[:, c, :], glu[:, c, META:KEYS], w, col("conf_dw_b", c),
                                                          ALU.mult, ALU.add)
                        else:
                            r0 = max(0, j - META)
                            dve.wait_ge(dve_chain, conv_last[c])
                            ins = nc.vector.scalar_tensor_tensor(conv[:, c, r0:], glu[:, c, META + r0 - j:KEYS - j], w,
                                                                 conv[:, c, r0:], ALU.mult, ALU.add)
                        if j == CONF_K - 1 and c == 1:
                            dve.wait_ge(dve_chain, conv_last[0])
                            ins.then_inc(s["conv_done"], 1)
                        else:
                            conv_last[c] = count(ins)

            def short_conv():
                dve.wait_ge(s["sc_ready"], 1)
                last = [0, 0]
                for k in range(SC_K):
                    for c in range(2):
                        w = col("sc_dw_w", 2 * k + c)
                        src = sc_x[:, c, META - SC_K + 1 + k:KEYS - SC_K + 1 + k]
                        if k == 0:
                            last[c] = count(nc.vector.tensor_scalar(sc_acc[:, c, :], src, w, None, ALU.mult))
                        else:
                            dve.wait_ge(dve_chain, last[c])
                            last[c] = count(nc.vector.scalar_tensor_tensor(sc_acc[:, c, :], src, w, sc_acc[:, c, :],
                                                                           ALU.mult, ALU.add))
                await_out(dve, "z7")
                dve.wait_ge(dve_chain, last[1])
                link(nc.vector.tensor_tensor(sc_acc[:], sc_acc[:], sc_b[:], ALU.mult))
                await_out(dve, "z8")
                nc.vector.tensor_tensor(sc_acc[:], sc_acc[:], sc_gate[:], ALU.mult).then_inc(s["sc_u"], 1)

            rope = slice(NOPE, QK)

            def two_heads(a):
                return a.unsqueeze(1).to_broadcast([ROPE, 2, ROWS])

            def rotate_keys():
                await_full(dve, "krs")
                read(nc.vector.tensor_tensor(rope_t[rope, 0:KEYS], bank("krs")[rope, 0:KEYS], cst("sin", KEYS, rope), ALU.mult),
                     "krs")
                await_full(dve, "krc")
                read(nc.vector.tensor_tensor(kr_t[rope, :], bank("krc")[rope, 0:KEYS], cst("cos", KEYS, rope), ALU.mult), "krc")
                await_read(dve, "krs")
                await_read(dve, "krc")
                nc.vector.tensor_tensor(kr_t[rope, :], kr_t[rope, :], rope_t[rope, 0:KEYS], ALU.add).then_inc(s["kr_roped"], 1)

            def rotate(t, q, name, sin, cos):
                await_full(dve, name)
                read(nc.vector.tensor_tensor(t, bank(name)[q.start_partition():q.start_partition() + ROPE, :]
                                             .rearrange("p (h r) -> p h r", h=2), two_heads(sin), ALU.mult), name)
                link(nc.vector.tensor_tensor(q, q, two_heads(cos), ALU.mult))
                await_read(dve, name)
                return nc.vector.tensor_tensor(q, q, t, ALU.add)

            def rotate_queries():
                dve.wait_ge(s["kr_roped"], 1)
                for j in range(4):
                    t = rope_t[rope, :].rearrange("p (h r) -> p h r", h=2)
                    rotate(t, qT[rope, 2 * j:2 * j + 2, :], "qs%d" % j, cst("sin", KEYS, rope)[:, META:],
                           cst("cos", KEYS, rope)[:, META:]).then_inc(s["q_roped"], 1)
                    dve.wait_ge(s["q_roped"], j + 1)

            for sl in over_slots(dve, 0, COUNT["z"], loops=0):
                lead(sl)
                if sl.at == 1:
                    trig_reduce()
                if sl.at == 6:
                    kvq_norm()
                if sl.at == 10:
                    dve.wait_ge(s["glu_ready"], 1)
                if 10 <= sl.at < 17:
                    conv_taps(2 * (sl.at - 10), 2 * (sl.at - 10) + 2)
                if sl.at == 18:
                    rotate_keys()
                    rotate_queries()
                if sl.at == 20:
                    short_conv()
                if sl.at == 22:
                    await_full(dve, "pool")
                    await_out(dve, "z9")
                    for c in range(2):
                        last = nc.vector.scalar_tensor_tensor(pool_gate[:, c, :], bank("pool")[:, c * ROWS:(c + 1) * ROWS],
                                                              col("pool_scale", c), pool_gate[:, c, :], ALU.mult, ALU.mult)
                    read(last, "pool")
                if sl.at == 24:
                    dve.wait_ge(s["sc_rounded"], 1)
                    rest(u_sc_lo[:], sc_acc[:], u_sc_hi[:]).then_inc(s["sc_split"], 1)

            gated = [0]

            def gate_out(b, i):
                name = "y_%s%d" % (b, i)
                if b == "sc":
                    taken(nc.vector.tensor_tensor(halves(m, i), out_t(name), halves(gates, i), ALU.mult), name)
                    return
                if b == "mla" and i >= 2:
                    dve.wait_ge(s["m_ready"], i - 1)
                elif b != "mla" and gated[0] >= 2:
                    dve.wait_ge(s["m_added"], gated[0] - 1)
                taken(nc.vector.tensor_tensor(y_gated[:, gated[0] % 2], out_t(name), halves(gates, i), ALU.mult), name)
                gated[0] += 1

            def conf_centre():
                await_full(dve, "conf_mean")
                for c in range(2):
                    last = nc.vector.scalar_tensor_tensor(conv[:, c, :], bank("conf_mean")[:, 0:ROWS], -1.0 / (2 * P),
                                                          conv[:, c, :], ALU.mult, ALU.add)
                read(last, "conf_mean")

            def conf_norm():
                v, r, t = [a[:, 0:ROWS] for a in kvq_rs]
                await_full(dve, "conf_var")
                read(mean_eps(v, bank("conf_var")[:, 0:ROWS], 2 * P, EPS), "conf_var")
                await_read(dve, "conf_var")
                link(newton(v, r, t))
                for c in range(2):
                    last = nc.vector.scalar_tensor_tensor(conv[:, c, :], conv[:, c, :], col("conf_ln_g", c), r, ALU.mult, ALU.mult)
                last.then_inc(s["conf_zn"], 1)

            def conf_operand():
                dve.wait_ge(s["conf_sig"], 1)
                for c in range(2):
                    last = nc.vector.scalar_tensor_tensor(conv[:, c, :], conv[:, c, :], col("conf_ln_b", c), conf_sq[:, c, :],
                                                          ALU.add, ALU.mult)
                link(last)
                nc.vector.tensor_tensor(conv[:], conv[:], conf_gate[:], ALU.mult).then_inc(s["conf_u"], 1)

            for b in ("sc", "pool", "conf"):
                for sl in over_slots(dve, FIRST["gate_" + b], 8, loops=0):
                    lead(sl)
                    if b == "sc" and sl.index == 0:
                        dve.wait_ge(s["pool_rounded"], 1)
                        rest(u_pool_lo[:], pool_gate[:], u_pool_hi[:]).then_inc(s["pool_split"], 1)
                    if b == "sc" and sl.index >= 1:
                        conv_taps(14 + 2 * (sl.index - 1), 16 + 2 * (sl.index - 1))
                    if b == "pool" and sl.index < 2:
                        conv_taps(28 + 2 * sl.index, min(CONF_K, 30 + 2 * sl.index))
                    if b == "conf" and sl.index == 0:
                        conf_centre()
                    if b == "conf" and sl.index == 4:
                        conf_norm()
                    if b == "conf" and sl.index == 6:
                        conf_operand()
                    if b == "conf" and sl.index == 7:
                        dve.wait_ge(s["conf_rounded"], 1)
                        rest(u_conf_lo[:], conv[:], u_conf_hi[:]).then_inc(s["conf_split"], 1)
                for sl in over_slots(dve, FIRST["y_" + b], 2):
                    lead(sl)
                    slot_done(dve, "y_" + b, sl.index)
                    gate_out(b, 2 * sl.index)
                    gate_out(b, 2 * sl.index + 1)

            def masked_max(i, name, n0, sc, scale, mask, done):
                n = sc.shape[-1]
                await_full(dve, name)
                read(nc.vector.scalar_tensor_tensor(sc, bank(name)[:, 0:n], scale, cst(mask, n), ALU.mult, ALU.add), name)
                await_read(dve, name)
                nc.vector.tensor_reduce(neg_max[:, i % 2, 0:1], sc[:, 0:n0], AX.X, ALU.max, negate=True)
                nc.vector.tensor_reduce(neg_max[:, i % 2, 1:2], sc[:, n0:], AX.X, ALU.max, negate=True).then_inc(done, 1)

            def normalise(i, pr, n0, exp_done, done):
                dve.wait_ge(exp_done, i + 1)
                link(nc.vector.reciprocal(inv_sum[:, i % 2, :], sums[:, i % 2, :]))
                nc.vector.tensor_scalar(pr[:, 0:n0], pr[:, 0:n0], inv_sum[:, i % 2, 0:1], None, ALU.mult)
                nc.vector.tensor_scalar(pr[:, n0:], pr[:, n0:], inv_sum[:, i % 2, 1:2], None, ALU.mult).then_inc(done, 1)

            def mla_norm(i):
                normalise(i, probs[:, i % 2, :], S0, s["exp_done"], s["probs_ready"])

            def mla_gated(i):
                dve.wait_ge(s["heads_done"], 2 * i + 2)
                taken(nc.vector.tensor_tensor(u_mla[:, i, :], acc[:, pair("heads%d" % i), 0, 0:ROWS], mla_gate[:, i, :],
                                              ALU.mult), "heads%d" % i)

            def mla_rest(i):
                dve.wait_ge(s["u_mla_rounded"], i + 1)
                rest(u_mla_lo[:, i, :], u_mla[:, i, :], u_mla_hi[:, i, :]).then_inc(s["u_mla_split"], 1)

            def mla_sigmoid(i):
                await_out(dve, "gate_mla%d" % i)
                link(nc.vector.tensor_scalar(halves(gates, i), halves(gates, i), 1.0, None, ALU.add))
                link(nc.vector.reciprocal(halves(gates, i), halves(gates, i)))

            for i in range(HEADS):
                lead(Slot(FIRST["gate_mla"] + i, i, None))
                if i >= 1:
                    mla_norm(i - 1)
                masked_max(i, "s%d" % i, S0, scores[:, i % 2, :], float(QK) ** -0.5, "mask_mla", s["max_ready"])
                if i in (4, 6):
                    mla_gated((i - 4) // 2)
                if i in (2, 4, 6):
                    mla_sigmoid(i // 2 - 1)
                if i == 6:
                    mla_rest(0)
            mla_norm(HEADS - 1)
            mla_sigmoid(3)
            mla_gated(2)
            mla_rest(1)
            mla_gated(3)
            mla_rest(2)
            mla_rest(3)
            dve.wait_ge(s["m_added"], 8)
            for i in range(4):
                lead(Slot(FIRST["y_mla"] + i, i, None))
                slot_done(dve, "y_mla", i)
                gate_out("mla", i)
                await_out(dve, "y_mla%d" % i)
                nc.vector.tensor_tensor(halves(m, i), halves(m, i), y_gated[:, (gated[0] - 1) % 2], ALU.add).then_inc(s["m_ready"], 1)
                dve.wait_ge(s["m_rounded"], i + 1)
                rest(halves(m_lo, i), halves(m, i), halves(m_hi, i)).then_inc(s["m_split"], 1)
            for sl in over_slots(dve, FIRST["w_o"], 8):
                lead(sl)
            await_out(dve, "w_o0")
            await_out(dve, "w_o1")
            parts = ssq[:, 0:4].rearrange("p (t h) -> p t h", t=TILES)
            link(nc.vector.tensor_tensor(rs[:, 2, 0:2], parts[:, :, 0], parts[:, :, 1], ALU.add))
            link(mean_eps(rs[:, 0, 0:2], rs[:, 2, 0:2], DM, EPS))
            link(newton(rs[:, 0, 0:2], rs[:, 1, 0:2], rs[:, 2, 0:2]))
            dve.wait_ge(s["gain_loaded"], 16)
            for t in range(TILES):
                link(nc.vector.scalar_tensor_tensor(y[:, t, :], y[:, t, :], rs[:, 1, t:t + 1], gain[:], ALU.mult, ALU.mult))
                nc.vector.tensor_tensor(x[:, t, :], x[:, t, :], y[:, t, :], ALU.add).then_inc(s["x_ready"], 1)

            splits = [0]

            def rest_rows(tag):
                for j in range(4):
                    splits[0] += 1
                    dve.wait_ge(s["x_rounded"], splits[0])
                    read(rest(x_lo[:, 2 * j:2 * j + 2, 0:ROWS], bank("%s_%d" % (tag, j)).rearrange("p (c r) -> p c r", c=2),
                              x_hi[:, 2 * j:2 * j + 2, 0:ROWS]), "%s_%d" % (tag, j))

            def residual(name, hf):
                cols = slice(hf * 512, hf * 512 + 512)
                taken(nc.vector.scalar_tensor_tensor(y[:, :, cols], x[:, :, cols], ALPHA, acc[:, pair(name), :, :],
                                                     ALU.mult, ALU.add), name)
                await_out(dve, name)
                for t in range(TILES):
                    link(nc.vector.bn_stats(stats[:, t, hf, :], y[:, t, cols]))

            def layer_norm(k):
                for t in range(TILES):
                    link(nc.vector.bn_aggr(mu_var[:, t, :], stats[:, t].rearrange("p h e -> p (h e)")))
                link(nc.vector.tensor_scalar(rs[:, 0, 0:2], mu_var[:, :, 1], LN_EPS, None, ALU.add))
                link(newton(rs[:, 0, 0:2], rs[:, 1, 0:2], rs[:, 2, 0:2]))
                nc.vector.scalar_tensor_tensor(nmr[:], mu_var[:, :, 0], -1.0, rs[:, 1, 0:2], ALU.mult,
                                               ALU.mult).then_inc(s["ln_stats"], 1)
                dve.wait_ge(s["norm_loaded"], 32 * (k + 1))
                for t in range(TILES):
                    dve.wait_ge(s["ln_hat"], 2 * k + t + 1)
                    link(nc.vector.tensor_tensor(x[:, t, :], x[:, t, :], gain[:], ALU.mult))
                    nc.vector.tensor_tensor(x[:, t, :], x[:, t, :], shift[:], ALU.add).then_inc(s["x_ready"], 1)

            rest_rows("x1")
            for stage in ("gla_gk", "gla_q"):
                for sl in over_slots(dve, FIRST[stage], COUNT[stage]):
                    lead(sl)
            for sl in over_slots(dve, FIRST["gla_k"], 4, loops=0):
                lead(sl)
                if sl.index == 0:
                    for j in range(2):
                        dve.wait_ge(s["la_abs"], j + 1)
                        for i in range(2):
                            c = 2 * j + i
                            last = nc.vector.tensor_scalar(la[:, c, :], bank("la%d" % j)[:, i * ROWS:(i + 1) * ROWS],
                                                           col("gla_b_gk_2", c), 0.0, ALU.add, ALU.min)
                        read(last, "la%d" % j)
                    dve.wait_ge(s["la_log"], 1)
                    await_read(dve, "la0")
                    await_read(dve, "la1")
                    link(nc.vector.tensor_tensor(la[:], la[:], la_e[:], ALU.subtract))
                    dve.wait_ge(s["zeroed"], 1)
                    flat = "p h r -> p (h r)"
                    nc.vector.tensor_tensor_scan(la_e[:].rearrange(flat), reset[:].rearrange(flat), la[:].rearrange(flat), 0.0,
                                                 ALU.mult, ALU.add).then_inc(s["cum_ready"], 1)
                    dve.wait_ge(s["cum_ready"], 1)
                    chunks = la_e[:].rearrange("p h (n i) -> p (h n) i", i=CH)
                    nc.vector.tensor_tensor(la[:].rearrange("p h (n i) -> p (h n) i", i=CH),
                                            chunks[:, :, CH - 1:CH].to_broadcast([P, GLA_H * NCH, CH]), chunks,
                                            ALU.subtract).then_inc(s["end_ready"], 1)
            for sl in over_slots(dve, FIRST["gla_v"], 8, loops=0):
                lead(sl)
                if sl.index == 0:
                    await_out(dve, "gla_q0")
                    await_out(dve, "gla_q1")
                    dve.wait_ge(s["e_ready"], 3)
                    nc.vector.tensor_tensor(qd[:], gq[:], e_cum[:], ALU.mult).then_inc(s["qd_ready"], 1)
                if sl.index == 1:
                    await_out(dve, "gla_k0")
                    await_out(dve, "gla_k1")
                    nc.vector.tensor_tensor(ki[:], gk[:], e_inv[:], ALU.mult).then_inc(s["ki_ready"], 1)
                if sl.index == 2:
                    nc.vector.tensor_tensor(ke[:], gk[:], e_end[:], ALU.mult).then_inc(s["ke_ready"], 1)
            for sl in over_slots(dve, FIRST["gla_g"], 8, loops=0):
                lead(sl)
                if sl.index == 3:
                    for hd in range(GLA_H):
                        a, b = "upd%da" % hd, "upd%db" % hd
                        await_full(dve, a)
                        nc.vector.tensor_copy(state[:, hd, 0, :], bank(a)[:, 0:DV]).then_inc(s["state_ready"], 1)
                        dve.wait_ge(s["state_ready"], hd + 1)
                        read(nc.vector.scalar_tensor_tensor(state[:, hd, 1, :], state[:, hd, 0, :],
                                                            e_cum[:, hd, 2 * CH - 1:2 * CH], bank(a)[:, DV:2 * DV],
                                                            ALU.mult, ALU.add), a)
                        await_full(dve, b)
                        await_read(dve, a)
                        read(nc.vector.scalar_tensor_tensor(state[:, hd, 2, :], state[:, hd, 1, :],
                                                            e_cum[:, hd, 3 * CH - 1:3 * CH], bank(b)[:, 0:DV],
                                                            ALU.mult, ALU.add), b)
            dve.wait_ge(s["o_ssq"], 8)
            link(mean_eps(rs[:, 0, :], ssq[:], DV, EPS))
            link(newton(rs[:, 0, :], rs[:, 1, :], rs[:, 2, :]))
            dve.wait_ge(s["gg_ready"], 2)
            for j in range(4):
                t = j // 2
                for i in range(2):
                    hd = j % 2 * 2 + i
                    cols = slice(hd * DV, (hd + 1) * DV)
                    last = nc.vector.scalar_tensor_tensor(gg[:, t, cols], bank("o%d" % j)[:, i * DV:(i + 1) * DV],
                                                          rs[:, 1, 2 * j + i:2 * j + i + 1], gg[:, t, cols], ALU.mult, ALU.mult)
                read(last, "o%d" % j)
            for j in range(4):
                dve.wait_ge(s["o_rounded"], j + 1)
                read(rest(halves(o_lo, j), bank("ot%d" % j).rearrange("p (c r) -> p c r", c=2), halves(o_hi, j)), "ot%d" % j)

            def out_stage(stage):
                for sl in over_slots(dve, FIRST[stage], 8, loops=0):
                    lead(sl)
                    if sl.index % 4 == 3:
                        slot_done(dve, stage, sl.index)
                        residual("%s%d" % (stage, sl.index // 4), sl.index // 4)

            out_stage("gla_out")
            layer_norm(0)

            def swiglu(layer):
                tag = "gu%d" % layer
                og = OUT[tag + "_0"]
                for sl in over_slots(dve, FIRST[tag], COUNT[tag]):
                    lead(sl)
                    if sl.index == 3:
                        dve.wait_ge(weights_used, sl.number(1))
                        dve.wait_ge(evacuated[og % 2], sl.loop + (og // 2 + 1))
                        nc.vector.tensor_tensor(h[:], h_gate[:], acc[:, (og + 1) % 2, :, 0:ROWS],
                                                ALU.mult).then_inc(evacuated[(og + 1) % 2], 1)
                        dve.wait_ge(s["h_rounded"], sl.loop + (layer * (FCH // 2) + 1))
                        rest(h_lo[:, bass.ds(sl.loop * 2, 2), :], h[:],
                             h_hi[:, bass.ds(sl.loop * 2, 2), :]).then_inc(s["h_split"], 1)
                tag = "down%d" % layer
                for sl in over_slots(dve, FIRST[tag], COUNT[tag], loops=5 - layer):
                    lead(sl)
                slot_done(dve, tag, FCH - 1)
                for hf in range(2):
                    residual("%s_%d" % (tag, hf), hf)

            rest_rows("x2")
            swiglu(0)
            layer_norm(1)
            rest_rows("x3")
            r32 = slice(0, ROPE)

            def moba_rotate(tag, src, done):
                t = mrope[r32, :].rearrange("p (h r) -> p h r", h=2)
                for j in range(4):
                    ins = rotate(t, src[r32, 2 * j:2 * j + 2, :], "%s%d" % (tag, j), trig[r32, 1, :], trig[r32, 0, :])
                    ins.then_inc(done, 1)
                    dve.wait_ge(done, j + 1)

            for sl in over_slots(dve, FIRST["moba_q"], 8):
                lead(sl)
            dve.wait_ge(s["trig_ready"], 1)
            for sl in over_slots(dve, FIRST["moba_k"], 8, loops=0):
                lead(sl)
                if sl.index == 4:
                    moba_rotate("rq", mq, s["mq_roped"])
            for i in range(4):
                lead(Slot(FIRST["moba_v"] + i, i, None))
                if i == 2:
                    moba_rotate("rk", mk, s["mk_roped"])

            def moba_norm(i):
                normalise(i, mprobs[:, i % 2, :], P, s["m_exp"], s["m_probs"])

            for i in range(HEADS):
                if i < 4:
                    lead(Slot(FIRST["moba_v"] + 4 + i, 4 + i, None))
                if i >= 1:
                    moba_norm(i - 1)
                masked_max(i, "ms%d" % i, P, mscores[:, i % 2, :], float(HD) ** -0.5, "mask_moba", s["m_max"])
            moba_norm(HEADS - 1)
            for i in range(4):
                dve.wait_ge(s["mo_rounded"], i + 1)
                taken(rest(halves(mo_lo, i), out_t("moba_heads%d" % i), halves(mo_hi, i)), "moba_heads%d" % i)
            out_stage("moba_out")
            layer_norm(2)
            rest_rows("x4")
            swiglu(1)
            layer_norm(3)

        @block.gpsimd
        def _(pool):
            chained = [0]

            def link(ins):
                chained[0] += 1
                ins.then_inc(pool_chain, 1)
                pool.wait_ge(pool_chain, chained[0])

            nc.gpsimd.memset(ssq[:], 0.0).then_inc(s["cleared"], 1)
            nc.gpsimd.memset(w_pool[:], 0.0).then_inc(s["cleared"], 1)
            nc.gpsimd.memset(half_pi[:], float(np.pi / 2)).then_inc(s["cleared"], 1)
            nc.gpsimd.memset(vt[:, 0, :], 0.0).then_inc(s["cleared"], 1)
            await_out(pool, "z2")
            src, reach = pool_v, 1
            for g, dst in enumerate((pool_a, pool_b, pool_a, pool_b)):
                w = 2 * reach
                lo = w - 1
                link(nc.gpsimd.tensor_tensor(dst[:, :, lo:], src[:, :, lo:], src[:, :, lo - reach:KEYS - reach], ALU.add))
                r = slice(g % 2 * 64, g % 2 * 64 + 64)
                link(nc.gpsimd.tensor_scalar(pooled[r, g // 2, :], dst[r, g // 2, META:], 1.0 / w, None, ALU.mult))
                ins = nc.gpsimd.tensor_tensor(pooled[r, g // 2, :], pooled[r, g // 2, :], pool_v[r, g // 2, META:], ALU.subtract)
                if g < 3:
                    link(ins)
                else:
                    ins.then_inc(s["pooled_ready"], 1)
                src, reach = dst, w
            pool.wait_ge(s["pooled_ready"], 1)
            await_out(pool, "z3")
            await_out(pool, "z4")
            nc.gpsimd.tensor_tensor(glu[:], glu[:], glu_g[:], ALU.mult).then_inc(s["glu_ready"], 1)
            await_out(pool, "z5")
            await_out(pool, "z6")
            nc.gpsimd.tensor_tensor(sc_x[:], sc_c[:], sc_x[:], ALU.mult).then_inc(s["sc_ready"], 1)
            pool.wait_ge(s["sc_ready"], 1)
            pool.wait_ge(s["kr_roped"], 1)
            for i in range(HEADS):
                last = nc.gpsimd.tensor_copy(kT[NOPE:QK, i, :], kr_t[NOPE:QK, :])
            last.then_inc(s["k_spread"], 1)
            pool.wait_ge(s["k_spread"], 1)
            pool.wait_ge(s["sc_split"], 1)
            pool.wait_ge(s["pool_split"], 1)
            nc.gpsimd.memset(metaT[:], 0.0).then_inc(s["meta_cleared"], 1)
            n = 0
            for b in ("pool", "conf"):
                for i in range(4):
                    await_out(pool, "y_%s%d" % (b, i))
                    if n >= 4:
                        pool.wait_ge(s["m_added"], n - 3)
                    nc.gpsimd.tensor_tensor(m[:, 2 * i:2 * i + 2, :], m[:, 2 * i:2 * i + 2, :], y_gated[:, n % 2],
                                            ALU.add).then_inc(s["m_added"], 1)
                    n += 1

            def load_norm(k):
                pool.wait_ge(s["x_ready"], 2 * k + 2)
                pool.dma_start(gain[:], d["ln_g_2"][k // 2, k % 2].partition_broadcast(P)).then_inc(s["norm_loaded"], 16)
                pool.dma_start(shift[:], d["ln_b_2"][k // 2, k % 2].partition_broadcast(P)).then_inc(s["norm_loaded"], 16)

            load_norm(0)
            link(nc.gpsimd.memset(reset[:], 1.0))
            nc.gpsimd.memset(reset[:].rearrange("p h (n i) -> p (h n) i", i=CH)[:, :, 0:1], 0.0).then_inc(s["zeroed"], 1)
            nc.gpsimd.memset(intra[:], 0.0).then_inc(s["zeroed"], 1)
            nc.gpsimd.memset(ke_half[:], 0.0).then_inc(s["zeroed"], 1)
            nc.gpsimd.memset(qd_half[:], 0.0).then_inc(s["zeroed"], 1)
            pool.wait_ge(s["qd_ready"], 1)
            pool.wait_ge(s["zeroed"], 4)
            for c in range(2):
                view = "p h (t c i) -> p (h t) c i"
                nc.gpsimd.tensor_copy(qd_half[:, c].rearrange(view, t=TILES, c=2)[:, :, c, :],
                                      qd[:].rearrange(view, t=TILES, c=2)[:, :, c, :]).then_inc(s["half_ready"], 1)
            await_read(pool, "sg0")
            await_read(pool, "sg1")
            pool.wait_ge(s["half_ready"], 2)
            for c in range(2):
                if c == 1:
                    pool.wait_ge(s["intra_ready"], 1)
                blk = intra[c * CH:c * CH + CH, :, c * CH:c * CH + CH]
                nc.gpsimd.affine_select(out=blk, in_=blk, pattern=[[0, GLA_H * TILES], [1, CH]], compare_op=ALU.is_ge, fill=0.0,
                                        base=0, channel_multiplier=-1).then_inc(s["intra_ready"], 1)
            pool.wait_ge(s["gk_loaded"], 32)
            pool.wait_ge(s["intra_ready"], 2)
            for hf in range(2):
                await_out(pool, "gla_g%d" % hf)
                for t in range(TILES):
                    g = gg[:, t, hf * 512:(hf + 1) * 512].rearrange("p (h e) -> p h e", h=2)
                    last = nc.gpsimd.tensor_tensor(g, g, head_gain[:].unsqueeze(1).to_broadcast([P, 2, DV]), ALU.mult)
                last.then_inc(s["gg_ready"], 1)
            for k in range(1, 4):
                load_norm(k)


_NAMES = ["x", "meta_tokens", "pre_norm_g", "w_in", "gate_bias", "pool_w", "pool_scale", "w_out_pool", "q_norm_g", "w_uq",
          "kv_norm_g", "w_ukv", "w_out_mla", "conf_dw_w", "conf_dw_b", "conf_ln_g", "conf_ln_b", "w_out_conf", "sc_dw_w",
          "w_out_sc", "w_o", "post_norm_g", "positions_2", "gla_w_in_2", "gla_w_gk_2", "gla_b_gk_2", "gla_norm_g_2",
          "gla_w_out_2", "moba_w_in_2", "moba_w_out_2", "ffn_w_gu_2", "ffn_w_down_2", "ln_g_2", "ln_b_2"]


def kernel(**inputs):
    import concourse.bacc as bacc
    from concourse.bass_utils import run_bass_kernel_spmd

    nc = bacc.Bacc("TRN2", target_bir_lowering=False, num_devices=1)
    arrays = {n: np.ascontiguousarray(inputs[n]) for n in _NAMES}
    arrays["constants"] = constants()
    d = {n: nc.dram_tensor("in_" + n, a.shape, mybir.dt.from_np(a.dtype), kind="ExternalInput").ap()
         for n, a in arrays.items()}
    out = nc.dram_tensor("out", (1, ROWS, DM), F32, kind="ExternalOutput").ap()
    hybrid_stack(nc, d, out)
    r = run_bass_kernel_spmd(nc, [{"in_" + n: a for n, a in arrays.items()}], core_ids=[0])
    return r.results[0]["out"]
```

```python
from contextlib import ExitStack

import numpy as np

import concourse.bass as bass
import concourse.mybir as mybir

F32 = mybir.dt.float32
F32R = mybir.dt.float32r
I32 = mybir.dt.int32
ALU = mybir.AluOpType
ACT = mybir.ActivationFunctionType
AX = mybir.AxisListType

P = 128
ROWS, META, DM = 256, 16, 1024
KEYS = ROWS + META
TILES, KC = ROWS // P, DM // P
EPS, LN_EPS = 1e-6, 1e-5
ALPHA = (2.0 * 2) ** 0.25
SLOT, RING, LEAD = 1024, 4, 3
HEADS, NOPE, ROPE, VD = 8, 64, 32, 64
QK = NOPE + ROPE
CONF_K, SC_K = 31, 3
GLA_H, DK, DV, CH = 4, 128, 256, 64
NCH = ROWS // CH
FFN = 2816
FCH = FFN // P
HD = 128
NEG = -1e30

Z_BLOCKS = [("ckv_kr", 768), ("cq", 512), ("pool_v", 0), ("conf_a", 1440), ("conf_g", 1696), ("sc_c", 2464),
            ("sc_x", 2720), ("sc_b", 2208), ("sc_gate", 2976), ("pool_gate", 256), ("conf_gate", 1952),
            ("mla_gate0", 928), ("mla_gate1", 1184)]
GATE_COL0 = 3232
BRANCH = {"pool": 0, "mla": 1, "conf": 2, "sc": 3}

STAGES = [("z", 26), ("gate_sc", 8)]
for _u, _b in (("sc", "pool"), ("pool", "conf"), ("conf", "mla")):
    STAGES += [("y_%s0" % _u, 1), ("gate_%s0" % _b, 4), ("y_%s1" % _u, 1), ("gate_%s1" % _b, 4)]
STAGES += [("y_mla", 4), ("w_o", 8), ("gla_gk", 2), ("gla_q", 4), ("gla_k", 4), ("gla_v", 8), ("gla_g", 8),
           ("gla_out", 8), ("gu0", 44), ("down0", 22), ("moba_q", 8), ("moba_k", 8), ("moba_v", 8), ("moba_out", 8),
           ("gu1", 44), ("down1", 22)]
FIRST, COUNT, TOTAL = {}, {}, 0
for _name, _n in STAGES:
    FIRST[_name], COUNT[_name] = TOTAL, _n
    TOTAL += _n

OUTS = ["z%d" % _i for _i in range(13)]
OUTS += ["gate_sc%d" % _i for _i in range(4)]
for _u, _b in (("sc", "pool"), ("pool", "conf")):
    for _i in (0, 2):
        OUTS += ["y_%s%d" % (_u, _i), "y_%s%d" % (_u, _i + 1), "gate_%s%d" % (_b, _i), "gate_%s%d" % (_b, _i + 1)]
OUTS += ["y_conf0", "y_conf1", "gate_mla0", "gate_mla1", "heads0", "y_conf2", "y_conf3", "heads1", "gate_mla2", "heads2",
         "gate_mla3", "heads3"]
OUTS += ["y_mla%d" % _i for _i in range(4)] + ["w_o0", "w_o1", "gla_gk", "gla_q0", "gla_q1", "gla_k0", "gla_k1",
                                              "gla_v0", "gla_v1", "gla_g0", "gla_g1", "gla_out0", "gla_out1"]
OUTS += ["gu0_%d" % _i for _i in range(22)] + ["down0_0", "down0_1"]
OUTS += ["moba_q%d" % _i for _i in range(4)] + ["moba_k%d" % _i for _i in range(4)] + ["moba_v0", "moba_v1"]
OUTS += ["moba_heads%d" % _i for _i in range(4)] + ["moba_out0", "moba_out1"]
OUTS += ["gu1_%d" % _i for _i in range(22)] + ["down1_0", "down1_1"]
OUT = {_n: _i for _i, _n in enumerate(OUTS)}

MISC = ["vec"] + ["x0_%d" % _i for _i in range(KC)] + ["ssq_kv", "ssq_cq"]
MISC += ["uq%d" % _i for _i in range(4)] + ["kn%d" % _i for _i in range(8)] + ["vt%d" % _i for _i in range(3)]
MISC += ["pool", "krs", "krc"] + ["qs%d" % _i for _i in range(4)] + ["conf_mean", "conf_var"]
for _h in range(HEADS + 2):
    MISC += (["s%d" % _h] if _h < HEADS else []) + (["pt%d" % (_h - 2), "pm%d" % (_h - 2)] if _h >= 2 else [])
MISC += ["x1_%d" % _i for _i in range(4)] + ["la0", "la1", "sg0", "sg1", "ke0", "ke1"]
for _h in range(GLA_H):
    MISC += ["upd%da" % _h, "upd%db" % _h]
MISC += ["o%d" % _i for _i in range(4)] + ["ot%d" % _i for _i in range(4)] + ["x2_%d" % _i for _i in range(4)]
MISC += ["x3_%d" % _i for _i in range(4)]
for _h in range(HEADS + 2):
    MISC += (["ms%d" % _h] if _h < HEADS else []) + (["mt%d" % (_h - 2)] if _h >= 2 else [])
MISC += ["x4_%d" % _i for _i in range(4)]
TAILS = {_n: _i + 1 for _i, _n in enumerate(["w_o", "gla_out", "moba_out"])}
BANK = {_n: _i for _i, _n in enumerate(MISC)}

VEC_ROWS = [("pre_norm_g", 8), ("gate_bias", 32), ("pool_scale", 2), ("q_norm_g", 2), ("kv_norm_g", 1),
            ("conf_dw_w", 2 * CONF_K), ("conf_dw_b", 2), ("conf_ln_g", 2), ("conf_ln_b", 2), ("sc_dw_w", 2 * SC_K),
            ("gla_b_gk_2", 4)]
VEC, VEC_N = {}, 0
for _name, _n in VEC_ROWS:
    VEC[_name] = VEC_N
    VEC_N += _n

S0, S1 = META + P, META + ROWS
CONST = {}
CONST_N = 0
for _name, _n in [("ident", P), ("ones", P), ("mask_mla", S0 + S1), ("mask_moba", P + ROWS), ("cos", KEYS),
                  ("sin", KEYS), ("swap", ROPE), ("inv_freq", 1), ("sign", 1)]:
    CONST[_name] = CONST_N
    CONST_N += _n


def constants():
    c = np.zeros((P, CONST_N), np.float32)

    def put(name, rows, block):
        c[rows, CONST[name]:CONST[name] + block.shape[1]] = block

    every = slice(0, P)
    put("ident", every, np.eye(P, dtype=np.float32))
    put("ones", every, np.ones((P, P), np.float32))
    q, k = np.arange(P)[:, None], np.arange(S1)[None, :]
    m0 = np.where(k[:, :S0] <= q + META, 0, NEG)
    m1 = np.where(k <= q + META + P, 0, NEG)
    put("mask_mla", every, np.concatenate([m0, m1], 1).astype(np.float32))
    k = np.arange(ROWS)[None, :]
    put("mask_moba", every, np.concatenate([np.where(k[:, :P] <= q, 0, NEG), np.where(k <= q + P, 0, NEG)], 1)
        .astype(np.float32))
    inv = (1.0 / (np.float32(10000.0) ** (np.arange(0, ROPE, 2, dtype=np.float32) / np.float32(ROPE)))).astype(np.float32)
    ang = (np.arange(KEYS, dtype=np.float32)[None, :] * inv[:, None]).astype(np.float32)
    rope = slice(NOPE, NOPE + ROPE)
    put("cos", rope, np.concatenate([np.cos(ang), np.cos(ang)]).astype(np.float32))
    put("sin", rope, np.concatenate([-np.sin(ang), np.sin(ang)]).astype(np.float32))
    swap = np.roll(np.eye(ROPE, dtype=np.float32), ROPE // 2, axis=1)
    put("swap", slice(0, ROPE), swap)
    put("swap", rope, swap)
    inv2 = np.power(np.float32(500000.0), -np.arange(0, 32, 2, dtype=np.float32) / np.float32(32)).astype(np.float32)
    put("inv_freq", slice(0, 32), np.concatenate([inv2, inv2])[:, None])
    put("sign", slice(0, 32), np.concatenate([-np.ones(16), np.ones(16)]).astype(np.float32)[:, None])
    return c


Z_TAPS = {10 + _i: (2 * _i, 2 * _i + 2) for _i in range(7)}
Z_TAPS.update({17: (14, 15), 18: (15, 16), 20: (16, 17), 21: (17, 18), 23: (18, 19), 25: (19, 21)})


class Slot:

    def __init__(self, at, index, loop, body=RING):
        self.at, self.index, self.loop, self.body = at, index, loop, body

    def number(self, ahead=0):
        return self.at + ahead if self.loop is None else self.loop * self.body + (self.at + ahead)

    def ring(self, ahead=0):
        return (self.at + ahead) % RING

    def uses(self, ahead=0):
        n = (self.at + ahead) // RING
        return n if self.loop is None else self.loop * (self.body // RING) + n


def over_slots(eng, first, count, loops=None, body=RING):
    groups = count // body if loops is None else loops
    done = 0
    if groups >= 2:
        with eng.Fori(0, groups) as g:
            for j in range(body):
                yield Slot(first + j, j, g, body)
        done = body * groups
    for j in range(done, count):
        yield Slot(first + j, j, None)


def hybrid_stack(nc, d, out):
    with ExitStack() as ctx:
        cursor = [(nc.sbuf_base + 63) // 64 * 64]

        def place(name, cols, dt=F32):
            cols = [cols] if isinstance(cols, int) else list(cols)
            t = nc.alloc_sbuf_tensor_at(name, [P] + cols, dt, offset=cursor[0])
            cursor[0] += (int(np.prod(cols)) * 4 + 31) // 32 * 32
            return t

        staged = place("staged", [RING, SLOT])
        w_hi = place("w_hi", [RING, SLOT], F32R)
        w_lo = place("w_lo", [RING, SLOT], F32R)
        const = place("const", CONST_N)
        vec_rows = place("vec_rows", P)
        vec = place("vec", P)
        x = place("x", [TILES, DM])
        y = place("y", [TILES, DM])
        x_hi = place("x_hi", [KC, KEYS], F32R)
        x_lo = place("x_lo", [KC, KEYS], F32R)
        gain = place("gain", DM)
        shift = place("shift", DM)
        trig = place("trig", [2, ROWS])
        w_gk = place("w_gk", GLA_H * DK)
        head_gain = place("head_gain", DV)
        ssq = place("ssq", 8)
        rs = place("rs", [3, 8])
        mu_var = place("mu_var", [2, 2])
        stats = place("stats", [2, 2, 6])
        half_pi = place("half_pi", 1)
        neg_max = place("neg_max", [2, 2])
        sums = place("sums", [2, 2])
        inv_sum = place("inv_sum", [2, 2])
        region = cursor[0]

        kT = place("kT", [HEADS, KEYS])
        qT = place("qT", [HEADS, ROWS])
        end_qk = cursor[0]
        vt = place("vt", [3, HEADS * VD])
        mla_gate = place("mla_gate", [4, ROWS])
        conv = place("conv", [2, ROWS])
        conf_gate = place("conf_gate", [2, ROWS])
        glu = place("glu", [2, KEYS])
        glu_g = place("glu_g", [2, KEYS])
        gates = place("gates", [KC, ROWS])
        conf_sq = place("conf_sq", [2, ROWS])
        early = cursor[0]
        kv_z = place("kv_z", KEYS)
        kr_z = place("kr_z", KEYS)
        cq_z = place("cq_z", [2, ROWS])
        sq_kv = place("sq_kv", KEYS)
        sq_cq = place("sq_cq", [2, ROWS])
        w_uq = place("w_uq", [2, HEADS * QK])
        w_ukv = place("w_ukv", HEADS * (NOPE + VD))
        early_end = cursor[0]
        cursor[0] = early
        m = place("m", [KC, ROWS])
        y_gated = place("y_gated", [2, 2, ROWS])
        u_pool_hi = place("u_pool_hi", [2, ROWS], F32R)
        u_pool_lo = place("u_pool_lo", [2, ROWS], F32R)
        u_conf_hi = place("u_conf_hi", [2, ROWS], F32R)
        u_conf_lo = place("u_conf_lo", [2, ROWS], F32R)
        cursor[0] = max(cursor[0], early_end)
        u_sc_hi = place("u_sc_hi", [2, ROWS], F32R)
        u_sc_lo = place("u_sc_lo", [2, ROWS], F32R)
        rope_t = place("rope_t", 2 * ROWS)
        kr_t = place("kr_t", KEYS)
        mid = cursor[0]
        pool_v = place("pool_v", [2, KEYS])
        pool_a = place("pool_a", [2, KEYS])
        pool_b = place("pool_b", [2, KEYS])
        pooled = place("pooled", [2, ROWS])
        pool_gate = place("pool_gate", [2, ROWS])
        w_pool = place("w_pool", [2, P])
        sc_c = place("sc_c", [2, KEYS])
        sc_x = place("sc_x", [2, KEYS])
        sc_b = place("sc_b", [2, ROWS])
        sc_gate = place("sc_gate", [2, ROWS])
        sc_acc = place("sc_acc", [2, ROWS])
        mid_end = cursor[0]
        cursor[0] = mid
        scores = place("scores", [2, S0 + S1])
        probs = place("probs", [2, S0 + S1])
        probsT = place("probsT", [2, 3 * P])
        metaT = place("metaT", [2, ROWS])
        u_mla_hi = place("u_mla_hi", [4, ROWS], F32R)
        u_mla_lo = place("u_mla_lo", [4, ROWS], F32R)
        u_mla = place("u_mla", [4, ROWS])
        end1 = max(cursor[0], mid_end)
        cursor[0] = region
        m_hi = place("m_hi", [KC, ROWS], F32R)
        m_lo = place("m_lo", [KC, ROWS], F32R)
        assert cursor[0] <= end_qk

        cursor[0] = region
        gq = place("gq", [GLA_H, ROWS])
        gk = place("gk", [GLA_H, ROWS])
        la = place("la", [GLA_H, ROWS])
        la_e = place("la_e", [GLA_H, ROWS])
        gla_dead = cursor[0]
        gk_low = place("gk_low", ROWS)
        reset = place("reset", [GLA_H, ROWS])
        e_cum = place("e_cum", [GLA_H, ROWS])
        e_inv = place("e_inv", [GLA_H, ROWS])
        e_end = place("e_end", [GLA_H, ROWS])
        qd = place("qd", [GLA_H, ROWS])
        qd_half = place("qd_half", [2, GLA_H, ROWS])
        ki = place("ki", [GLA_H, ROWS])
        ke = place("ke", [GLA_H, ROWS])
        ke_half = place("ke_half", [2, GLA_H * TILES, P])
        gv = place("gv", [TILES, GLA_H * DV])
        gg = place("gg", [TILES, GLA_H * DV])
        state = place("state", [GLA_H, NCH - 1, DV])
        intra = place("intra", [GLA_H * TILES, P])
        end2 = cursor[0]
        cursor[0] = region
        o_hi = place("o_hi", [KC, ROWS], F32R)
        o_lo = place("o_lo", [KC, ROWS], F32R)
        assert cursor[0] <= gla_dead

        cursor[0] = region
        h_hi = place("h_hi", [FCH, ROWS], F32R)
        h_lo = place("h_lo", [FCH, ROWS], F32R)
        h_gate = place("h_gate", [2, ROWS])
        hidden = place("hidden", [2, ROWS])
        ffn_end = cursor[0]

        cursor[0] = region
        mo_hi = place("mo_hi", [KC, ROWS], F32R)
        mo_lo = place("mo_lo", [KC, ROWS], F32R)
        mq = place("mq", [HEADS, ROWS])
        mk = place("mk", [HEADS, ROWS])
        mv = place("mv", [TILES, DM])
        mscores = place("mscores", [2, P + ROWS])
        mprobs = place("mprobs", [2, P + ROWS])
        mprobsT = place("mprobsT", [HEADS, P + ROWS])
        mrope = place("mrope", 2 * ROWS)
        mq_swap = place("mq_swap", [HEADS, ROWS])
        mk_swap = place("mk_swap", [HEADS, ROWS])
        end4 = cursor[0]
        assert max(end1, end2, ffn_end, end4) <= nc.sbuf_usable_end, (end1, end2, ffn_end, end4, nc.sbuf_usable_end)

        scratch = y[:].rearrange("p t c -> p (t c)")
        flat_gates = gates[:].rearrange("p c r -> p (c r)")
        m_rows, meta_h = flat_gates[0:META, 0:DM], flat_gates[0:META, DM:2 * DM]
        pos_i = kr_t[0:ROPE, 0:ROWS].bitcast(I32)
        trig_r, trig_abs = rope_t[0:ROPE, 0:ROWS], rope_t[0:ROPE, ROWS:2 * ROWS]
        trig_k, trig_kh = conf_sq[0:ROPE, 0, :], conf_sq[0:ROPE, 1, :]
        kvq_rs = [scratch[:, i * 528:(i + 1) * 528] for i in range(3)]

        acc = ctx.enter_context(nc.psum_tensor("acc", [P, 2, 2, 512], F32))
        misc = ctx.enter_context(nc.psum_tensor("misc", [P, 4, 512], F32))

        def sem(name):
            return ctx.enter_context(nc.semaphore(name))

        landed = [sem("landed%d" % i) for i in range(RING)]
        rounded, split, weights_used = sem("rounded"), sem("split"), sem("weights_used")
        evacuated = [sem("evacuated%d" % i) for i in range(2)]
        bank_full = [sem("bank_full%d" % i) for i in range(4)]
        bank_read = [sem("bank_read%d" % i) for i in range(4)]
        dve_chain, act_chain, pool_chain = sem("dve_chain"), sem("act_chain"), sem("pool_chain")
        s = {n: sem(n) for n in (
            "cleared", "conf_rounded", "conf_sig", "conf_split", "conf_squared", "conf_u",
            "conf_zn", "const_loaded", "conv_done", "cum_ready", "e_ready",
            "end_ready", "exp_done", "gain_loaded", "o_gated", "gg0_ready", "gg1_ready", "swapped_q0", "swapped_q1", "swapped_k0", "swapped_k1", "down_part","gk_loaded", "glu_ready",
            "h_rounded", "h_split", "half_ready", "heads_done", "intra_ready", "k_spread", "tile0_done", "wo_ssq",
            "ke_ready", "ki_ready", "kr_roped", "kv_normed", "la_abs", "la_log",
            "m_added", "mla_gates", "y_first", "m_exp", "m_heads_done", "m_max",
            "m_probs", "m_ready", "m_rounded", "m_split", "max_ready", "meta_cleared",
            "mk_roped", "mla_loaded", "mo_rounded", "mq_roped", "norm_loaded", "normed",
            "o_rounded", "o_ssq", "pool_loaded", "pool_rounded", "pool_split", "pooled_ready",
            "pos_loaded", "probs_ready", "q_roped", "qd_ready", "rstd0", "sc_ready",
            "sc_rounded", "sc_split", "sc_u", "ssq0", "state_ready", "stored",
            "trig_args", "trig_ready", "u_mla_rounded", "u_mla_split", "vec_loaded", "x0_rounded",
            "x_loaded", "x1_loaded", "meta_loaded", "tables_loaded", "x_ready0", "x_ready1", "scaled0", "rstd_tile0", "x_rounded", "zeroed")}

        def col(name, i=0):
            return vec[:, VEC[name] + i:VEC[name] + i + 1]

        def cst(name, n, rows=slice(0, P)):
            return const[rows, CONST[name]:CONST[name] + n]

        ident, ones = cst("ident", P), cst("ones", P)

        def pair(name):
            return OUT[name] % 2

        def await_out(eng, name):
            eng.wait_ge(evacuated[OUT[name] % 2], OUT[name] // 2 + 1)

        def bank(name):
            return misc[:, BANK[name] % 4, :]

        def await_full(eng, name):
            eng.wait_ge(bank_full[BANK[name] % 4], BANK[name] // 4 + 1)

        def await_read(eng, name):
            eng.wait_ge(bank_read[BANK[name] % 4], BANK[name] // 4 + 1)

        def read_sem(name):
            return bank_read[BANK[name] % 4]

        def slot_done(eng, stage, index):
            eng.wait_ge(weights_used, FIRST[stage] + index + 1)

        block = ctx.enter_context(nc.Block())

        @block.sync
        def _(sp):
            def slot_free(sl):
                if sl.loop is not None or sl.at >= RING:
                    sp.wait_ge(split, sl.number(1 - RING))

            def load(sl, src, cols=None):
                slot_free(sl)
                dst = staged[:, sl.ring(), :]
                if len(src.shape) == 3:
                    dst = dst.rearrange("p (c n) -> p c n", c=src.shape[1])
                if cols is not None:
                    dst = staged[:, sl.ring(), :].rearrange("p (c n) -> p c n", c=src.shape[1])[:, :, 0:cols]
                sp.dma_start(dst, src).then_inc(landed[sl.ring()], 16)

            def k_half(w, half, c0, n=256):
                return w[half * 512:(half + 1) * 512, bass.ds(c0, n)].rearrange("(c p) n -> p c n", p=P)

            def by_columns(stage, w, c0):
                for sl in over_slots(sp, FIRST[stage], COUNT[stage]):
                    block0 = c0 + sl.index // 2 * 256
                    load(sl, k_half(w, sl.index % 2, block0 if sl.loop is None else sl.loop * 512 + block0))

            def by_rows(stage, w, c0=0):
                for sl in over_slots(sp, FIRST[stage], COUNT[stage]):
                    q = sl.index % 4
                    cols = c0 + sl.index // 4 * 512
                    if sl.loop is not None:
                        cols = sl.loop * 512 + cols
                    load(sl, w[q * 256:(q + 1) * 256, bass.ds(cols, 512)].rearrange("(c p) n -> p c n", p=P))

            for t, name in enumerate(("x_loaded", "x1_loaded")):
                sp.dma_start(x[:, t, :], d["x"][0, t * P:t * P + P, :]).then_inc(s[name], 16)
            sp.dma_start(m_rows, d["meta_tokens"]).then_inc(s["meta_loaded"], 16)
            sp.dma_start(const[:, 0:2 * P], d["constants"][:, 0:2 * P]).then_inc(s["const_loaded"], 16)
            for name, n in VEC_ROWS:
                src = d[name]
                flat = src.rearrange("a k (c p) -> (a k c) p", p=P) if len(src.shape) == 3 else \
                    src.rearrange("a (c p) -> (a c) p", p=P)
                sp.dma_start(vec_rows[VEC[name]:VEC[name] + n, :], flat).then_inc(s["vec_loaded"], 16)
            w_in = d["w_in"][0]

            def z_slots(lo, hi):
                for sl in over_slots(sp, lo, hi - lo, loops=0):
                    load(sl, k_half(w_in, sl.at % 2, Z_BLOCKS[sl.at // 2][1]))

            z_slots(0, RING)
            sp.dma_start(const[:, 2 * P:], d["constants"][:, 2 * P:]).then_inc(s["tables_loaded"], 16)
            sp.dma_start(w_uq[:], d["w_uq"][0].rearrange("(c p) n -> p c n", p=P)).then_inc(s["mla_loaded"], 16)
            sp.dma_start(w_ukv[:], d["w_ukv"][0]).then_inc(s["mla_loaded"], 16)
            sp.dma_start(w_gk[0:16, :], d["gla_w_gk_2"][0]).then_inc(s["gk_loaded"], 16)
            sp.dma_start(head_gain[:], d["gla_norm_g_2"][0].partition_broadcast(P)).then_inc(s["gk_loaded"], 16)
            sp.dma_start(gain[:], d["post_norm_g"][0].partition_broadcast(P)).then_inc(s["gain_loaded"], 16)
            sp.dma_start(pos_i, d["positions_2"][0].partition_broadcast(32)).then_inc(s["pos_loaded"], 16)
            z_slots(RING, 2 * RING)
            sp.wait_ge(s["cleared"], 2)
            for g in range(4):
                r = slice(g % 2 * 64, g % 2 * 64 + 64)
                sp.dma_start(w_pool[r, g // 2, r], d["pool_w"][0, g]).then_inc(s["pool_loaded"], 16)
            z_slots(2 * RING, COUNT["z"])
            def gates_half(b, h):
                by_columns("gate_%s%d" % (b, h), w_in, GATE_COL0 + BRANCH[b] * DM + h * 512)

            by_columns("gate_sc", w_in, GATE_COL0 + BRANCH["sc"] * DM)
            for before, b in (("sc", "pool"), ("pool", "conf"), ("conf", "mla")):
                for h in range(2):
                    load(Slot(FIRST["y_%s%d" % (before, h)], 0, None),
                         d["w_out_" + before][0][:, h * 512:(h + 1) * 512].rearrange("(c p) n -> p c n", p=P))
                    gates_half(b, h)
            for sl in over_slots(sp, FIRST["y_mla"], 4, loops=0):
                load(sl, k_half(d["w_out_mla"][0], 0, sl.index * 256))
            by_rows("w_o", d["w_o"][0])
            gla = d["gla_w_in_2"][0]
            for sl in over_slots(sp, FIRST["gla_gk"], 2):
                load(sl, k_half(gla, sl.index, 3072, 16), cols=16)
            by_columns("gla_q", gla, 0)
            by_columns("gla_k", gla, 512)
            by_rows("gla_v", gla, 1024)
            by_rows("gla_g", gla, 2048)
            by_rows("gla_out", d["gla_w_out_2"][0])
            for layer in range(2):
                gu = d["ffn_w_gu_2"][layer]
                for sl in over_slots(sp, FIRST["gu%d" % layer], COUNT["gu%d" % layer]):
                    load(sl, k_half(gu, sl.index % 2, sl.loop * 256 + (FFN if sl.index % 4 >= 2 else 0)))
                dn = d["ffn_w_down_2"][layer]
                for sl in over_slots(sp, FIRST["down%d" % layer], COUNT["down%d" % layer]):
                    row = sl.index * P if sl.loop is None else sl.loop * (RING * P) + sl.index * P
                    load(sl, dn[bass.ds(row, P), :])
                if layer == 0:
                    mw = d["moba_w_in_2"][0]
                    by_columns("moba_q", mw, 0)
                    by_columns("moba_k", mw, DM)
                    by_rows("moba_v", mw, 2 * DM)
                    by_rows("moba_out", d["moba_w_out_2"][0])
            sp.wait_ge(s["x_ready0"], 10)
            sp.dma_start(out[0, 0:P, :], x[:, 0, :]).then_inc(s["stored"], 16)
            for hf in range(2):
                sp.wait_ge(s["x_ready1"], 9 + hf)
                cols = slice(hf * 512, hf * 512 + 512)
                sp.dma_start(out[0, P:ROWS, cols], x[:, 1, cols]).then_inc(s["stored"], 16)
            sp.wait_ge(s["stored"], 48)

        @block.tensor
        def _(pe):
            def open_out(name_or_index):
                o = OUT[name_or_index]
                if o >= 2:
                    pe.wait_ge(evacuated[o % 2], o // 2)

            def ready(sl):
                pe.wait_ge(split, sl.number(1))

            def exact(dst, st_hi, st_lo, mv_hi, mv_lo, start, stop):
                pe.matmul(dst, st_hi, mv_hi, start=start, stop=False)
                pe.matmul(dst, st_hi, mv_lo, start=False, stop=False)
                return pe.matmul(dst, st_lo, mv_hi, start=False, stop=stop)

            def t_slot(sl, p, half, mv_hi, mv_lo, kcs=4, last=True, halves=2, first=True):
                ready(sl)
                n = mv_hi.shape[-1]
                hi = w_hi[:, sl.ring(), :].rearrange("p (c n) -> p c n", c=4)
                lo = w_lo[:, sl.ring(), :].rearrange("p (c n) -> p c n", c=4)
                for b in range(halves):
                    for c in range(kcs):
                        cols = slice(b * P, b * P + P)
                        mm = exact(acc[:, p, b, 0:n], hi[:, c, cols], lo[:, c, cols],
                                   mv_hi[:, half * 4 + c, :], mv_lo[:, half * 4 + c, :],
                                   start=first and c == 0, stop=last and c == kcs - 1)
                mm.then_inc(weights_used, 1)

            def t_stage(first, count, out0, mv_hi, mv_lo, halves=2, body=RING):
                for sl in over_slots(pe, first, count, body=body):
                    o = out0 + sl.index // 2
                    if sl.index % 2 == 0:
                        if sl.loop is not None:
                            pe.wait_ge(evacuated[o % 2], sl.loop * (body // 4) + o // 2)
                        elif o >= 2:
                            pe.wait_ge(evacuated[o % 2], o // 2)
                    t_slot(sl, o % 2, sl.index % 2, mv_hi, mv_lo, halves=halves,
                           first=sl.index % 2 == 0, last=sl.index % 2 == 1)

            def t_first(first, name, tag, count, halves=2):
                turn_rows(tag, count)
                open_out(name)
                keep_awake(acc[:, pair(name), 0, :], 2)
                for half in range(2):
                    half_ready(tag, half)
                    t_slot(Slot(first + half, half, None), pair(name), half, xt_hi, xt_lo, halves=halves,
                           first=half == 0, last=half == 1)

            def n_slots(stage, names, st_hi, st_lo, lo=0, hi=None):
                for i in range(lo, COUNT[stage] if hi is None else hi):
                    sl = Slot(FIRST[stage] + i, i, None)
                    q, name = i % 4, names[i // 4]
                    if q == 0:
                        open_out(name)
                    ready(sl)
                    for c in range(2):
                        cols = slice(c * 512, c * 512 + 512)
                        for t in range(TILES):
                            rows = slice(t * P, t * P + P)
                            k = q * 2 + c
                            mm = exact(acc[:, pair(name), t, :], st_hi[:, k, rows], st_lo[:, k, rows],
                                         w_hi[:, sl.ring(), cols], w_lo[:, sl.ring(), cols],
                                         start=k == 0, stop=k == KC - 1)
                    mm.then_inc(weights_used, 1)

            def n_product(stage, st_hi, st_lo, chunks_ready):
                names = [stage + "0", stage + "1"]
                for q in range(4):
                    chunks_ready(q)
                    n_slots(stage, names, st_hi, st_lo, q, q + 1)
                open_out(names[1])
                for t in range(TILES):
                    rows = slice(t * P, t * P + P)
                    for q in range(4):
                        sl = Slot(FIRST[stage] + 4 + q, 4 + q, None)
                        if t == 0:
                            ready(sl)
                        for c in range(2):
                            cols = slice(c * 512, c * 512 + 512)
                            k = q * 2 + c
                            mm = exact(acc[:, pair(names[1]), t, :], st_hi[:, k, rows], st_lo[:, k, rows],
                                       w_hi[:, sl.ring(), cols], w_lo[:, sl.ring(), cols], start=k == 0, stop=k == KC - 1)
                        if t == 1:
                            mm.then_inc(weights_used, 1)
                    if t == 0:
                        mm.then_inc(s["tile0_done"], 1)

            def open_bank(name):
                u = BANK[name]
                if u >= 4:
                    pe.wait_ge(bank_read[u % 4], u // 4)
                return misc[:, u % 4, :]

            def filled(ins, name):
                ins.then_inc(bank_full[BANK[name] % 4], 1)

            def keep_awake(b, n):
                for _ in range(n):
                    pe.matmul(b[:, 0:2 * P], ident, const[:, 0:2 * P], start=True, stop=True)

            def turn_rows(tag, count):
                for u in range(4):
                    t, j = u // 2, u % 2
                    b = open_bank("%s_%d" % (tag, u))
                    if j == 0:
                        keep_awake(b, (2, 6)[t])
                    pe.wait_ge(s["x_ready%d" % t], count + j + 1)
                    for c in range(4):
                        tr = pe.transpose(b[:, c * P:c * P + P], x[:, t, (4 * j + c) * P:(4 * j + c) * P + P], ident)
                    filled(tr, "%s_%d" % (tag, u))

            def half_ready(tag, half):
                await_read(pe, "%s_%d" % (tag, half))
                await_read(pe, "%s_%d" % (tag, 2 + half))

            xt_hi, xt_lo = x_hi[:, :, 0:ROWS], x_lo[:, :, 0:ROWS]
            xm_hi, xm_lo = x_hi[:, :, META:KEYS], x_lo[:, :, META:KEYS]

            pe.wait_ge(s["const_loaded"], 16)
            pe.wait_ge(s["vec_loaded"], 16 * len(VEC_ROWS))
            filled(pe.transpose(open_bank("vec")[:, 0:VEC_N], vec_rows[0:VEC_N, :], ident[0:VEC_N, 0:VEC_N]), "vec")
            keep_awake(open_bank("x0_0"), 5)
            pe.wait_ge(s["normed"], 3)
            for c in range(KC):
                b = open_bank("x0_%d" % c)
                cols = slice(c * P, c * P + P)
                pe.transpose(b[:, 0:META], meta_h[:, cols], ident[0:META, 0:META])
                for t in range(TILES):
                    tr = pe.transpose(b[:, META + t * P:META + t * P + P], y[:, t, cols], ident)
                filled(tr, "x0_%d" % c)
            def z(lo, hi, meta=True):
                t_stage(lo, hi - lo, lo // 2, x_hi if meta else xm_hi, x_lo if meta else xm_lo)

            for half in range(2):
                for c in range(4 * half, 4 * half + 4):
                    await_read(pe, "x0_%d" % c)
                t_slot(Slot(half, half, None), pair("z0"), half, x_hi, x_lo, first=half == 0, last=half == 1)
            z(2, 4, meta=False)
            z(4, 6)
            await_out(pe, "z0")
            filled(pe.matmul(open_bank("ssq_kv")[:, 0:KEYS], ones, sq_kv[:], start=True, stop=True), "ssq_kv")
            await_out(pe, "z1")
            b = open_bank("ssq_cq")
            pe.matmul(b[:, 0:ROWS], ones, sq_cq[:, 0, :], start=True, stop=False)
            filled(pe.matmul(b[:, 0:ROWS], ones, sq_cq[:, 1, :], start=False, stop=True), "ssq_cq")
            z(6, 14)
            z(14, 18, meta=False)
            pe.wait_ge(s["mla_loaded"], 32)
            pe.wait_ge(s["kv_normed"], 1)
            for j in range(4):
                b = open_bank("uq%d" % j)
                for i in range(2):
                    for c in range(2):
                        mm = pe.matmul(b[0:QK, i * ROWS:(i + 1) * ROWS], w_uq[:, c, (2 * j + i) * QK:(2 * j + i + 1) * QK],
                                       cq_z[:, c, :], start=c == 0, stop=c == 1)
                filled(mm, "uq%d" % j)
            wkv = w_ukv[:].rearrange("p (h e) -> p h e", h=HEADS)
            for i in range(HEADS):
                filled(pe.matmul(open_bank("kn%d" % i)[0:NOPE, 0:KEYS], wkv[:, i, 0:NOPE], kv_z[:], start=True, stop=True),
                       "kn%d" % i)
            for i, (lo, n) in enumerate([(0, META), (META, P), (META + P, P)]):
                filled(pe.matmul(open_bank("vt%d" % i)[0:n, :], kv_z[:, lo:lo + n], wkv[:, :, NOPE:NOPE + VD],
                                 start=True, stop=True), "vt%d" % i)
            z(18, 22, meta=False)
            pe.wait_ge(s["pool_loaded"], 64)
            pe.wait_ge(s["pooled_ready"], 1)
            b = open_bank("pool")
            for c in range(2):
                mm = pe.matmul(b[:, c * ROWS:(c + 1) * ROWS], w_pool[:, c, :], pooled[:, c, :], start=True, stop=True)
            filled(mm, "pool")
            z(22, 24, meta=False)
            pe.wait_ge(s["tables_loaded"], 16)
            rope = slice(NOPE, QK)
            filled(pe.matmul(open_bank("krs")[rope, 0:KEYS], cst("swap", ROPE, slice(0, ROPE)), kr_z[0:ROPE, :],
                             start=True, stop=True), "krs")
            filled(pe.matmul(open_bank("krc")[rope, 0:KEYS], ident[0:ROPE, 0:ROPE], kr_z[0:ROPE, :],
                             start=True, stop=True), "krc")
            def swap_queries(pairs):
                for j in pairs:
                    await_read(pe, "uq%d" % j)
                    filled(pe.matmul(open_bank("qs%d" % j)[rope, :], cst("swap", ROPE, rope), qT[rope, 2 * j:2 * j + 2, :],
                                     start=True, stop=True), "qs%d" % j)

            swap_queries(range(2))
            z(24, 26, meta=False)
            swap_queries(range(2, 4))

            def y_slot(b, i, u_hi, u_lo):
                sl = Slot(FIRST["y_%s%d" % (b, i)], 0, None)
                ready(sl)
                hi = w_hi[:, sl.ring(), :].rearrange("p (c n) -> p c n", c=2)
                lo = w_lo[:, sl.ring(), :].rearrange("p (c n) -> p c n", c=2)
                for q in range(4):
                    name = "y_%s%d" % (b, 2 * i + q // 2)
                    if q % 2 == 0:
                        open_out(name)
                    for c in range(2):
                        cols = slice(q * P, q * P + P)
                        mm = exact(acc[:, pair(name), q % 2, 0:ROWS], hi[:, c, cols], lo[:, c, cols],
                                   u_hi[:, c, :], u_lo[:, c, :], start=c == 0, stop=c == 1)
                    if q == 1:
                        mm.then_inc(s["y_first"], 1)
                mm.then_inc(weights_used, 1)

            t_stage(FIRST["gate_sc"], 8, OUT["gate_sc0"], xm_hi, xm_lo)
            pe.wait_ge(s["sc_split"], 1)
            for h in range(2):
                y_slot("sc", h, u_sc_hi, u_sc_lo)
                t_stage(FIRST["gate_pool%d" % h], 4, OUT["gate_pool%d" % (2 * h)], xm_hi, xm_lo)
                if h == 0:
                    pe.wait_ge(s["conv_done"], 1)
                    b = open_bank("conf_mean")
                    src = conv
                else:
                    pe.wait_ge(s["conf_squared"], 1)
                    b = open_bank("conf_var")
                    src = conf_sq
                pe.matmul(b[:, 0:ROWS], ones, src[:, 0, :], start=True, stop=False)
                filled(pe.matmul(b[:, 0:ROWS], ones, src[:, 1, :], start=False, stop=True), "conf_var" if h else "conf_mean")
            pe.wait_ge(s["pool_split"], 1)
            for h in range(2):
                y_slot("pool", h, u_pool_hi, u_pool_lo)
                t_stage(FIRST["gate_conf%d" % h], 4, OUT["gate_conf%d" % (2 * h)], xm_hi, xm_lo)
            pe.wait_ge(s["conf_split"], 1)

            pe.wait_ge(s["q_roped"], 4)
            pe.wait_ge(s["k_spread"], 1)

            def mla_scores(i):
                b = open_bank("s%d" % i)
                pe.matmul(b[:, 0:S0], qT[0:QK, i, 0:P], kT[0:QK, i, 0:S0], start=True, stop=True)
                filled(pe.matmul(b[:, S0:S0 + S1], qT[0:QK, i, P:ROWS], kT[0:QK, i, :], start=True, stop=True), "s%d" % i)

            def mla_turn(i):
                pe.wait_ge(s["probs_ready"], i + 1)
                pr = probs[:, i % 2, :]
                b = open_bank("pt%d" % i)
                pe.transpose(b[:, 0:P], pr[:, META:S0], ident)
                pe.transpose(b[:, P:2 * P], pr[:, S0 + META:S0 + S0], ident)
                filled(pe.transpose(b[:, 2 * P:3 * P], pr[:, S0 + S0:S0 + S1], ident), "pt%d" % i)
                b = open_bank("pm%d" % i)
                pe.transpose(b[0:META, 0:P], pr[:, 0:META], ident)
                filled(pe.transpose(b[0:META, P:2 * P], pr[:, S0:S0 + META], ident), "pm%d" % i)

            def mla_heads(i):
                name = "heads%d" % (i // 2)
                if i % 2 == 0:
                    open_out(name)
                await_read(pe, "pt%d" % i)
                await_read(pe, "pm%d" % i)
                dst = acc[i % 2 * VD:i % 2 * VD + VD, pair(name), 0, :]
                cols = slice(i * VD, i * VD + VD)
                pe.matmul(dst[:, 0:ROWS], vt[:, 0, cols], metaT[:, i % 2, :], start=True, stop=False)
                pe.matmul(dst[:, 0:ROWS], vt[:, 1, cols], probsT[:, i % 2, 0:ROWS], start=False, stop=False)
                pe.matmul(dst[:, P:ROWS], vt[:, 2, cols], probsT[:, i % 2, ROWS:ROWS + P], start=False,
                          stop=True).then_inc(s["heads_done"], 1)

            for n in range(HEADS + 2):
                if n % 5 == 0:
                    y_slot("conf", n // 5, u_conf_hi, u_conf_lo)
                else:
                    g = n - 1 - n // 5
                    name = "gate_mla%d" % (g // 2)
                    if g % 2 == 0:
                        open_out(name)
                    t_slot(Slot(FIRST["gate_mla%d" % (g // 4)] + g % 4, g % 4, None), pair(name), g % 2, xm_hi, xm_lo,
                           first=g % 2 == 0, last=g % 2 == 1)
                if n < HEADS:
                    mla_scores(n)
                if n >= 2:
                    mla_turn(n - 2)
                if n >= 3:
                    mla_heads(n - 3)
            mla_heads(HEADS - 1)
            for i in range(4):
                open_out("y_mla%d" % i)
                sl = Slot(FIRST["y_mla"] + i, i, None)
                ready(sl)
                hi = w_hi[:, sl.ring(), :].rearrange("p (c n) -> p c n", c=4)
                lo = w_lo[:, sl.ring(), :].rearrange("p (c n) -> p c n", c=4)
                for c in range(4):
                    if i == 0:
                        pe.wait_ge(s["u_mla_split"], c + 1)
                    for b in range(2):
                        cols = slice(b * P, b * P + P)
                        mm = exact(acc[:, pair("y_mla%d" % i), b, 0:ROWS], hi[:, c, cols], lo[:, c, cols],
                                   u_mla_hi[:, c, :], u_mla_lo[:, c, :], start=c == 0, stop=c == 3)
                mm.then_inc(weights_used, 1)
            n_product("w_o", m_hi, m_lo, lambda q: pe.wait_ge(s["m_split"], q + 1))

            t_first(FIRST["gla_gk"], "gla_gk", "x1", 0, halves=1)
            t_stage(FIRST["gla_q"], 4, OUT["gla_q0"], xt_hi, xt_lo)
            pe.wait_ge(s["gk_loaded"], 32)
            await_out(pe, "gla_gk")
            for j in range(2):
                b = open_bank("la%d" % j)
                for i in range(2):
                    c = 2 * j + i
                    mm = pe.matmul(b[:, i * ROWS:(i + 1) * ROWS], w_gk[0:16, c * DK:(c + 1) * DK], gk_low[0:16, :],
                                   start=True, stop=True)
                filled(mm, "la%d" % j)
            t_stage(FIRST["gla_k"], 4, OUT["gla_k0"], xt_hi, xt_lo)
            n_slots("gla_v", ["gla_v0", "gla_v1"], xt_hi, xt_lo)
            pe.wait_ge(s["qd_ready"], 1)
            pe.wait_ge(s["ki_ready"], 1)
            for j in range(2):
                b = open_bank("sg%d" % j)
                for i in range(4):
                    hd, t = 2 * j + i // 2, i % 2
                    rows = slice(t * P, t * P + P)
                    mm = pe.matmul(b[:, i * P:(i + 1) * P], ki[:, hd, rows], qd[:, hd, rows], start=True, stop=True)
                filled(mm, "sg%d" % j)
            pe.wait_ge(s["ke_ready"], 1)
            for j in range(2):
                b = open_bank("ke%d" % j)
                for i in range(4):
                    hd, t = 2 * j + i // 2, i % 2
                    tr = pe.transpose(b[:, i * P:(i + 1) * P], ke[:, hd, t * P:t * P + P], ident)
                filled(tr, "ke%d" % j)
            n_slots("gla_g", ["gla_g0", "gla_g1"], xt_hi, xt_lo, 0, 2)
            await_read(pe, "ke0")
            await_read(pe, "ke1")
            await_out(pe, "gla_v0")
            await_out(pe, "gla_v1")
            for hd in range(GLA_H):
                for half, chunks in (("a", (0, 1)), ("b", (2,))):
                    b = open_bank("upd%d%s" % (hd, half))
                    for n in chunks:
                        mm = pe.matmul(b[:, n % 2 * DV:n % 2 * DV + DV], ke_half[:, n % 2, hd * TILES + n // 2, :],
                                       gv[:, n // 2, hd * DV:(hd + 1) * DV], start=True, stop=True)
                    filled(mm, "upd%d%s" % (hd, half))
            n_slots("gla_g", ["gla_g0", "gla_g1"], xt_hi, xt_lo, 2, 4)
            pe.wait_ge(s["intra_ready"], 2)
            pe.wait_ge(s["half_ready"], 2)
            for hd in range(GLA_H - 2, GLA_H):
                await_read(pe, "upd%da" % hd)
                await_read(pe, "upd%db" % hd)
            for j in range(4):
                b = open_bank("o%d" % j)
                t = j // 2
                for i in range(2):
                    hd = j % 2 * 2 + i
                    dst = b[:, i * DV:(i + 1) * DV]
                    rows = slice(t * P, t * P + P)
                    pe.matmul(dst, intra[:, hd * TILES + t, :], gv[:, t, hd * DV:(hd + 1) * DV], start=True, stop=False)
                    if t == 1:
                        pe.matmul(dst, qd_half[:, 0, hd, rows], state[:, hd, 1, :], start=False, stop=False)
                    mm = pe.matmul(dst, qd_half[:, 1, hd, rows], state[:, hd, 2 * t, :], start=False, stop=True)
                filled(mm, "o%d" % j)
            n_slots("gla_g", ["gla_g0", "gla_g1"], xt_hi, xt_lo, 4, 7)

            def turn_gated(hf):
                for j in (2 * hf, 2 * hf + 1):
                    if hf == 0:
                        await_read(pe, "o0")
                        await_read(pe, "o2")
                    else:
                        pe.wait_ge(s["o_gated"], j - 1)
                    b = open_bank("ot%d" % j)
                    for c in range(2):
                        for t in range(TILES):
                            tr = pe.transpose(b[:, c * ROWS + t * P:c * ROWS + t * P + P],
                                              gg[:, t, (2 * j + c) * P:(2 * j + c) * P + P], ident)
                    filled(tr, "ot%d" % j)

            turn_gated(0)
            n_slots("gla_g", ["gla_g0", "gla_g1"], xt_hi, xt_lo, 7, 8)

            def gated_ready(q):
                if q == 1:
                    turn_gated(1)
                await_read(pe, "ot%d" % q)

            n_product("gla_out", o_hi, o_lo, gated_ready)

            def swiglu(layer):
                tag = "gu%d" % layer
                t_first(FIRST[tag], tag + "_0", "x2" if layer == 0 else "x4", 2 + 4 * layer)
                t_stage(FIRST[tag] + 2, COUNT[tag] - 2, OUT[tag + "_1"], xt_hi, xt_lo, body=2 * RING)
                tag = "down%d" % layer
                names = [tag + "_0", tag + "_1"]

                def down_half(k, t, hf):
                    sl = Slot(FIRST[tag] + k, k, None)
                    rows, cols = slice(t * P, t * P + P), slice(hf * 512, hf * 512 + 512)
                    return exact(acc[:, pair(names[hf]), t, :], h_hi[:, k, rows], h_lo[:, k, rows],
                                 w_hi[:, sl.ring(), cols], w_lo[:, sl.ring(), cols], start=k == 0, stop=k == FCH - 1)

                def down_ready(k):
                    if k % 2 == 0:
                        pe.wait_ge(s["h_split"], layer * FCH // 2 + k // 2 + 1)
                    ready(Slot(FIRST[tag] + k, k, None))

                for n in names:
                    open_out(n)
                for k in range(FCH - RING):
                    down_ready(k)
                    for t in range(TILES):
                        for hf in range(2):
                            mm = down_half(k, t, hf)
                    mm.then_inc(weights_used, 1)
                for t in range(TILES):
                    for hf in range(2):
                        for k in range(FCH - RING, FCH):
                            if t == 0 and hf == 0:
                                down_ready(k)
                            mm = down_half(k, t, hf)
                            if t == 1 and hf == 1:
                                mm.then_inc(weights_used, 1)
                        if t == 0 or hf == 0:
                            mm.then_inc(s["down_part"], 1)

            swiglu(0)

            t_first(FIRST["moba_q"], "moba_q0", "x3", 4)
            t_stage(FIRST["moba_q"] + 2, 6, OUT["moba_q1"], xt_hi, xt_lo)
            t_stage(FIRST["moba_k"], 8, OUT["moba_k0"], xt_hi, xt_lo)

            def moba_scores(i):
                b = open_bank("ms%d" % i)
                pe.matmul(b[:, 0:P], mq[:, i, 0:P], mk[:, i, 0:P], start=True, stop=True)
                filled(pe.matmul(b[:, P:P + ROWS], mq[:, i, P:ROWS], mk[:, i, :], start=True, stop=True), "ms%d" % i)

            def moba_turn(i):
                pe.wait_ge(s["m_probs"], i + 1)
                b = open_bank("mt%d" % i)
                for c in range(3):
                    tr = pe.transpose(b[:, c * P:(c + 1) * P], mprobs[:, i % 2, c * P:(c + 1) * P], ident)
                filled(tr, "mt%d" % i)

            pe.wait_ge(s["mq_roped"], 4)
            for i in range(HEADS + 2):
                if i < HEADS:
                    n_slots("moba_v", ["moba_v0", "moba_v1"], xt_hi, xt_lo, i, i + 1)
                    if i % 2 == 0:
                        pe.wait_ge(s["mk_roped"], i // 2 + 1)
                    moba_scores(i)
                if 2 <= i < HEADS + 1:
                    moba_turn(i - 2)
            await_out(pe, "moba_v0")
            await_out(pe, "moba_v1")
            for i in range(HEADS):
                if i == HEADS // 2:
                    moba_turn(HEADS - 1)
                name = "moba_heads%d" % (i // 2)
                if i % 2 == 0:
                    open_out(name)
                await_read(pe, "mt%d" % i)
                dst = acc[:, pair(name), i % 2, :]
                cols = slice(i * HD, (i + 1) * HD)
                pe.matmul(dst[:, 0:ROWS], mv[:, 0, cols], mprobsT[:, i, 0:ROWS], start=True, stop=False)
                pe.matmul(dst[:, P:ROWS], mv[:, 1, cols], mprobsT[:, i, ROWS:ROWS + P], start=False,
                          stop=True).then_inc(s["m_heads_done"], 1)
            n_product("moba_out", mo_hi, mo_lo, lambda q: await_out(pe, "moba_heads%d" % q))
            swiglu(1)

        @block.scalar
        def _(act):
            chained = [0]

            def link(ins):
                chained[0] += 1
                ins.then_inc(act_chain, 1)
                act.wait_ge(act_chain, chained[0])

            def round_slot(sl, ahead):
                k = sl.ring(ahead)
                act.wait_ge(landed[k], (sl.uses(ahead) + 1) * 16)
                if sl.loop is not None or sl.at + ahead >= RING:
                    act.wait_ge(weights_used, sl.number(ahead + 1 - RING))
                nc.scalar.copy(w_hi[:, k, :], staged[:, k, :]).then_inc(rounded, 1)

            def lead(sl):
                if sl.loop is not None or sl.at + LEAD < TOTAL:
                    round_slot(sl, LEAD)

            def copy_out(dst, src, name, func=ACT.Copy, **kw):
                nc.scalar.activation(dst, src, func, **kw).then_inc(evacuated[OUT[name] % 2], 1)

            def out_t(name, n=ROWS, lo=0):
                return acc[:, pair(name), :, lo:lo + n]

            def halves(dst, i):
                return dst[:, 2 * i:2 * i + 2, :]

            act.wait_ge(s["x_loaded"], 16)
            act.wait_ge(s["cleared"], 1)
            nc.scalar.activation(y[:, 0, :], x[:, 0, :], ACT.Square, accum_out=ssq[:, 0:1])
            act.wait_ge(s["meta_loaded"], 16)
            nc.scalar.activation(meta_h, m_rows, ACT.Square, accum_out=ssq[0:META, 1:2]).then_inc(s["ssq0"], 1)
            act.wait_ge(s["rstd0"], 1)
            nc.scalar.activation(y[:, 0, :], x[:, 0, :], ACT.Copy, scale=rs[:, 1, 0:1]).then_inc(s["normed"], 1)
            round_slot(Slot(0, 0, None), 0)
            await_read(act, "vec")
            for c in range(KC):
                if 1 <= c < LEAD:
                    round_slot(Slot(c, c, None), 0)
                await_full(act, "x0_%d" % c)
                nc.scalar.activation(x_hi[:, c, :], bank("x0_%d" % c)[:, 0:KEYS], ACT.Copy,
                                     scale=col("pre_norm_g", c)).then_inc(s["x0_rounded"], 1)

            for sl in over_slots(act, 0, COUNT["z"], loops=0):
                lead(sl)
                if sl.at % 2 == 0:
                    continue
                name = "z%d" % (sl.at // 2)
                what = Z_BLOCKS[sl.at // 2][0]
                slot_done(act, "z", sl.at)
                if what == "ckv_kr":
                    nc.scalar.copy(kv_z[:], acc[:, pair(name), 0, 0:KEYS])
                    nc.scalar.copy(kr_z[0:ROPE, :], acc[0:ROPE, pair(name), 1, 0:KEYS])
                    copy_out(sq_kv[:], acc[:, pair(name), 0, 0:KEYS], name, ACT.Square)
                elif what == "cq":
                    nc.scalar.copy(cq_z[:], out_t(name))
                    copy_out(sq_cq[:], out_t(name), name, ACT.Square)
                elif what in ("pool_v", "conf_a", "sc_c", "sc_x"):
                    dst = {"pool_v": pool_v, "conf_a": glu, "sc_c": sc_c, "sc_x": sc_x}[what]
                    copy_out(dst[:], out_t(name, KEYS), name)
                elif what == "conf_g":
                    copy_out(glu_g[:], out_t(name, KEYS), name, ACT.Sigmoid)
                elif what == "sc_b":
                    copy_out(sc_b[:], out_t(name), name)
                else:
                    dst = {"sc_gate": sc_gate[:], "pool_gate": pool_gate[:], "conf_gate": conf_gate[:],
                           "mla_gate0": halves(mla_gate, 0), "mla_gate1": halves(mla_gate, 1)}[what]
                    copy_out(dst, out_t(name), name, ACT.Silu)
                if what == "sc_gate":
                    act.wait_ge(s["trig_args"], 1)
                    act.wait_ge(s["cleared"], 3)
                    nc.scalar.activation(trig[0:ROPE, 0, :], trig_abs, ACT.Sin, bias=half_pi[0:ROPE, :], scale=-1.0)
                    nc.scalar.activation(trig[0:ROPE, 1, :], trig_r, ACT.Sin,
                                         scale=cst("sign", 1, slice(0, ROPE))).then_inc(s["trig_ready"], 1)
                    for j in range(4):
                        await_full(act, "uq%d" % j)
                        nc.scalar.copy(qT[0:QK, 2 * j:2 * j + 2, :], bank("uq%d" % j)[0:QK, :]
                                       .rearrange("p (h r) -> p h r", h=2)).then_inc(read_sem("uq%d" % j), 1)
                    for i in range(HEADS):
                        await_full(act, "kn%d" % i)
                        nc.scalar.copy(kT[0:NOPE, i, :], bank("kn%d" % i)[0:NOPE, 0:KEYS]).then_inc(read_sem("kn%d" % i), 1)
                    act.wait_ge(s["cleared"], 4)
                    for i, n in enumerate((META, P, P)):
                        await_full(act, "vt%d" % i)
                        nc.scalar.copy(vt[0:n, i, :], bank("vt%d" % i)[0:n, :]).then_inc(read_sem("vt%d" % i), 1)
                if sl.at == 23:
                    act.wait_ge(s["sc_u"], 1)
                    nc.scalar.copy(u_sc_hi[:], sc_acc[:]).then_inc(s["sc_rounded"], 1)
                if sl.at == 25:
                    await_read(act, "pool")
                    nc.scalar.copy(u_pool_hi[:], pool_gate[:]).then_inc(s["pool_rounded"], 1)

            def gate_bias(b, c):
                return col("gate_bias", BRANCH[b] * KC + c)

            def take_gates(b, before, i):
                name = "gate_%s%d" % (b, i)
                if before:
                    await_out(act, "y_%s%d" % (before, i))
                nc.scalar.activation(gates[:, 2 * i, :], acc[:, pair(name), 0, 0:ROWS], ACT.Sigmoid,
                                     bias=gate_bias(b, 2 * i))
                copy_out(gates[:, 2 * i + 1, :], acc[:, pair(name), 1, 0:ROWS], name, ACT.Sigmoid,
                         bias=gate_bias(b, 2 * i + 1))

            for sl in over_slots(act, FIRST["gate_sc"], 8, loops=0):
                lead(sl)
                if sl.index % 2 == 1:
                    slot_done(act, "gate_sc", sl.index)
                    take_gates("sc", None, sl.index // 2)
            for before, b in (("sc", "pool"), ("pool", "conf")):
                for h in range(2):
                    lead(Slot(FIRST["y_%s%d" % (before, h)], 0, None))
                    stage = "gate_%s%d" % (b, h)
                    for sl in over_slots(act, FIRST[stage], 4, loops=0):
                        lead(sl)
                        if sl.index % 2 == 1:
                            slot_done(act, stage, sl.index)
                            take_gates(b, before, 2 * h + sl.index // 2)
                        if stage == "gate_pool1" and sl.index == 1:
                            await_read(act, "conf_mean")
                            nc.scalar.square(conf_sq[:], conv[:]).then_inc(s["conf_squared"], 1)
                        if stage == "gate_conf0" and sl.index == 2:
                            act.wait_ge(s["conf_zn"], 1)
                            nc.scalar.activation(conf_sq[:, 0, :], conv[:, 0, :], ACT.Sigmoid, bias=col("conf_ln_b", 0))
                            nc.scalar.activation(conf_sq[:, 1, :], conv[:, 1, :], ACT.Sigmoid,
                                                 bias=col("conf_ln_b", 1)).then_inc(s["conf_sig"], 1)
                        if stage == "gate_conf1" and sl.index == 0:
                            act.wait_ge(s["conf_u"], 1)
                            nc.scalar.copy(u_conf_hi[:], conv[:]).then_inc(s["conf_rounded"], 1)

            def mla_probsT(i):
                await_full(act, "pt%d" % i)
                nc.scalar.copy(probsT[:, i % 2, :], bank("pt%d" % i)[:, 0:3 * P]).then_inc(read_sem("pt%d" % i), 1)
                await_full(act, "pm%d" % i)
                nc.scalar.copy(metaT[0:META, i % 2, :], bank("pm%d" % i)[0:META, 0:ROWS]).then_inc(read_sem("pm%d" % i), 1)

            def mla_u_hi(i):
                await_out(act, "heads%d" % i)
                nc.scalar.copy(u_mla_hi[:, i, :], u_mla[:, i, :]).then_inc(s["u_mla_rounded"], 1)

            act.wait_ge(s["meta_cleared"], 1)
            for n in range(HEADS + 2):
                g = n - 1 - n // 5
                lead(Slot(FIRST["y_conf0"] + n, n, None))
                if n == HEADS:
                    for b in (1, 2):
                        await_out(act, "gate_mla%d" % b)
                    for b in range(3):
                        nc.scalar.activation(halves(gates, b), halves(gates, b), ACT.Sigmoid).then_inc(s["mla_gates"], 1)
                if n % 5 and g % 2 == 1:
                    b, name = g // 2, "gate_mla%d" % (g // 2)
                    slot_done(act, "gate_mla%d" % (g // 4), g % 4)
                    await_out(act, "y_conf%d" % b)
                    func = ACT.Identity if b < 3 else ACT.Sigmoid
                    nc.scalar.activation(gates[:, 2 * b, :], acc[:, pair(name), 0, 0:ROWS], func, bias=gate_bias("mla", 2 * b))
                    copy_out(gates[:, 2 * b + 1, :], acc[:, pair(name), 1, 0:ROWS], name, func,
                             bias=gate_bias("mla", 2 * b + 1))
                if n >= 2:
                    mla_probsT(n - 2)
                if n < HEADS:
                    act.wait_ge(s["max_ready"], n + 1)
                    nc.scalar.activation(probs[:, n % 2, 0:S0], scores[:, n % 2, 0:S0], ACT.Exp, bias=neg_max[:, n % 2, 0:1],
                                         accum_out=sums[:, n % 2, 0:1])
                    nc.scalar.activation(probs[:, n % 2, S0:], scores[:, n % 2, S0:], ACT.Exp, bias=neg_max[:, n % 2, 1:2],
                                         accum_out=sums[:, n % 2, 1:2]).then_inc(s["exp_done"], 1)
                if n in (6, 8):
                    mla_u_hi((n - 6) // 2)
            mla_u_hi(2)
            mla_u_hi(3)
            for i in range(4):
                lead(Slot(FIRST["y_mla"] + i, i, None))
                act.wait_ge(s["m_ready"], i + 1)
                nc.scalar.copy(halves(m_hi, i), halves(m, i)).then_inc(s["m_rounded"], 1)
            junk = m[:].rearrange("p c r -> p (c r)")
            def squares(t, hf):
                k = 2 * t + hf
                return nc.scalar.activation(junk[:, k * 512:(k + 1) * 512], acc[:, pair("w_o%d" % hf), t, :], ACT.Square,
                                            accum_out=ssq[:, k:k + 1])

            for sl in over_slots(act, FIRST["w_o"], 8, loops=0):
                lead(sl)
                if sl.index == 3:
                    slot_done(act, "w_o", 3)
                    act.wait_ge(s["m_split"], 4)
                    squares(0, 0)
                    squares(1, 0)
                if sl.index == 4:
                    act.wait_ge(s["tile0_done"], TAILS["w_o"])
                    squares(0, 1).then_inc(s["wo_ssq"], 1)
            slot_done(act, "w_o", 7)
            squares(1, 1).then_inc(s["wo_ssq"], 1)

            def scale_tile0(k):
                act.wait_ge(s["rstd_tile0"], k + 1)
                for hf in range(2):
                    cols = slice(hf * 512, hf * 512 + 512)
                    nc.scalar.activation(y[:, 0, cols], y[:, 0, cols], ACT.Copy, scale=rs[:, 1, 0:1]).then_inc(s["scaled0"], 1)

            def round_rows(tag):
                for u in range(4):
                    t, j = u // 2, u % 2
                    await_full(act, "%s_%d" % (tag, u))
                    nc.scalar.copy(x_hi[:, 4 * j:4 * j + 4, t * P:t * P + P], bank("%s_%d" % (tag, u))
                                   .rearrange("p (c r) -> p c r", c=4)).then_inc(s["x_rounded"], 1)

            round_rows("x1")
            for sl in over_slots(act, FIRST["gla_gk"], 2):
                lead(sl)
            slot_done(act, "gla_gk", 1)
            copy_out(gk_low[0:16, :], acc[0:16, pair("gla_gk"), 0, 0:ROWS], "gla_gk")
            for sl in over_slots(act, FIRST["gla_q"], 4, loops=0):
                lead(sl)
                if sl.index % 2 == 1:
                    slot_done(act, "gla_q", sl.index)
                    name = "gla_q%d" % (sl.index // 2)
                    copy_out(halves(gq, sl.index // 2), out_t(name), name, scale=float(DK) ** -0.5)
            for sl in over_slots(act, FIRST["gla_k"], 4, loops=0):
                lead(sl)
                if sl.index == 0:
                    for j in range(2):
                        await_full(act, "la%d" % j)
                        for i in range(2):
                            c = 2 * j + i
                            ab = nc.scalar.activation(la_e[:, c, :], bank("la%d" % j)[:, i * ROWS:(i + 1) * ROWS], ACT.Abs,
                                                      bias=col("gla_b_gk_2", c))
                        ab.then_inc(s["la_abs"], 1)
                    act.wait_ge(s["la_abs"], 2)
                    link(nc.scalar.activation(la_e[:], la_e[:], ACT.Exp, scale=-1.0))
                    nc.scalar.activation(la_e[:], la_e[:], ACT.Ln, bias=1.0).then_inc(s["la_log"], 1)
                if sl.index % 2 == 1:
                    slot_done(act, "gla_k", sl.index)
                    name = "gla_k%d" % (sl.index // 2)
                    copy_out(halves(gk, sl.index // 2), out_t(name), name)
                if sl.index == 2:
                    act.wait_ge(s["cum_ready"], 1)
                    nc.scalar.activation(e_cum[:], la_e[:], ACT.Exp, scale=1.0 / 16.0).then_inc(s["e_ready"], 1)
                    nc.scalar.activation(e_inv[:], la_e[:], ACT.Exp, scale=-1.0 / 16.0).then_inc(s["e_ready"], 1)
                    act.wait_ge(s["end_ready"], 1)
                    nc.scalar.activation(e_end[:], la[:], ACT.Exp, scale=1.0 / 16.0).then_inc(s["e_ready"], 1)
            for sl in over_slots(act, FIRST["gla_v"], 8, loops=0):
                lead(sl)
                if sl.index % 4 == 3:
                    hf = sl.index // 4
                    slot_done(act, "gla_v", sl.index)
                    copy_out(gv[:, :, hf * 512:(hf + 1) * 512], acc[:, pair("gla_v%d" % hf), :, :], "gla_v%d" % hf)
            def round_gated(hf):
                for j in (2 * hf, 2 * hf + 1):
                    await_full(act, "ot%d" % j)
                    nc.scalar.copy(halves(o_hi, j), bank("ot%d" % j).rearrange("p (c r) -> p c r", c=2)).then_inc(s["o_rounded"], 1)

            for sl in over_slots(act, FIRST["gla_g"], 8, loops=0):
                lead(sl)
                if sl.index == 0:
                    act.wait_ge(s["zeroed"], 4)
                    for j in range(2):
                        await_full(act, "sg%d" % j)
                        b = bank("sg%d" % j).rearrange("p (g r) -> p g r", g=4)
                        nc.scalar.copy(intra[0:CH, 4 * j:4 * j + 4, 0:CH], b[0:CH, :, 0:CH])
                        nc.scalar.copy(intra[CH:P, 4 * j:4 * j + 4, CH:P], b[CH:P, :, CH:P]).then_inc(read_sem("sg%d" % j), 1)
                    for j in range(2):
                        await_full(act, "ke%d" % j)
                        b = bank("ke%d" % j).rearrange("p (g r) -> p g r", g=4)
                        nc.scalar.copy(ke_half[0:CH, 0, 4 * j:4 * j + 4, :], b[0:CH])
                        nc.scalar.copy(ke_half[CH:P, 1, 4 * j:4 * j + 4, :], b[CH:P]).then_inc(read_sem("ke%d" % j), 1)
                if sl.index == 4:
                    junk1 = e_inv[:].rearrange("p h r -> p (h r)")
                    junk2 = e_end[:].rearrange("p h r -> p (h r)")
                    for j in range(4):
                        await_full(act, "o%d" % j)
                        for i in range(2):
                            k = 2 * j + i
                            dst = (junk1 if k < 4 else junk2)[:, k % 4 * DV:(k % 4 + 1) * DV]
                            nc.scalar.activation(dst, bank("o%d" % j)[:, i * DV:(i + 1) * DV], ACT.Square,
                                                 accum_out=ssq[:, k:k + 1]).then_inc(s["o_ssq"], 1)
                if sl.index == 7:
                    round_gated(0)
                if sl.index % 4 == 3:
                    hf = sl.index // 4
                    slot_done(act, "gla_g", sl.index)
                    if hf == 0:
                        copy_out(gg[:, :, 0:512], acc[:, pair("gla_g0"), :, :], "gla_g0", ACT.Silu)
                    else:
                        nc.scalar.activation(gg[:, :, 512:768], acc[:, pair("gla_g1"), :, 0:256], ACT.Silu).then_inc(s["gg1_ready"], 1)
                        copy_out(gg[:, :, 768:1024], acc[:, pair("gla_g1"), :, 256:512], "gla_g1", ACT.Silu)
            for sl in over_slots(act, FIRST["gla_out"], 8, loops=0):
                lead(sl)
                if sl.index == 1:
                    round_gated(1)

            def swiglu(layer):
                tag = "gu%d" % layer
                for sl in over_slots(act, FIRST[tag], COUNT[tag]):
                    lead(sl)
                    og = OUT[tag + "_0"]
                    if sl.index == 1:
                        act.wait_ge(weights_used, sl.number(1))
                        nc.scalar.activation(h_gate[:], acc[:, og % 2, :, 0:ROWS], ACT.Silu).then_inc(evacuated[og % 2], 1)
                    if sl.index == 3:
                        act.wait_ge(evacuated[(og + 1) % 2], sl.loop + ((og + 1) // 2 + 1))
                        nc.scalar.copy(h_hi[:, bass.ds(sl.loop * 2, 2), :], hidden[:]).then_inc(s["h_rounded"], 1)
                tag = "down%d" % layer
                for sl in over_slots(act, FIRST[tag], COUNT[tag], loops=4):
                    lead(sl)

            scale_tile0(0)
            round_rows("x2")
            swiglu(0)
            scale_tile0(1)
            round_rows("x3")
            for tag, dst in (("moba_q", mq), ("moba_k", mk)):
                for sl in over_slots(act, FIRST[tag], 8, loops=0):
                    lead(sl)
                    if sl.index % 2 == 1:
                        slot_done(act, tag, sl.index)
                        name = "%s%d" % (tag, sl.index // 2)
                        copy_out(halves(dst, sl.index // 2), out_t(name), name)

            def moba_probsT(i):
                await_full(act, "mt%d" % i)
                nc.scalar.copy(mprobsT[:, i, :], bank("mt%d" % i)[:, 0:P + ROWS]).then_inc(read_sem("mt%d" % i), 1)

            for i in range(HEADS + 2):
                if i < HEADS:
                    lead(Slot(FIRST["moba_v"] + i, i, None))
                if i >= 2:
                    moba_probsT(i - 2)
                if i < HEADS:
                    act.wait_ge(s["m_max"], i + 1)
                    nc.scalar.activation(mprobs[:, i % 2, 0:P], mscores[:, i % 2, 0:P], ACT.Exp, bias=neg_max[:, i % 2, 0:1],
                                         accum_out=sums[:, i % 2, 0:1])
                    nc.scalar.activation(mprobs[:, i % 2, P:], mscores[:, i % 2, P:], ACT.Exp, bias=neg_max[:, i % 2, 1:2],
                                         accum_out=sums[:, i % 2, 1:2]).then_inc(s["m_exp"], 1)
                    if i % 4 == 3:
                        hf = i // 4
                        slot_done(act, "moba_v", i)
                        copy_out(mv[:, :, hf * 512:(hf + 1) * 512], acc[:, pair("moba_v%d" % hf), :, :], "moba_v%d" % hf)
            for i in range(4):
                act.wait_ge(s["m_heads_done"], 2 * i + 2)
                nc.scalar.copy(halves(mo_hi, i), out_t("moba_heads%d" % i)).then_inc(s["mo_rounded"], 1)
            for sl in over_slots(act, FIRST["moba_out"], 8):
                lead(sl)
            scale_tile0(2)
            round_rows("x4")
            swiglu(1)
            scale_tile0(3)

        @block.vector
        def _(dve):
            chained = [0]

            def count(ins):
                chained[0] += 1
                ins.then_inc(dve_chain, 1)
                return chained[0]

            def link(ins):
                dve.wait_ge(dve_chain, count(ins))

            def split_slot(sl, ahead):
                k = sl.ring(ahead)
                dve.wait_ge(rounded, sl.number(ahead + 1))
                nc.vector.tensor_tensor(w_lo[:, k, :], staged[:, k, :], w_hi[:, k, :].bitcast(F32),
                                        ALU.subtract).then_inc(split, 1)

            def lead(sl):
                if sl.loop is not None or sl.at + LEAD < TOTAL:
                    split_slot(sl, LEAD)

            def rest(dst, src, hi):
                return nc.vector.tensor_tensor(dst, src, hi.bitcast(F32), ALU.subtract)

            def newton(v, r, t):
                link(nc.vector.tensor_scalar(r.bitcast(I32), v.bitcast(I32), 1, None, ALU.logical_shift_right))
                link(nc.vector.tensor_scalar(r.bitcast(I32), r.bitcast(I32), -1.0, float(0x5F3759DF), ALU.mult, ALU.add))
                for step in range(3):
                    link(nc.vector.tensor_tensor(t, r, r, ALU.mult))
                    link(nc.vector.scalar_tensor_tensor(t, t, -0.5, v, ALU.mult, ALU.mult))
                    last = nc.vector.scalar_tensor_tensor(r, t, 1.5, r, ALU.add, ALU.mult)
                    if step < 2:
                        link(last)
                return last

            def newton_col(v, r, t, beside=lambda step: None, done=None):
                n = count(nc.vector.tensor_scalar(r.bitcast(I32), v.bitcast(I32), 1, None, ALU.logical_shift_right))
                beside(0)
                dve.wait_ge(dve_chain, n)
                n = count(nc.vector.tensor_scalar(r.bitcast(I32), r.bitcast(I32), -1.0, float(0x5F3759DF), ALU.mult, ALU.add))
                beside(1)
                dve.wait_ge(dve_chain, n)
                for step, three in enumerate((3.0, 12.0, 768.0)):
                    n = count(nc.vector.scalar_tensor_tensor(t, r, v, r, ALU.mult, ALU.mult))
                    if step == 0:
                        beside(2)
                    dve.wait_ge(dve_chain, n)
                    n = count(nc.vector.scalar_tensor_tensor(r, t, -three, r, ALU.add, ALU.mult))
                    if step == 0:
                        beside(3)
                    dve.wait_ge(dve_chain, n)
                ins = nc.vector.tensor_scalar(r, r, -1.0 / 8192, None, ALU.mult)
                if done is None:
                    link(ins)
                else:
                    ins.then_inc(done, 1)

            def handed_back(stage):
                dve.wait_ge(split, FIRST[stage] + LEAD)

            def mean_eps(dst, src, n, eps):
                return nc.vector.tensor_scalar(dst, src, 1.0 / n, eps, ALU.mult, ALU.add)

            def halves(dst, i):
                return dst[:, 2 * i:2 * i + 2, :]

            def out_t(name):
                return acc[:, pair(name), :, 0:ROWS]

            def taken(ins, name):
                ins.then_inc(evacuated[pair(name)], 1)

            def read(ins, name):
                ins.then_inc(read_sem(name), 1)

            dve.wait_ge(s["x1_loaded"], 16)
            for hf in range(2):
                last = nc.vector.bn_stats(stats[:, 1, hf, :], x[:, 1, hf * 512:hf * 512 + 512])
            link(last)
            link(nc.vector.bn_aggr(mu_var[:, 1, :], stats[:, 1].rearrange("p h e -> p (h e)")))
            link(nc.vector.scalar_tensor_tensor(rs[:, 0, 2:3], mu_var[:, 1, 0:1], mu_var[:, 1, 0:1], mu_var[:, 1, 1:2],
                                                ALU.mult, ALU.add))
            nc.vector.tensor_scalar(rs[:, 0, 2:3], rs[:, 0, 2:3], EPS, None, ALU.add)
            dve.wait_ge(s["ssq0"], 1)
            link(mean_eps(rs[:, 0, 0:2], ssq[:, 0:2], DM, EPS))
            newton(rs[:, 0, 0:3], rs[:, 1, 0:3], rs[:, 2, 0:3]).then_inc(s["rstd0"], 1)
            dve.wait_ge(s["rstd0"], 1)
            nc.vector.tensor_scalar(y[:, 1, :], x[:, 1, :], rs[:, 1, 2:3], None, ALU.mult).then_inc(s["normed"], 1)
            nc.vector.tensor_scalar(meta_h, m_rows, rs[0:META, 1, 1:2], None, ALU.mult).then_inc(s["normed"], 1)
            await_full(dve, "vec")
            read(nc.vector.tensor_copy(vec[:, 0:VEC_N], bank("vec")[:, 0:VEC_N]), "vec")
            await_read(dve, "vec")
            for c in range(KC):
                if c < LEAD:
                    split_slot(Slot(c, c, None), 0)
                dve.wait_ge(s["x0_rounded"], c + 1)
                read(nc.vector.scalar_tensor_tensor(x_lo[:, c, :], bank("x0_%d" % c)[:, 0:KEYS], col("pre_norm_g", c),
                                                    x_hi[:, c, :].bitcast(F32), ALU.mult, ALU.subtract), "x0_%d" % c)

            def trig_reduce():
                dve.wait_ge(s["pos_loaded"], 16)
                dve.wait_ge(s["tables_loaded"], 16)
                link(nc.vector.tensor_scalar(trig_r, pos_i, cst("inv_freq", 1, slice(0, ROPE)), None, ALU.mult))
                magic = 1.5 * 2.0 ** 23
                link(nc.vector.tensor_scalar(trig_k, trig_r, float(1 / (2 * np.pi)), magic, ALU.mult, ALU.add))
                link(nc.vector.tensor_scalar(trig_k, trig_k, -magic, None, ALU.add))
                link(nc.vector.tensor_scalar(trig_kh, trig_k, 1.0 / 2048, magic, ALU.mult, ALU.add))
                link(nc.vector.tensor_scalar(trig_kh, trig_kh, -magic, 2048.0, ALU.add, ALU.mult))
                link(nc.vector.tensor_tensor(trig_k, trig_k, trig_kh, ALU.subtract))
                rest_2pi, parts = 2 * np.pi, []
                for bits in (11, 11, 11):
                    e = np.floor(np.log2(rest_2pi))
                    unit = 2.0 ** (e - bits + 1)
                    parts.append(np.floor(rest_2pi / unit) * unit)
                    rest_2pi -= parts[-1]
                for part in parts + [rest_2pi]:
                    for k in (trig_kh, trig_k):
                        link(nc.vector.scalar_tensor_tensor(trig_r, k, -float(part), trig_r, ALU.mult, ALU.add))
                link(nc.vector.tensor_scalar(trig_r, trig_r, 3.1415925, -3.1415925, ALU.min, ALU.max))
                nc.vector.scalar_tensor_tensor(trig_abs, trig_r, -1.0, trig_r, ALU.mult, ALU.max).then_inc(s["trig_args"], 1)

            def kvq_norm():
                v, r, t = kvq_rs
                await_full(dve, "ssq_kv")
                read(mean_eps(v[:, 0:KEYS], bank("ssq_kv")[:, 0:KEYS], P, EPS), "ssq_kv")
                await_full(dve, "ssq_cq")
                read(mean_eps(v[:, KEYS:], bank("ssq_cq")[:, 0:ROWS], 2 * P, EPS), "ssq_cq")
                await_read(dve, "ssq_kv")
                await_read(dve, "ssq_cq")
                link(newton(v, r, t))
                nc.vector.scalar_tensor_tensor(kv_z[:], kv_z[:], col("kv_norm_g"), r[:, 0:KEYS], ALU.mult, ALU.mult)
                for c in range(2):
                    last = nc.vector.scalar_tensor_tensor(cq_z[:, c, :], cq_z[:, c, :], col("q_norm_g", c), r[:, KEYS:],
                                                          ALU.mult, ALU.mult)
                last.then_inc(s["kv_normed"], 1)

            conv_last = [0, 0]

            def conv_taps(lo, hi):
                for j in range(lo, hi):
                    k = CONF_K - 1 - j
                    for c in range(2):
                        w = col("conf_dw_w", 2 * k + c)
                        if j == 0:
                            ins = nc.vector.tensor_scalar(conv[:, c, :], glu[:, c, META:KEYS], w, col("conf_dw_b", c),
                                                          ALU.mult, ALU.add)
                        else:
                            r0 = max(0, j - META)
                            dve.wait_ge(dve_chain, conv_last[c])
                            ins = nc.vector.scalar_tensor_tensor(conv[:, c, r0:], glu[:, c, META + r0 - j:KEYS - j], w,
                                                                 conv[:, c, r0:], ALU.mult, ALU.add)
                        if j == CONF_K - 1 and c == 1:
                            dve.wait_ge(dve_chain, conv_last[0])
                            ins.then_inc(s["conv_done"], 1)
                        else:
                            conv_last[c] = count(ins)

            def short_conv():
                dve.wait_ge(s["sc_ready"], 1)
                last = [0, 0]
                for k in range(SC_K):
                    for c in range(2):
                        w = col("sc_dw_w", 2 * k + c)
                        src = sc_x[:, c, META - SC_K + 1 + k:KEYS - SC_K + 1 + k]
                        if k == 0:
                            last[c] = count(nc.vector.tensor_scalar(sc_acc[:, c, :], src, w, None, ALU.mult))
                        else:
                            dve.wait_ge(dve_chain, last[c])
                            last[c] = count(nc.vector.scalar_tensor_tensor(sc_acc[:, c, :], src, w, sc_acc[:, c, :],
                                                                           ALU.mult, ALU.add))
                await_out(dve, "z7")
                dve.wait_ge(dve_chain, last[1])
                link(nc.vector.tensor_tensor(sc_acc[:], sc_acc[:], sc_b[:], ALU.mult))
                await_out(dve, "z8")
                nc.vector.tensor_tensor(sc_acc[:], sc_acc[:], sc_gate[:], ALU.mult).then_inc(s["sc_u"], 1)

            rope = slice(NOPE, QK)

            def two_heads(a):
                return a.unsqueeze(1).to_broadcast([ROPE, 2, ROWS])

            def rotate_keys():
                await_full(dve, "krs")
                read(nc.vector.tensor_tensor(rope_t[rope, 0:KEYS], bank("krs")[rope, 0:KEYS], cst("sin", KEYS, rope), ALU.mult),
                     "krs")
                await_full(dve, "krc")
                read(nc.vector.tensor_tensor(kr_t[rope, :], bank("krc")[rope, 0:KEYS], cst("cos", KEYS, rope), ALU.mult), "krc")
                await_read(dve, "krs")
                await_read(dve, "krc")
                nc.vector.tensor_tensor(kr_t[rope, :], kr_t[rope, :], rope_t[rope, 0:KEYS], ALU.add).then_inc(s["kr_roped"], 1)

            def rotate(t, q, name, sin, cos):
                await_full(dve, name)
                read(nc.vector.tensor_tensor(t, bank(name)[q.start_partition():q.start_partition() + ROPE, :]
                                             .rearrange("p (h r) -> p h r", h=2), two_heads(sin), ALU.mult), name)
                link(nc.vector.tensor_tensor(q, q, two_heads(cos), ALU.mult))
                await_read(dve, name)
                return nc.vector.tensor_tensor(q, q, t, ALU.add)

            def rotate_queries(pairs):
                dve.wait_ge(s["kr_roped"], 1)
                for j in pairs:
                    t = rope_t[rope, :].rearrange("p (h r) -> p h r", h=2)
                    rotate(t, qT[rope, 2 * j:2 * j + 2, :], "qs%d" % j, cst("sin", KEYS, rope)[:, META:],
                           cst("cos", KEYS, rope)[:, META:]).then_inc(s["q_roped"], 1)
                    dve.wait_ge(s["q_roped"], j + 1)

            for sl in over_slots(dve, 0, COUNT["z"], loops=0):
                lead(sl)
                if sl.at == 1:
                    trig_reduce()
                if sl.at == 6:
                    kvq_norm()
                if sl.at == 10:
                    dve.wait_ge(s["glu_ready"], 1)
                conv_taps(*Z_TAPS.get(sl.at, (0, 0)))
                if sl.at == 19:
                    short_conv()
                if sl.at == 22:
                    await_full(dve, "pool")
                    await_out(dve, "z9")
                    for c in range(2):
                        last = nc.vector.scalar_tensor_tensor(pool_gate[:, c, :], bank("pool")[:, c * ROWS:(c + 1) * ROWS],
                                                              col("pool_scale", c), pool_gate[:, c, :], ALU.mult, ALU.mult)
                    read(last, "pool")
                if sl.at == 24:
                    dve.wait_ge(s["sc_rounded"], 1)
                    rest(u_sc_lo[:], sc_acc[:], u_sc_hi[:]).then_inc(s["sc_split"], 1)
                    rotate_keys()
                    rotate_queries(range(2))

            gated = [0]

            def gate_out(b, i):
                name = "y_%s%d" % (b, i)
                if b == "sc":
                    taken(nc.vector.tensor_tensor(halves(m, i), out_t(name), halves(gates, i), ALU.mult), name)
                    return
                if b == "mla" and i >= 2:
                    dve.wait_ge(s["m_ready"], i - 1)
                elif b != "mla" and gated[0] >= 2:
                    dve.wait_ge(s["m_added"], gated[0] - 1)
                taken(nc.vector.tensor_tensor(y_gated[:, gated[0] % 2], out_t(name), halves(gates, i), ALU.mult), name)
                gated[0] += 1

            def conf_centre():
                await_full(dve, "conf_mean")
                for c in range(2):
                    last = nc.vector.scalar_tensor_tensor(conv[:, c, :], bank("conf_mean")[:, 0:ROWS], -1.0 / (2 * P),
                                                          conv[:, c, :], ALU.mult, ALU.add)
                read(last, "conf_mean")

            def conf_norm():
                v, r, t = [a[:, 0:ROWS] for a in kvq_rs]
                await_full(dve, "conf_var")
                read(mean_eps(v, bank("conf_var")[:, 0:ROWS], 2 * P, EPS), "conf_var")
                await_read(dve, "conf_var")
                link(newton(v, r, t))
                for c in range(2):
                    last = nc.vector.scalar_tensor_tensor(conv[:, c, :], conv[:, c, :], col("conf_ln_g", c), r, ALU.mult, ALU.mult)
                last.then_inc(s["conf_zn"], 1)

            def conf_operand():
                dve.wait_ge(s["conf_sig"], 1)
                for c in range(2):
                    last = nc.vector.scalar_tensor_tensor(conv[:, c, :], conv[:, c, :], col("conf_ln_b", c), conf_sq[:, c, :],
                                                          ALU.add, ALU.mult)
                link(last)
                nc.vector.tensor_tensor(conv[:], conv[:], conf_gate[:], ALU.mult).then_inc(s["conf_u"], 1)

            halves_taken = [0]

            def take_out(b, h):
                halves_taken[0] += 1
                dve.wait_ge(s["y_first"], halves_taken[0])
                gate_out(b, 2 * h)
                slot_done(dve, "y_%s%d" % (b, h), 0)
                gate_out(b, 2 * h + 1)

            for sl in over_slots(dve, FIRST["gate_sc"], 8, loops=0):
                lead(sl)
                if sl.index == 0:
                    dve.wait_ge(s["pool_rounded"], 1)
                    rest(u_pool_lo[:], pool_gate[:], u_pool_hi[:]).then_inc(s["pool_split"], 1)
                    rotate_queries(range(2, 4))
                elif sl.index <= 5:
                    conv_taps(19 + 2 * sl.index, 21 + 2 * sl.index)
            for before, b in (("sc", "pool"), ("pool", "conf")):
                for h in range(2):
                    take_out(before, h)
                    lead(Slot(FIRST["y_%s%d" % (before, h)], 0, None))
                    stage = "gate_%s%d" % (b, h)
                    for sl in over_slots(dve, FIRST[stage], 4, loops=0):
                        lead(sl)
                        if stage == "gate_pool1" and sl.index == 0:
                            conf_centre()
                        if stage == "gate_conf0" and sl.index == 0:
                            conf_norm()
                        if stage == "gate_conf0" and sl.index == 3:
                            conf_operand()
                        if stage == "gate_conf1" and sl.index == 1:
                            dve.wait_ge(s["conf_rounded"], 1)
                            rest(u_conf_lo[:], conv[:], u_conf_hi[:]).then_inc(s["conf_split"], 1)

            def masked_max(i, name, n0, sc, scale, mask, done):
                n = sc.shape[-1]
                await_full(dve, name)
                read(nc.vector.scalar_tensor_tensor(sc, bank(name)[:, 0:n], scale, cst(mask, n), ALU.mult, ALU.add), name)
                await_read(dve, name)
                nc.vector.tensor_reduce(neg_max[:, i % 2, 0:1], sc[:, 0:n0], AX.X, ALU.max, negate=True)
                nc.vector.tensor_reduce(neg_max[:, i % 2, 1:2], sc[:, n0:], AX.X, ALU.max, negate=True).then_inc(done, 1)

            def normalise(i, pr, n0, exp_done, done):
                dve.wait_ge(exp_done, i + 1)
                link(nc.vector.reciprocal(inv_sum[:, i % 2, :], sums[:, i % 2, :]))
                nc.vector.tensor_scalar(pr[:, 0:n0], pr[:, 0:n0], inv_sum[:, i % 2, 0:1], None, ALU.mult)
                nc.vector.tensor_scalar(pr[:, n0:], pr[:, n0:], inv_sum[:, i % 2, 1:2], None, ALU.mult).then_inc(done, 1)

            def mla_norm(i):
                normalise(i, probs[:, i % 2, :], S0, s["exp_done"], s["probs_ready"])

            def mla_gated(i):
                dve.wait_ge(s["heads_done"], 2 * i + 2)
                taken(nc.vector.tensor_tensor(u_mla[:, i, :], acc[:, pair("heads%d" % i), 0, 0:ROWS], mla_gate[:, i, :],
                                              ALU.mult), "heads%d" % i)

            def mla_rest(i):
                dve.wait_ge(s["u_mla_rounded"], i + 1)
                rest(u_mla_lo[:, i, :], u_mla[:, i, :], u_mla_hi[:, i, :]).then_inc(s["u_mla_split"], 1)

            for n in range(HEADS + 2):
                if n in (5, 7, 9):
                    mla_gated((n - 5) // 2)
                if 1 <= n <= HEADS:
                    mla_norm(n - 1)
                if n % 5 == 0:
                    take_out("conf", n // 5)
                if n < HEADS:
                    masked_max(n, "s%d" % n, S0, scores[:, n % 2, :], float(QK) ** -0.5, "mask_mla", s["max_ready"])
                lead(Slot(FIRST["y_conf0"] + n, n, None))
                if n in (7, 9):
                    mla_rest((n - 7) // 2)
            mla_gated(3)
            mla_rest(2)
            mla_rest(3)
            dve.wait_ge(s["m_added"], 8)
            dve.wait_ge(s["mla_gates"], 3)
            for i in range(5):
                if i < 4:
                    slot_done(dve, "y_mla", i)
                    gate_out("mla", i)
                    await_out(dve, "y_mla%d" % i)
                    nc.vector.tensor_tensor(halves(m, i), halves(m, i), y_gated[:, (gated[0] - 1) % 2],
                                            ALU.add).then_inc(s["m_ready"], 1)
                if i >= 1:
                    dve.wait_ge(s["m_rounded"], i)
                    rest(halves(m_lo, i - 1), halves(m, i - 1), halves(m_hi, i - 1)).then_inc(s["m_split"], 1)
            handed_back("w_o")
            for sl in over_slots(dve, FIRST["w_o"], 5, loops=0):
                lead(sl)
            dve.wait_ge(s["gain_loaded"], 16)
            for t in range(TILES):
                dve.wait_ge(s["wo_ssq"], t + 1)
                v, r, u = [rs[:, i, t:t + 1] for i in range(3)]
                link(nc.vector.tensor_tensor(u, ssq[:, 2 * t:2 * t + 1], ssq[:, 2 * t + 1:2 * t + 2], ALU.add))
                link(mean_eps(v, u, DM, EPS))
                newton_col(v, r, u)
                for hf in range(2):
                    cols = slice(hf * 512, hf * 512 + 512)
                    name = "w_o%d" % hf
                    ins = nc.vector.scalar_tensor_tensor(y[:, t, cols], acc[:, pair(name), t, :], r, gain[:, cols],
                                                         ALU.mult, ALU.mult)
                    if t == TILES - 1:
                        taken(ins, name)
                        await_out(dve, name)
                    else:
                        link(ins)
                    add = nc.vector.tensor_tensor(x[:, t, cols], x[:, t, cols], y[:, t, cols], ALU.add)
                    add.then_inc(s["x_ready%d" % t], 1)

            splits = [0]

            def rest_rows(tag):
                for u in range(4):
                    t, j = u // 2, u % 2
                    splits[0] += 1
                    dve.wait_ge(s["x_rounded"], splits[0])
                    read(rest(x_lo[:, 4 * j:4 * j + 4, t * P:t * P + P], bank("%s_%d" % (tag, u))
                              .rearrange("p (c r) -> p c r", c=4), x_hi[:, 4 * j:4 * j + 4, t * P:t * P + P]), "%s_%d" % (tag, u))

            def residuals(t, parts):
                for name, hf in parts:
                    cols = slice(hf * 512, hf * 512 + 512)
                    ins = nc.vector.scalar_tensor_tensor(y[:, t, cols], x[:, t, cols], ALPHA, acc[:, pair(name), t, :],
                                                         ALU.mult, ALU.add)
                    if t == TILES - 1:
                        taken(ins, name)
                    else:
                        n = count(ins)
                for name, hf in parts:
                    if t == TILES - 1:
                        await_out(dve, name)
                    else:
                        dve.wait_ge(dve_chain, n)
                    last = nc.vector.bn_stats(stats[:, t, hf, :], y[:, t, hf * 512:hf * 512 + 512])
                link(last)

            def norm_tile(k, t):
                mean, var = mu_var[:, t, 0:1], mu_var[:, t, 1:2]
                v, r, u = [rs[:, i, t:t + 1] for i in range(3)]

                def centre(q):
                    cols = slice(q * 256, q * 256 + 256)
                    nc.vector.scalar_tensor_tensor(y[:, t, cols], y[:, t, cols], mean, gain[:, cols], ALU.subtract, ALU.mult)

                link(nc.vector.bn_aggr(mu_var[:, t, :], stats[:, t].rearrange("p h e -> p (h e)")))
                link(nc.vector.tensor_scalar(v, var, LN_EPS, None, ALU.add))
                dve.wait_ge(s["norm_loaded"], 32 * (k + 1))
                newton_col(v, r, u, centre, s["rstd_tile0"] if t == 0 else None)
                if t == 1:
                    for hf in range(2):
                        cols = slice(hf * 512, hf * 512 + 512)
                        nc.vector.scalar_tensor_tensor(x[:, t, cols], y[:, t, cols], r, shift[:, cols], ALU.mult,
                                                       ALU.add).then_inc(s["x_ready1"], 1)

            rest_rows("x1")
            handed_back("gla_gk")
            for stage in ("gla_gk", "gla_q"):
                for sl in over_slots(dve, FIRST[stage], COUNT[stage]):
                    lead(sl)
            for sl in over_slots(dve, FIRST["gla_k"], 4, loops=0):
                lead(sl)
                if sl.index == 0:
                    for j in range(2):
                        dve.wait_ge(s["la_abs"], j + 1)
                        for i in range(2):
                            c = 2 * j + i
                            last = nc.vector.tensor_scalar(la[:, c, :], bank("la%d" % j)[:, i * ROWS:(i + 1) * ROWS],
                                                           col("gla_b_gk_2", c), 0.0, ALU.add, ALU.min)
                        read(last, "la%d" % j)
                    dve.wait_ge(s["la_log"], 1)
                    await_read(dve, "la0")
                    await_read(dve, "la1")
                    link(nc.vector.tensor_tensor(la[:], la[:], la_e[:], ALU.subtract))
                    dve.wait_ge(s["zeroed"], 1)
                    flat = "p h r -> p (h r)"
                    nc.vector.tensor_tensor_scan(la_e[:].rearrange(flat), reset[:].rearrange(flat), la[:].rearrange(flat), 0.0,
                                                 ALU.mult, ALU.add).then_inc(s["cum_ready"], 1)
                    dve.wait_ge(s["cum_ready"], 1)
                    chunks = la_e[:].rearrange("p h (n i) -> p (h n) i", i=CH)
                    nc.vector.tensor_tensor(la[:].rearrange("p h (n i) -> p (h n) i", i=CH),
                                            chunks[:, :, CH - 1:CH].to_broadcast([P, GLA_H * NCH, CH]), chunks,
                                            ALU.subtract).then_inc(s["end_ready"], 1)
            for sl in over_slots(dve, FIRST["gla_v"], 8, loops=0):
                lead(sl)
                if sl.index == 0:
                    await_out(dve, "gla_q0")
                    await_out(dve, "gla_q1")
                    dve.wait_ge(s["e_ready"], 3)
                    nc.vector.tensor_tensor(qd[:], gq[:], e_cum[:], ALU.mult).then_inc(s["qd_ready"], 1)
                if sl.index == 1:
                    await_out(dve, "gla_k0")
                    await_out(dve, "gla_k1")
                    nc.vector.tensor_tensor(ki[:], gk[:], e_inv[:], ALU.mult).then_inc(s["ki_ready"], 1)
                if sl.index == 2:
                    nc.vector.tensor_tensor(ke[:], gk[:], e_end[:], ALU.mult).then_inc(s["ke_ready"], 1)
            def gate_head(hd):
                if hd == 2:
                    dve.wait_ge(s["gg1_ready"], 1)
                else:
                    await_out(dve, "gla_g1")
                cols = slice(hd * DV, (hd + 1) * DV)
                nc.vector.tensor_tensor(gg[:, :, cols], gg[:, :, cols], y[:, :, cols], ALU.mult).then_inc(s["o_gated"], 1)

            def rest_gated(hf):
                for j in (2 * hf, 2 * hf + 1):
                    dve.wait_ge(s["o_rounded"], j + 1)
                    read(rest(halves(o_lo, j), bank("ot%d" % j).rearrange("p (c r) -> p c r", c=2), halves(o_hi, j)), "ot%d" % j)

            for sl in over_slots(dve, FIRST["gla_g"], 8, loops=0):
                lead(sl)
                if sl.index == 2:
                    for hd in range(GLA_H):
                        a, b = "upd%da" % hd, "upd%db" % hd
                        await_full(dve, a)
                        nc.vector.tensor_copy(state[:, hd, 0, :], bank(a)[:, 0:DV]).then_inc(s["state_ready"], 1)
                        dve.wait_ge(s["state_ready"], hd + 1)
                        read(nc.vector.scalar_tensor_tensor(state[:, hd, 1, :], state[:, hd, 0, :],
                                                            e_cum[:, hd, 2 * CH - 1:2 * CH], bank(a)[:, DV:2 * DV],
                                                            ALU.mult, ALU.add), a)
                        await_full(dve, b)
                        await_read(dve, a)
                        read(nc.vector.scalar_tensor_tensor(state[:, hd, 2, :], state[:, hd, 1, :],
                                                            e_cum[:, hd, 3 * CH - 1:3 * CH], bank(b)[:, 0:DV],
                                                            ALU.mult, ALU.add), b)
                if sl.index == 4:
                    dve.wait_ge(s["o_ssq"], 8)
                    link(mean_eps(rs[:, 0, :], ssq[:], DV, EPS))
                    link(newton(rs[:, 0, :], rs[:, 1, :], rs[:, 2, :]))
                    dve.wait_ge(s["gg0_ready"], 1)
                    for j in (0, 2, 1, 3):
                        for i in range(2):
                            hd = j % 2 * 2 + i
                            cols = slice(hd * DV, (hd + 1) * DV)
                            dst, by = (gg, gg[:, j // 2, cols]) if hd < 2 else (y, head_gain[:])
                            last = nc.vector.scalar_tensor_tensor(dst[:, j // 2, cols], bank("o%d" % j)[:, i * DV:(i + 1) * DV],
                                                                  rs[:, 1, 2 * j + i:2 * j + i + 1], by, ALU.mult, ALU.mult)
                        read(last, "o%d" % j)
                if sl.index == 7:
                    rest_gated(0)
            for j in (1, 3):
                await_read(dve, "o%d" % j)
            gate_head(2)
            gate_head(3)

            def out_stage(stage, k):
                lent = 0
                if stage == "gla_out":
                    rest_gated(1)
                    lent = 3
                    dve.wait_ge(split, FIRST[stage] + LEAD + lent)
                for sl in over_slots(dve, FIRST[stage], 5, loops=0):
                    if sl.index >= lent:
                        lead(sl)
                    if sl.index == 3:
                        slot_done(dve, stage, 3)
                        for t in range(TILES):
                            residuals(t, [(stage + "0", 0)])
                dve.wait_ge(s["tile0_done"], TAILS[stage])
                for t in range(TILES):
                    if t == 1:
                        slot_done(dve, stage, 7)
                    residuals(t, [(stage + "1", 1)])
                    norm_tile(k, t)

            out_stage("gla_out", 0)

            def swiglu(layer):
                tag = "gu%d" % layer
                og = OUT[tag + "_0"]
                for sl in over_slots(dve, FIRST[tag], COUNT[tag]):
                    lead(sl)
                    if sl.index == 3:
                        dve.wait_ge(weights_used, sl.number(1))
                        dve.wait_ge(evacuated[og % 2], sl.loop + (og // 2 + 1))
                        nc.vector.tensor_tensor(hidden[:], h_gate[:], acc[:, (og + 1) % 2, :, 0:ROWS],
                                                ALU.mult).then_inc(evacuated[(og + 1) % 2], 1)
                        dve.wait_ge(s["h_rounded"], sl.loop + (layer * (FCH // 2) + 1))
                        rest(h_lo[:, bass.ds(sl.loop * 2, 2), :], hidden[:],
                             h_hi[:, bass.ds(sl.loop * 2, 2), :]).then_inc(s["h_split"], 1)
                stage = "down%d" % layer
                for sl in over_slots(dve, FIRST[stage], COUNT[stage] - 3, loops=4):
                    lead(sl)
                for t in range(TILES):
                    for hf in range(2):
                        if t == 0 or hf == 0:
                            dve.wait_ge(s["down_part"], 3 * layer + 2 * t + hf + 1)
                        else:
                            slot_done(dve, stage, COUNT[stage] - 1)
                        residuals(t, [("%s_%d" % (stage, hf), hf)])
                    norm_tile(2 * layer + 1, t)

            rest_rows("x2")
            handed_back("gu0")
            swiglu(0)
            rest_rows("x3")
            handed_back("moba_q")
            r32 = slice(0, ROPE)

            def moba_rotate(src, swap, swapped, done, pairs):
                t = mrope[r32, :].rearrange("p (h r) -> p h r", h=2)
                for j in pairs:
                    hs = slice(2 * j, 2 * j + 2)
                    dve.wait_ge(s["swapped_%s%d" % (swapped, j // 2)], 32)
                    nc.vector.tensor_tensor(t, swap[r32, hs, :], two_heads(trig[r32, 1, :]), ALU.mult)
                    link(nc.vector.tensor_tensor(src[r32, hs, :], src[r32, hs, :], two_heads(trig[r32, 0, :]), ALU.mult))
                    nc.vector.tensor_tensor(src[r32, hs, :], src[r32, hs, :], t, ALU.add).then_inc(done, 1)
                    dve.wait_ge(done, j + 1)

            for sl in over_slots(dve, FIRST["moba_q"], 8):
                lead(sl)
            dve.wait_ge(s["trig_ready"], 1)
            for sl in over_slots(dve, FIRST["moba_k"], 8, loops=0):
                lead(sl)
                if sl.index == 4:
                    moba_rotate(mq, mq_swap, "q", s["mq_roped"], range(4))
            moba_rotate(mk, mk_swap, "k", s["mk_roped"], range(2))

            def moba_norm(i):
                normalise(i, mprobs[:, i % 2, :], P, s["m_exp"], s["m_probs"])

            for i in range(HEADS):
                if i == 0:
                    moba_rotate(mk, mk_swap, "k", s["mk_roped"], range(2, 4))
                if i >= 1:
                    moba_norm(i - 1)
                masked_max(i, "ms%d" % i, P, mscores[:, i % 2, :], float(HD) ** -0.5, "mask_moba", s["m_max"])
                lead(Slot(FIRST["moba_v"] + i, i, None))
            moba_norm(HEADS - 1)
            for i in range(4):
                dve.wait_ge(s["mo_rounded"], i + 1)
                taken(rest(halves(mo_lo, i), out_t("moba_heads%d" % i), halves(mo_hi, i)), "moba_heads%d" % i)
            out_stage("moba_out", 2)
            rest_rows("x4")
            handed_back("gu1")
            swiglu(1)

        @block.gpsimd
        def _(pool):
            chained = [0]

            def link(ins):
                chained[0] += 1
                ins.then_inc(pool_chain, 1)
                pool.wait_ge(pool_chain, chained[0])

            nc.gpsimd.memset(ssq[:], 0.0).then_inc(s["cleared"], 1)
            nc.gpsimd.memset(w_pool[:], 0.0).then_inc(s["cleared"], 1)
            nc.gpsimd.memset(half_pi[:], float(np.pi / 2)).then_inc(s["cleared"], 1)
            nc.gpsimd.memset(vt[:, 0, :], 0.0).then_inc(s["cleared"], 1)
            await_out(pool, "z2")
            src, reach = pool_v, 1
            for g, dst in enumerate((pool_a, pool_b, pool_a, pool_b)):
                w = 2 * reach
                lo = w - 1
                link(nc.gpsimd.tensor_tensor(dst[:, :, lo:], src[:, :, lo:], src[:, :, lo - reach:KEYS - reach], ALU.add))
                r = slice(g % 2 * 64, g % 2 * 64 + 64)
                link(nc.gpsimd.tensor_scalar(pooled[r, g // 2, :], dst[r, g // 2, META:], 1.0 / w, None, ALU.mult))
                ins = nc.gpsimd.tensor_tensor(pooled[r, g // 2, :], pooled[r, g // 2, :], pool_v[r, g // 2, META:], ALU.subtract)
                if g < 3:
                    link(ins)
                else:
                    ins.then_inc(s["pooled_ready"], 1)
                src, reach = dst, w
            pool.wait_ge(s["pooled_ready"], 1)
            await_out(pool, "z3")
            await_out(pool, "z4")
            nc.gpsimd.tensor_tensor(glu[:], glu[:], glu_g[:], ALU.mult).then_inc(s["glu_ready"], 1)
            await_out(pool, "z5")
            await_out(pool, "z6")
            nc.gpsimd.tensor_tensor(sc_x[:], sc_c[:], sc_x[:], ALU.mult).then_inc(s["sc_ready"], 1)
            pool.wait_ge(s["sc_ready"], 1)
            pool.wait_ge(s["kr_roped"], 1)
            for i in range(HEADS):
                last = nc.gpsimd.tensor_copy(kT[NOPE:QK, i, :], kr_t[NOPE:QK, :])
            last.then_inc(s["k_spread"], 1)
            pool.wait_ge(s["k_spread"], 1)
            pool.wait_ge(s["sc_split"], 1)
            pool.wait_ge(s["pool_split"], 1)
            nc.gpsimd.memset(metaT[:], 0.0).then_inc(s["meta_cleared"], 1)
            n = 0
            for b in ("pool", "conf"):
                for i in range(4):
                    await_out(pool, "y_%s%d" % (b, i))
                    if n >= 4:
                        pool.wait_ge(s["m_added"], n - 3)
                    nc.gpsimd.tensor_tensor(m[:, 2 * i:2 * i + 2, :], m[:, 2 * i:2 * i + 2, :], y_gated[:, n % 2],
                                            ALU.add).then_inc(s["m_added"], 1)
                    n += 1

            def lend(first, count):
                for at in range(first, min(first + count, TOTAL)):
                    k = at % RING
                    pool.wait_ge(rounded, at + 1)
                    pool.wait_ge(split, at)
                    nc.gpsimd.tensor_tensor(w_lo[:, k, :], staged[:, k, :], w_hi[:, k, :].bitcast(F32),
                                            ALU.subtract).then_inc(split, 1)

            def load_norm(k):
                pool.wait_ge(s["x_ready0"], 2 * k + 2)
                pool.wait_ge(s["x_ready1"], 2 * k + 2)
                pool.dma_start(gain[:], d["ln_g_2"][k // 2, k % 2].partition_broadcast(P)).then_inc(s["norm_loaded"], 16)
                pool.dma_start(shift[:], d["ln_b_2"][k // 2, k % 2].partition_broadcast(P)).then_inc(s["norm_loaded"], 16)

            lend(FIRST["y_mla"] + LEAD, 4)
            lend(FIRST["gla_gk"], LEAD)
            load_norm(0)
            link(nc.gpsimd.memset(reset[:], 1.0))
            nc.gpsimd.memset(reset[:].rearrange("p h (n i) -> p (h n) i", i=CH)[:, :, 0:1], 0.0).then_inc(s["zeroed"], 1)
            nc.gpsimd.memset(intra[:], 0.0).then_inc(s["zeroed"], 1)
            nc.gpsimd.memset(ke_half[:], 0.0).then_inc(s["zeroed"], 1)
            nc.gpsimd.memset(qd_half[:], 0.0).then_inc(s["zeroed"], 1)
            pool.wait_ge(s["qd_ready"], 1)
            pool.wait_ge(s["zeroed"], 4)
            for c in range(2):
                view = "p h (t c i) -> p (h t) c i"
                nc.gpsimd.tensor_copy(qd_half[:, c].rearrange(view, t=TILES, c=2)[:, :, c, :],
                                      qd[:].rearrange(view, t=TILES, c=2)[:, :, c, :]).then_inc(s["half_ready"], 1)
            await_read(pool, "sg0")
            await_read(pool, "sg1")
            pool.wait_ge(s["half_ready"], 2)
            for c in range(2):
                if c == 1:
                    pool.wait_ge(s["intra_ready"], 1)
                blk = intra[c * CH:c * CH + CH, :, c * CH:c * CH + CH]
                nc.gpsimd.affine_select(out=blk, in_=blk, pattern=[[0, GLA_H * TILES], [1, CH]], compare_op=ALU.is_ge, fill=0.0,
                                        base=0, channel_multiplier=-1).then_inc(s["intra_ready"], 1)
            pool.wait_ge(s["gk_loaded"], 32)
            pool.wait_ge(s["intra_ready"], 2)
            await_out(pool, "gla_g0")
            for t in range(TILES):
                g = gg[:, t, 0:512].rearrange("p (h e) -> p h e", h=2)
                last = nc.gpsimd.tensor_tensor(g, g, head_gain[:].unsqueeze(1).to_broadcast([P, 2, DV]), ALU.mult)
            last.then_inc(s["gg0_ready"], 1)
            lend(FIRST["gla_out"] + LEAD, 3)
            def norm_tile0(k):
                for hf in range(2):
                    cols = slice(hf * 512, hf * 512 + 512)
                    pool.wait_ge(s["scaled0"], 2 * k + hf + 1)
                    nc.gpsimd.tensor_tensor(x[:, 0, cols], y[:, 0, cols], shift[:, cols], ALU.add).then_inc(s["x_ready0"], 1)

            for k, stage in enumerate(("gu0", "moba_q", "gu1")):
                lend(FIRST[stage], 1)
                norm_tile0(k)
                lend(FIRST[stage] + 1, LEAD - 1)
                load_norm(k + 1)
                if stage == "moba_q":
                    half = ROPE // 2
                    for name, src, swap, swapped in (("moba_q", mq, mq_swap, "q"), ("moba_k", mk, mk_swap, "k")):
                        for j in range(2):
                            hs = slice(4 * j, 4 * j + 4)
                            done = s["swapped_%s%d" % (swapped, j)]
                            await_out(pool, "%s%d" % (name, 2 * j))
                            await_out(pool, "%s%d" % (name, 2 * j + 1))
                            pool.dma_start(swap[0:half, hs, :], src[half:ROPE, hs, :]).then_inc(done, 16)
                            pool.dma_start(swap[half:ROPE, hs, :], src[0:half, hs, :]).then_inc(done, 16)
            norm_tile0(3)


_NAMES = ["x", "meta_tokens", "pre_norm_g", "w_in", "gate_bias", "pool_w", "pool_scale", "w_out_pool", "q_norm_g", "w_uq",
          "kv_norm_g", "w_ukv", "w_out_mla", "conf_dw_w", "conf_dw_b", "conf_ln_g", "conf_ln_b", "w_out_conf", "sc_dw_w",
          "w_out_sc", "w_o", "post_norm_g", "positions_2", "gla_w_in_2", "gla_w_gk_2", "gla_b_gk_2", "gla_norm_g_2",
          "gla_w_out_2", "moba_w_in_2", "moba_w_out_2", "ffn_w_gu_2", "ffn_w_down_2", "ln_g_2", "ln_b_2"]


def kernel(**inputs):
    import concourse.bacc as bacc
    from concourse.bass_utils import run_bass_kernel_spmd

    nc = bacc.Bacc("TRN2", target_bir_lowering=False, num_devices=1)
    arrays = {n: np.ascontiguousarray(inputs[n]) for n in _NAMES}
    arrays["constants"] = constants()
    d = {n: nc.dram_tensor("in_" + n, a.shape, mybir.dt.from_np(a.dtype), kind="ExternalInput").ap()
         for n, a in arrays.items()}
    out = nc.dram_tensor("out", (1, ROWS, DM), F32, kind="ExternalOutput").ap()
    hybrid_stack(nc, d, out)
    r = run_bass_kernel_spmd(nc, [{"in_" + n: a for n, a in arrays.items()}], core_ids=[0])
    return r.results[0]["out"]
```

```python
from contextlib import ExitStack

import numpy as np

import concourse.bass as bass
import concourse.mybir as mybir

F32 = mybir.dt.float32
F32R = mybir.dt.float32r
I32 = mybir.dt.int32
ALU = mybir.AluOpType
ACT = mybir.ActivationFunctionType
AX = mybir.AxisListType

P = 128
ROWS, META, DM = 256, 16, 1024
KEYS = ROWS + META
TILES, KC = ROWS // P, DM // P
EPS, LN_EPS = 1e-6, 1e-5
ALPHA = (2.0 * 2) ** 0.25
SLOT, RING, LEAD = 1024, 4, 3
HEADS, NOPE, ROPE, VD = 8, 64, 32, 64
QK = NOPE + ROPE
CONF_K, SC_K = 31, 3
GLA_H, DK, DV, CH = 4, 128, 256, 64
NCH = ROWS // CH
FFN = 2816
FCH = FFN // P
HD = 128
NEG = -1e30

Z_BLOCKS = [("ckv_kr", 768), ("cq", 512), ("pool_v", 0), ("conf_a", 1440), ("conf_g", 1696), ("sc_c", 2464),
            ("sc_x", 2720), ("sc_b", 2208), ("sc_gate", 2976), ("pool_gate", 256), ("conf_gate", 1952),
            ("mla_gate0", 928), ("mla_gate1", 1184)]
GATE_COL0 = 3232
BRANCH = {"pool": 0, "mla": 1, "conf": 2, "sc": 3}

STAGES = [("z", 26), ("gate_sc", 8)]
for _u, _b in (("sc", "pool"), ("pool", "conf"), ("conf", "mla")):
    STAGES += [("y_%s0" % _u, 1), ("gate_%s0" % _b, 4), ("y_%s1" % _u, 1), ("gate_%s1" % _b, 4)]
STAGES += [("y_mla", 4), ("w_o", 8), ("gla_gk", 2), ("gla_q", 4), ("gla_k", 4), ("gla_v", 8), ("gla_g", 8),
           ("gla_out", 8), ("gu0", 44), ("down0", 22), ("moba_q", 8), ("moba_k", 8), ("moba_v", 8), ("moba_out", 8),
           ("gu1", 44), ("down1", 22)]
FIRST, COUNT, TOTAL = {}, {}, 0
for _name, _n in STAGES:
    FIRST[_name], COUNT[_name] = TOTAL, _n
    TOTAL += _n

OUTS = ["z%d" % _i for _i in range(13)]
OUTS += ["gate_sc%d" % _i for _i in range(4)]
for _u, _b in (("sc", "pool"), ("pool", "conf")):
    for _i in (0, 2):
        OUTS += ["y_%s%d" % (_u, _i), "y_%s%d" % (_u, _i + 1), "gate_%s%d" % (_b, _i), "gate_%s%d" % (_b, _i + 1)]
OUTS += ["y_conf0", "y_conf1", "gate_mla0", "gate_mla1", "heads0", "y_conf2", "y_conf3", "heads1", "gate_mla2", "heads2",
         "gate_mla3", "heads3"]
OUTS += ["y_mla%d" % _i for _i in range(4)] + ["w_o0", "w_o1", "gla_gk", "gla_q0", "gla_q1", "gla_k0", "gla_k1",
                                              "gla_v0", "gla_v1", "gla_g0", "gla_g1", "gla_out0", "gla_out1"]
OUTS += ["gu0_%d" % _i for _i in range(22)] + ["down0_0", "down0_1"]
OUTS += ["moba_q%d" % _i for _i in range(4)] + ["moba_k%d" % _i for _i in range(4)] + ["moba_v0", "moba_v1"]
OUTS += ["moba_heads0", "moba_heads1", "moba_out0", "moba_out1"]
OUTS += ["gu1_%d" % _i for _i in range(22)] + ["down1_0", "down1_1"]
OUT = {_n: _i for _i, _n in enumerate(OUTS)}

MISC = ["vec"] + ["x0_%d" % _i for _i in range(KC)] + ["ssq_kv", "ssq_cq"]
MISC += ["uq%d" % _i for _i in range(4)] + ["kn%d" % _i for _i in range(8)] + ["vt%d" % _i for _i in range(3)]
MISC += ["pool", "krs", "krc", "conf_mean", "conf_var"]
for _h in range(HEADS + 2):
    MISC += (["s%d" % _h] if _h < HEADS else []) + (["pt%d" % (_h - 2), "pm%d" % (_h - 2)] if _h >= 2 else [])
MISC += ["x1_%d" % _i for _i in range(4)] + ["la0", "la1", "sg0", "sg1", "ke0", "ke1"]
for _h in range(GLA_H):
    MISC += ["upd%da" % _h, "upd%db" % _h]
MISC += ["o%d" % _i for _i in range(4)] + ["ot%d" % _i for _i in range(4)] + ["x2_%d" % _i for _i in range(4)]
MISC += ["x3_%d" % _i for _i in range(4)]
for _h in range(HEADS + 2):
    MISC += (["ms%d" % _h] if _h < HEADS else []) + (["mt%d" % (_h - 2)] if _h >= 2 else [])
MISC += ["x4_%d" % _i for _i in range(4)]
TURN_ORDER = (0, 2, 1, 3)
TAILS = {_n: _i + 1 for _i, _n in enumerate(["w_o", "gla_out", "moba_out"])}
BANK = {_n: _i for _i, _n in enumerate(MISC)}

VEC_ROWS = [("pre_norm_g", 8), ("gate_bias", 32), ("pool_scale", 2), ("q_norm_g", 2), ("kv_norm_g", 1),
            ("conf_dw_w", 2 * CONF_K), ("conf_dw_b", 2), ("conf_ln_g", 2), ("conf_ln_b", 2), ("sc_dw_w", 2 * SC_K),
            ("gla_b_gk_2", 4)]
VEC, VEC_N = {}, 0
for _name, _n in VEC_ROWS:
    VEC[_name] = VEC_N
    VEC_N += _n

S0, S1 = META + P, META + ROWS
CONST = {}
CONST_N = 0
for _name, _n in [("ident", P), ("ones", P), ("mask_mla", S0 + S1), ("mask_moba", P + ROWS), ("cos", KEYS),
                  ("sin", KEYS), ("swap", ROPE), ("inv_freq", 1), ("sign", 1)]:
    CONST[_name] = CONST_N
    CONST_N += _n


def constants():
    c = np.zeros((P, CONST_N), np.float32)

    def put(name, rows, block):
        c[rows, CONST[name]:CONST[name] + block.shape[1]] = block

    every = slice(0, P)
    put("ident", every, np.eye(P, dtype=np.float32))
    put("ones", every, np.ones((P, P), np.float32))
    q, k = np.arange(P)[:, None], np.arange(S1)[None, :]
    m0 = np.where(k[:, :S0] <= q + META, 0, NEG)
    m1 = np.where(k <= q + META + P, 0, NEG)
    put("mask_mla", every, np.concatenate([m0, m1], 1).astype(np.float32))
    k = np.arange(ROWS)[None, :]
    put("mask_moba", every, np.concatenate([np.where(k[:, :P] <= q, 0, NEG), np.where(k <= q + P, 0, NEG)], 1)
        .astype(np.float32))
    inv = (1.0 / (np.float32(10000.0) ** (np.arange(0, ROPE, 2, dtype=np.float32) / np.float32(ROPE)))).astype(np.float32)
    ang = (np.arange(KEYS, dtype=np.float32)[None, :] * inv[:, None]).astype(np.float32)
    rope = slice(NOPE, NOPE + ROPE)
    put("cos", rope, np.concatenate([np.cos(ang), np.cos(ang)]).astype(np.float32))
    put("sin", rope, np.concatenate([-np.sin(ang), np.sin(ang)]).astype(np.float32))
    swap = np.roll(np.eye(ROPE, dtype=np.float32), ROPE // 2, axis=1)
    put("swap", slice(0, ROPE), swap)
    put("swap", rope, swap)
    inv2 = np.power(np.float32(500000.0), -np.arange(0, 32, 2, dtype=np.float32) / np.float32(32)).astype(np.float32)
    put("inv_freq", slice(0, 32), np.concatenate([inv2, inv2])[:, None])
    put("sign", slice(0, 32), np.concatenate([-np.ones(16), np.ones(16)]).astype(np.float32)[:, None])
    return c


Z_TAPS = {11 + _i: (2 * _i, 2 * _i + 2) for _i in range(6)}
Z_TAPS.update({17: (12, 13), 18: (13, 14), 20: (14, 15), 21: (15, 16), 23: (16, 17), 25: (17, 19)})


class Slot:

    def __init__(self, at, index, loop, body=RING):
        self.at, self.index, self.loop, self.body = at, index, loop, body

    def number(self, ahead=0):
        return self.at + ahead if self.loop is None else self.loop * self.body + (self.at + ahead)

    def ring(self, ahead=0):
        return (self.at + ahead) % RING

    def uses(self, ahead=0):
        n = (self.at + ahead) // RING
        return n if self.loop is None else self.loop * (self.body // RING) + n


def over_slots(eng, first, count, loops=None, body=RING):
    groups = count // body if loops is None else loops
    done = 0
    if groups >= 2:
        with eng.Fori(0, groups) as g:
            for j in range(body):
                yield Slot(first + j, j, g, body)
        done = body * groups
    for j in range(done, count):
        yield Slot(first + j, j, None)


def hybrid_stack(nc, d, out):
    with ExitStack() as ctx:
        cursor = [(nc.sbuf_base + 63) // 64 * 64]

        def place(name, cols, dt=F32):
            cols = [cols] if isinstance(cols, int) else list(cols)
            t = nc.alloc_sbuf_tensor_at(name, [P] + cols, dt, offset=cursor[0])
            cursor[0] += (int(np.prod(cols)) * 4 + 31) // 32 * 32
            return t

        staged = place("staged", [RING, SLOT])
        w_hi = place("w_hi", [RING, SLOT], F32R)
        w_lo = place("w_lo", [RING, SLOT], F32R)
        const = place("const", CONST_N)
        vec_rows = place("vec_rows", P)
        vec = place("vec", P)
        x = place("x", [TILES, DM])
        y = place("y", [TILES, DM])
        x_hi = place("x_hi", [KC, KEYS], F32R)
        x_lo = place("x_lo", [KC, KEYS], F32R)
        gain = place("gain", DM)
        shift = place("shift", DM)
        trig = place("trig", [2, ROWS])
        w_gk = place("w_gk", GLA_H * DK)
        head_gain = place("head_gain", DV)
        ssq = place("ssq", 8)
        rs = place("rs", [3, 8])
        mu_var = place("mu_var", [2, 2])
        stats = place("stats", [2, 2, 6])
        half_pi = place("half_pi", 1)
        neg_max = place("neg_max", [2, 2])
        sums = place("sums", [2, 2])
        inv_sum = place("inv_sum", [2, 2])
        region = cursor[0]

        kT = place("kT", [HEADS, KEYS])
        qT = place("qT", [HEADS, ROWS])
        end_qk = cursor[0]
        vt = place("vt", [3, HEADS * VD])
        mla_gate = place("mla_gate", [4, ROWS])
        conv = place("conv", [2, ROWS])
        conf_gate = place("conf_gate", [2, ROWS])
        glu = place("glu", [2, KEYS])
        glu_g = place("glu_g", [2, KEYS])
        gates = place("gates", [KC, ROWS])
        conf_sq = place("conf_sq", [2, ROWS])
        early = cursor[0]
        kv_z = place("kv_z", KEYS)
        kr_z = place("kr_z", KEYS)
        cq_z = place("cq_z", [2, ROWS])
        sq_kv = place("sq_kv", KEYS)
        sq_cq = place("sq_cq", [2, ROWS])
        w_uq = place("w_uq", [2, HEADS * QK])
        w_ukv = place("w_ukv", HEADS * (NOPE + VD))
        early_end = cursor[0]
        cursor[0] = early
        m = place("m", [KC, ROWS])
        y_gated = place("y_gated", [2, 2, ROWS])
        u_pool_hi = place("u_pool_hi", [2, ROWS], F32R)
        u_pool_lo = place("u_pool_lo", [2, ROWS], F32R)
        u_conf_hi = place("u_conf_hi", [2, ROWS], F32R)
        u_conf_lo = place("u_conf_lo", [2, ROWS], F32R)
        cursor[0] = max(cursor[0], early_end)
        u_sc_hi = place("u_sc_hi", [2, ROWS], F32R)
        u_sc_lo = place("u_sc_lo", [2, ROWS], F32R)
        rope_t = place("rope_t", 2 * ROWS)
        kr_t = place("kr_t", KEYS)
        mid = cursor[0]
        pool_v = place("pool_v", [2, KEYS])
        pool_a = place("pool_a", [2, KEYS])
        pool_b = place("pool_b", [2, KEYS])
        pooled = place("pooled", [2, ROWS])
        pool_gate = place("pool_gate", [2, ROWS])
        w_pool = place("w_pool", [2, P])
        sc_c = place("sc_c", [2, KEYS])
        sc_x = place("sc_x", [2, KEYS])
        sc_b = place("sc_b", [2, ROWS])
        sc_gate = place("sc_gate", [2, ROWS])
        sc_acc = place("sc_acc", [2, ROWS])
        mid_end = cursor[0]
        cursor[0] = mid
        scores = place("scores", [2, S0 + S1])
        probs = place("probs", [2, S0 + S1])
        probsT = place("probsT", [2, 3 * P])
        metaT = place("metaT", [2, ROWS])
        u_mla_hi = place("u_mla_hi", [4, ROWS], F32R)
        u_mla_lo = place("u_mla_lo", [4, ROWS], F32R)
        u_mla = place("u_mla", [4, ROWS])
        cursor[0] = max(cursor[0], mid_end)
        q_swap = place("q_swap", [HEADS, ROWS])
        end1 = cursor[0]
        cursor[0] = region
        m_hi = place("m_hi", [KC, ROWS], F32R)
        m_lo = place("m_lo", [KC, ROWS], F32R)
        assert cursor[0] <= end_qk

        cursor[0] = region
        gq = place("gq", [GLA_H, ROWS])
        gk = place("gk", [GLA_H, ROWS])
        la = place("la", [GLA_H, ROWS])
        la_e = place("la_e", [GLA_H, ROWS])
        gla_dead = cursor[0]
        gk_low = place("gk_low", ROWS)
        reset = place("reset", [GLA_H, ROWS])
        e_cum = place("e_cum", [GLA_H, ROWS])
        e_inv = place("e_inv", [GLA_H, ROWS])
        e_end = place("e_end", [GLA_H, ROWS])
        qd = place("qd", [GLA_H, ROWS])
        qd_half = place("qd_half", [2, GLA_H, ROWS])
        ki = place("ki", [GLA_H, ROWS])
        ke = place("ke", [GLA_H, ROWS])
        ke_half = place("ke_half", [2, GLA_H * TILES, P])
        gv = place("gv", [TILES, GLA_H * DV])
        gg = place("gg", [TILES, GLA_H * DV])
        state = place("state", [GLA_H, NCH - 1, DV])
        intra = place("intra", [GLA_H * TILES, P])
        end2 = cursor[0]
        cursor[0] = region
        o_hi = place("o_hi", [KC, ROWS], F32R)
        o_lo = place("o_lo", [KC, ROWS], F32R)
        assert cursor[0] <= gla_dead

        cursor[0] = region
        h_hi = place("h_hi", [FCH, ROWS], F32R)
        h_lo = place("h_lo", [FCH, ROWS], F32R)
        h_gate = place("h_gate", [2, ROWS])
        hidden = place("hidden", [2, ROWS])
        ffn_end = cursor[0]

        cursor[0] = region
        mo_hi = place("mo_hi", [KC, ROWS], F32R)
        mo_lo = place("mo_lo", [KC, ROWS], F32R)
        mq = place("mq", [HEADS, ROWS])
        mk = place("mk", [HEADS, ROWS])
        mv = place("mv", [TILES, DM])
        mscores = place("mscores", [2, P + ROWS])
        mprobs = place("mprobs", [2, P + ROWS])
        mprobsT = place("mprobsT", [HEADS, P + ROWS])
        mrope = place("mrope", 2 * ROWS)
        mrope_pool = place("mrope_pool", 2 * ROWS)
        mq_swap = place("mq_swap", [HEADS, ROWS])
        mk_swap = place("mk_swap", [HEADS, ROWS])
        end4 = cursor[0]
        assert max(end1, end2, ffn_end, end4) <= nc.sbuf_usable_end, (end1, end2, ffn_end, end4, nc.sbuf_usable_end)

        scratch = y[:].rearrange("p t c -> p (t c)")
        flat_gates = gates[:].rearrange("p c r -> p (c r)")
        m_rows, meta_h = flat_gates[0:META, 0:DM], flat_gates[0:META, DM:2 * DM]
        pos_i = kr_t[0:ROPE, 0:ROWS].bitcast(I32)
        trig_r, trig_abs = rope_t[0:ROPE, 0:ROWS], rope_t[0:ROPE, ROWS:2 * ROWS]
        trig_k, trig_kh = conf_sq[0:ROPE, 0, :], conf_sq[0:ROPE, 1, :]
        kvq_rs = [scratch[:, i * 528:(i + 1) * 528] for i in range(3)]

        acc = ctx.enter_context(nc.psum_tensor("acc", [P, 2, 2, 512], F32))
        misc = ctx.enter_context(nc.psum_tensor("misc", [P, 4, 512], F32))

        def sem(name):
            return ctx.enter_context(nc.semaphore(name))

        landed = [sem("landed%d" % i) for i in range(RING)]
        rounded, split, weights_used = sem("rounded"), sem("split"), sem("weights_used")
        evacuated = [sem("evacuated%d" % i) for i in range(2)]
        bank_full = [sem("bank_full%d" % i) for i in range(4)]
        bank_read = [sem("bank_read%d" % i) for i in range(4)]
        dve_chain, act_chain, pool_chain = sem("dve_chain"), sem("act_chain"), sem("pool_chain")
        s = {n: sem(n) for n in (
            "cleared", "conf_rounded", "conf_sig", "conf_split", "conf_squared", "conf_u", "conf_zn", "const_loaded",
            "conv_done", "cum_ready", "down_part", "e_ready", "end_ready", "exp_done", "gain_loaded", "gg0_ready",
            "gg1_ready", "gk_loaded", "glu_ready", "h_rounded", "h_split", "half_ready", "heads_done", "intra_ready",
            "k_spread", "ke_ready", "ki_ready", "kr_roped", "kv_normed", "la_abs", "la_log", "m_added", "m_exp",
            "m_heads_done", "m_max", "m_probs", "m_ready", "m_rounded", "m_split", "max_ready", "meta_cleared",
            "meta_loaded", "mk_roped", "mk_roped_pool", "mla_gates", "mla_loaded", "mo_rounded", "mo_split",
            "mq_roped", "mq_roped_pool", "norm_loaded", "normed", "o_gated", "o_rounded", "o_ssq", "pool_loaded",
            "pool_rounded", "pool_split", "pooled_ready", "pos_loaded", "probs_ready", "q_roped", "q_swapped",
            "qd_ready", "rstd0", "rstd_tile0", "sc_ready", "sc_rounded", "sc_split", "sc_u", "scaled0", "ssq0",
            "state_ready", "stored", "swapped_k0", "swapped_k1", "swapped_q0", "swapped_q1", "tables_loaded",
            "tile0_done", "trig_args", "trig_ready", "u_mla_rounded", "u_mla_split", "vec_loaded", "wo_ssq",
            "x0_rounded", "x1_loaded", "x_loaded", "x_ready0", "x_ready1", "x_rounded", "y_first", "zeroed")}

        def col(name, i=0):
            return vec[:, VEC[name] + i:VEC[name] + i + 1]

        def cst(name, n, rows=slice(0, P)):
            return const[rows, CONST[name]:CONST[name] + n]

        ident, ones = cst("ident", P), cst("ones", P)

        def pair(name):
            return OUT[name] % 2

        def await_out(eng, name):
            eng.wait_ge(evacuated[OUT[name] % 2], OUT[name] // 2 + 1)

        def bank(name):
            return misc[:, BANK[name] % 4, :]

        def await_full(eng, name):
            eng.wait_ge(bank_full[BANK[name] % 4], BANK[name] // 4 + 1)

        def await_read(eng, name):
            eng.wait_ge(bank_read[BANK[name] % 4], BANK[name] // 4 + 1)

        def read_sem(name):
            return bank_read[BANK[name] % 4]

        def slot_done(eng, stage, index):
            eng.wait_ge(weights_used, FIRST[stage] + index + 1)

        block = ctx.enter_context(nc.Block())

        @block.sync
        def _(sp):
            def slot_free(sl):
                if sl.loop is not None or sl.at >= RING:
                    sp.wait_ge(split, sl.number(1 - RING))

            def load(sl, src, cols=None):
                slot_free(sl)
                dst = staged[:, sl.ring(), :]
                if len(src.shape) == 3:
                    dst = dst.rearrange("p (c n) -> p c n", c=src.shape[1])
                if cols is not None:
                    dst = staged[:, sl.ring(), :].rearrange("p (c n) -> p c n", c=src.shape[1])[:, :, 0:cols]
                sp.dma_start(dst, src).then_inc(landed[sl.ring()], 16)

            def k_half(w, half, c0, n=256):
                return w[half * 512:(half + 1) * 512, bass.ds(c0, n)].rearrange("(c p) n -> p c n", p=P)

            def by_columns(stage, w, c0):
                for sl in over_slots(sp, FIRST[stage], COUNT[stage]):
                    block0 = c0 + sl.index // 2 * 256
                    load(sl, k_half(w, sl.index % 2, block0 if sl.loop is None else sl.loop * 512 + block0))

            def by_rows(stage, w, c0=0):
                for sl in over_slots(sp, FIRST[stage], COUNT[stage]):
                    q = sl.index % 4
                    cols = c0 + sl.index // 4 * 512
                    if sl.loop is not None:
                        cols = sl.loop * 512 + cols
                    load(sl, w[q * 256:(q + 1) * 256, bass.ds(cols, 512)].rearrange("(c p) n -> p c n", p=P))

            for t, name in enumerate(("x_loaded", "x1_loaded")):
                sp.dma_start(x[:, t, :], d["x"][0, t * P:t * P + P, :]).then_inc(s[name], 16)
            sp.dma_start(m_rows, d["meta_tokens"]).then_inc(s["meta_loaded"], 16)
            sp.dma_start(const[:, 0:2 * P], d["constants"][:, 0:2 * P]).then_inc(s["const_loaded"], 16)
            for name, n in VEC_ROWS:
                src = d[name]
                flat = src.rearrange("a k (c p) -> (a k c) p", p=P) if len(src.shape) == 3 else \
                    src.rearrange("a (c p) -> (a c) p", p=P)
                sp.dma_start(vec_rows[VEC[name]:VEC[name] + n, :], flat).then_inc(s["vec_loaded"], 16)
            w_in = d["w_in"][0]

            def z_slots(lo, hi):
                for sl in over_slots(sp, lo, hi - lo, loops=0):
                    load(sl, k_half(w_in, sl.at % 2, Z_BLOCKS[sl.at // 2][1]))

            z_slots(0, RING)
            sp.dma_start(const[:, 2 * P:], d["constants"][:, 2 * P:]).then_inc(s["tables_loaded"], 16)
            sp.dma_start(w_uq[:], d["w_uq"][0].rearrange("(c p) n -> p c n", p=P)).then_inc(s["mla_loaded"], 16)
            sp.dma_start(w_ukv[:], d["w_ukv"][0]).then_inc(s["mla_loaded"], 16)
            sp.dma_start(pos_i, d["positions_2"][0].partition_broadcast(32)).then_inc(s["pos_loaded"], 16)
            z_slots(RING, 2 * RING)
            sp.wait_ge(s["cleared"], 2)
            for g in range(4):
                r = slice(g % 2 * 64, g % 2 * 64 + 64)
                sp.dma_start(w_pool[r, g // 2, r], d["pool_w"][0, g]).then_inc(s["pool_loaded"], 16)
            z_slots(2 * RING, COUNT["z"])
            sp.dma_start(w_gk[0:16, :], d["gla_w_gk_2"][0]).then_inc(s["gk_loaded"], 16)
            sp.dma_start(head_gain[:], d["gla_norm_g_2"][0].partition_broadcast(P)).then_inc(s["gk_loaded"], 16)
            sp.dma_start(gain[:], d["post_norm_g"][0].partition_broadcast(P)).then_inc(s["gain_loaded"], 16)
            def gates_half(b, h):
                by_columns("gate_%s%d" % (b, h), w_in, GATE_COL0 + BRANCH[b] * DM + h * 512)

            by_columns("gate_sc", w_in, GATE_COL0 + BRANCH["sc"] * DM)
            for before, b in (("sc", "pool"), ("pool", "conf"), ("conf", "mla")):
                for h in range(2):
                    load(Slot(FIRST["y_%s%d" % (before, h)], 0, None),
                         d["w_out_" + before][0][:, h * 512:(h + 1) * 512].rearrange("(c p) n -> p c n", p=P))
                    gates_half(b, h)
            for sl in over_slots(sp, FIRST["y_mla"], 4, loops=0):
                load(sl, k_half(d["w_out_mla"][0], 0, sl.index * 256))
            by_rows("w_o", d["w_o"][0])
            gla = d["gla_w_in_2"][0]
            for sl in over_slots(sp, FIRST["gla_gk"], 2):
                load(sl, k_half(gla, sl.index, 3072, 16), cols=16)
            by_columns("gla_q", gla, 0)
            by_columns("gla_k", gla, 512)
            by_rows("gla_v", gla, 1024)
            by_rows("gla_g", gla, 2048)
            by_rows("gla_out", d["gla_w_out_2"][0])
            for layer in range(2):
                gu = d["ffn_w_gu_2"][layer]
                for sl in over_slots(sp, FIRST["gu%d" % layer], COUNT["gu%d" % layer]):
                    load(sl, k_half(gu, sl.index % 2, sl.loop * 256 + (FFN if sl.index % 4 >= 2 else 0)))
                dn = d["ffn_w_down_2"][layer]
                for sl in over_slots(sp, FIRST["down%d" % layer], COUNT["down%d" % layer]):
                    row = sl.index * P if sl.loop is None else sl.loop * (RING * P) + sl.index * P
                    load(sl, dn[bass.ds(row, P), :])
                if layer == 0:
                    mw = d["moba_w_in_2"][0]
                    by_columns("moba_q", mw, 0)
                    by_columns("moba_k", mw, DM)
                    by_rows("moba_v", mw, 2 * DM)
                    by_rows("moba_out", d["moba_w_out_2"][0])
            sp.wait_ge(s["x_ready0"], 10)
            sp.dma_start(out[0, 0:P, :], x[:, 0, :]).then_inc(s["stored"], 16)
            for hf in range(2):
                sp.wait_ge(s["x_ready1"], 9 + hf)
                cols = slice(hf * 512, hf * 512 + 512)
                sp.dma_start(out[0, P:ROWS, cols], x[:, 1, cols]).then_inc(s["stored"], 16)
            sp.wait_ge(s["stored"], 48)

        @block.tensor
        def _(pe):
            def open_out(name_or_index):
                o = OUT[name_or_index]
                if o >= 2:
                    pe.wait_ge(evacuated[o % 2], o // 2)

            def ready(sl):
                pe.wait_ge(split, sl.number(1))

            def exact(dst, st_hi, st_lo, mv_hi, mv_lo, start, stop):
                pe.matmul(dst, st_hi, mv_hi, start=start, stop=False)
                pe.matmul(dst, st_hi, mv_lo, start=False, stop=False)
                return pe.matmul(dst, st_lo, mv_hi, start=False, stop=stop)

            def t_slot(sl, p, half, mv_hi, mv_lo, kcs=4, last=True, halves=2, first=True):
                ready(sl)
                n = mv_hi.shape[-1]
                hi = w_hi[:, sl.ring(), :].rearrange("p (c n) -> p c n", c=4)
                lo = w_lo[:, sl.ring(), :].rearrange("p (c n) -> p c n", c=4)
                for b in range(halves):
                    for c in range(kcs):
                        cols = slice(b * P, b * P + P)
                        mm = exact(acc[:, p, b, 0:n], hi[:, c, cols], lo[:, c, cols],
                                   mv_hi[:, half * 4 + c, :], mv_lo[:, half * 4 + c, :],
                                   start=first and c == 0, stop=last and c == kcs - 1)
                mm.then_inc(weights_used, 1)

            def t_stage(first, count, out0, mv_hi, mv_lo, halves=2, body=RING):
                for sl in over_slots(pe, first, count, body=body):
                    o = out0 + sl.index // 2
                    if sl.index % 2 == 0:
                        if sl.loop is not None:
                            pe.wait_ge(evacuated[o % 2], sl.loop * (body // 4) + o // 2)
                        elif o >= 2:
                            pe.wait_ge(evacuated[o % 2], o // 2)
                    t_slot(sl, o % 2, sl.index % 2, mv_hi, mv_lo, halves=halves,
                           first=sl.index % 2 == 0, last=sl.index % 2 == 1)

            def t_slot_by_parts(sl, p, half, mv_hi, mv_lo, hi_ready, lo_ready, halves=2):
                ready(sl)
                n = mv_hi.shape[-1]
                hi = w_hi[:, sl.ring(), :].rearrange("p (c n) -> p c n", c=4)
                lo = w_lo[:, sl.ring(), :].rearrange("p (c n) -> p c n", c=4)
                for st, mv, await_rows in ((hi, mv_hi, hi_ready), (lo, mv_hi, None), (hi, mv_lo, lo_ready)):
                    if await_rows:
                        await_rows()
                    for b in range(halves):
                        for c in range(4):
                            mm = pe.matmul(acc[:, p, b, 0:n], st[:, c, b * P:b * P + P], mv[:, half * 4 + c, :],
                                           start=half == 0 and mv is mv_hi and st is hi and c == 0,
                                           stop=half == 1 and mv is mv_lo and c == 3)
                mm.then_inc(weights_used, 1)

            def t_first(first, name, tag, count, halves=2):
                turn_rows(tag, count)
                open_out(name)
                done = 4 * (int(tag[1]) - 1)
                for half in range(2):
                    t_slot_by_parts(Slot(first + half, half, None), pair(name), half, xt_hi, xt_lo,
                                    lambda: pe.wait_ge(s["x_rounded"], done + 2 * half + 2), lambda: half_ready(tag, half),
                                    halves=halves)

            def n_slots(stage, names, st_hi, st_lo, lo=0, hi=None):
                for i in range(lo, COUNT[stage] if hi is None else hi):
                    sl = Slot(FIRST[stage] + i, i, None)
                    q, name = i % 4, names[i // 4]
                    if q == 0:
                        open_out(name)
                    ready(sl)
                    for c in range(2):
                        cols = slice(c * 512, c * 512 + 512)
                        for t in range(TILES):
                            rows = slice(t * P, t * P + P)
                            k = q * 2 + c
                            mm = exact(acc[:, pair(name), t, :], st_hi[:, k, rows], st_lo[:, k, rows],
                                         w_hi[:, sl.ring(), cols], w_lo[:, sl.ring(), cols],
                                         start=k == 0, stop=k == KC - 1)
                    mm.then_inc(weights_used, 1)

            def n_product(stage, st_hi, st_lo, chunks_ready):
                names = [stage + "0", stage + "1"]
                for q in range(4):
                    chunks_ready(q)
                    n_slots(stage, names, st_hi, st_lo, q, q + 1)
                open_out(names[1])
                for t in range(TILES):
                    rows = slice(t * P, t * P + P)
                    for q in range(4):
                        sl = Slot(FIRST[stage] + 4 + q, 4 + q, None)
                        if t == 0:
                            ready(sl)
                        for c in range(2):
                            cols = slice(c * 512, c * 512 + 512)
                            k = q * 2 + c
                            mm = exact(acc[:, pair(names[1]), t, :], st_hi[:, k, rows], st_lo[:, k, rows],
                                       w_hi[:, sl.ring(), cols], w_lo[:, sl.ring(), cols], start=k == 0, stop=k == KC - 1)
                        if t == 1:
                            mm.then_inc(weights_used, 1)
                    if t == 0:
                        mm.then_inc(s["tile0_done"], 1)

            def open_bank(name):
                u = BANK[name]
                if u >= 4:
                    pe.wait_ge(bank_read[u % 4], u // 4)
                return misc[:, u % 4, :]

            def filled(ins, name):
                ins.then_inc(bank_full[BANK[name] % 4], 1)

            def keep_awake(b, n):
                for _ in range(n):
                    pe.matmul(b[:, 0:2 * P], ident, const[:, 0:2 * P], start=True, stop=True)

            def turn_rows(tag, count):
                for u in TURN_ORDER:
                    t, j = u // 2, u % 2
                    b = open_bank("%s_%d" % (tag, u))
                    if u == 0:
                        keep_awake(b, 2)
                        if count:
                            pe.wait_ge(s["scaled0"], count - 1)
                            keep_awake(b, 2)
                            pe.wait_ge(s["scaled0"], count)
                            keep_awake(b, 2)
                    if u == 2:
                        keep_awake(b, 2 if count else 5)
                    pe.wait_ge(s["x_ready%d" % t], count + j + 1)
                    for c in range(4):
                        tr = pe.transpose(b[:, c * P:c * P + P], x[:, t, (4 * j + c) * P:(4 * j + c) * P + P], ident)
                    filled(tr, "%s_%d" % (tag, u))

            def half_ready(tag, half):
                await_read(pe, "%s_%d" % (tag, half))
                await_read(pe, "%s_%d" % (tag, 2 + half))

            xt_hi, xt_lo = x_hi[:, :, 0:ROWS], x_lo[:, :, 0:ROWS]
            xm_hi, xm_lo = x_hi[:, :, META:KEYS], x_lo[:, :, META:KEYS]

            pe.wait_ge(s["const_loaded"], 16)
            keep_awake(open_bank("vec"), 4)
            pe.wait_ge(s["vec_loaded"], 16 * len(VEC_ROWS))
            filled(pe.transpose(open_bank("vec")[:, 0:VEC_N], vec_rows[0:VEC_N, :], ident[0:VEC_N, 0:VEC_N]), "vec")
            keep_awake(open_bank("x0_0"), 1)
            pe.wait_ge(s["normed"], 3)

            def turn_x0(half):
                for c in range(4 * half, 4 * half + 4):
                    b = open_bank("x0_%d" % c)
                    cols = slice(c * P, c * P + P)
                    pe.transpose(b[:, 0:META], meta_h[:, cols], ident[0:META, 0:META])
                    for t in range(TILES):
                        tr = pe.transpose(b[:, META + t * P:META + t * P + P], y[:, t, cols], ident)
                    filled(tr, "x0_%d" % c)

            turn_x0(0)
            keep_awake(acc[:, pair("z0"), 0, :], 3)

            def z(lo, hi, meta=True):
                t_stage(lo, hi - lo, lo // 2, x_hi if meta else xm_hi, x_lo if meta else xm_lo)

            for half in range(2):
                def lo_ready():
                    if half == 0:
                        turn_x0(1)
                    for c in range(4 * half, 4 * half + 4):
                        await_read(pe, "x0_%d" % c)

                t_slot_by_parts(Slot(half, half, None), pair("z0"), half, x_hi, x_lo,
                                lambda: pe.wait_ge(s["x0_rounded"], 4 * half + 4), lo_ready)
            z(2, 4, meta=False)
            z(4, 6)
            await_out(pe, "z0")
            filled(pe.matmul(open_bank("ssq_kv")[:, 0:KEYS], ones, sq_kv[:], start=True, stop=True), "ssq_kv")
            await_out(pe, "z1")
            b = open_bank("ssq_cq")
            pe.matmul(b[:, 0:ROWS], ones, sq_cq[:, 0, :], start=True, stop=False)
            filled(pe.matmul(b[:, 0:ROWS], ones, sq_cq[:, 1, :], start=False, stop=True), "ssq_cq")
            z(6, 14)
            z(14, 18, meta=False)
            pe.wait_ge(s["mla_loaded"], 32)
            pe.wait_ge(s["kv_normed"], 1)
            for j in range(4):
                b = open_bank("uq%d" % j)
                for i in range(2):
                    for c in range(2):
                        mm = pe.matmul(b[0:QK, i * ROWS:(i + 1) * ROWS], w_uq[:, c, (2 * j + i) * QK:(2 * j + i + 1) * QK],
                                       cq_z[:, c, :], start=c == 0, stop=c == 1)
                filled(mm, "uq%d" % j)
            wkv = w_ukv[:].rearrange("p (h e) -> p h e", h=HEADS)
            for i in range(HEADS):
                filled(pe.matmul(open_bank("kn%d" % i)[0:NOPE, 0:KEYS], wkv[:, i, 0:NOPE], kv_z[:], start=True, stop=True),
                       "kn%d" % i)
            for i, (lo, n) in enumerate([(0, META), (META, P), (META + P, P)]):
                filled(pe.matmul(open_bank("vt%d" % i)[0:n, :], kv_z[:, lo:lo + n], wkv[:, :, NOPE:NOPE + VD],
                                 start=True, stop=True), "vt%d" % i)
            z(18, 22, meta=False)
            pe.wait_ge(s["pool_loaded"], 64)
            pe.wait_ge(s["pooled_ready"], 1)
            b = open_bank("pool")
            for c in range(2):
                mm = pe.matmul(b[:, c * ROWS:(c + 1) * ROWS], w_pool[:, c, :], pooled[:, c, :], start=True, stop=True)
            filled(mm, "pool")
            z(22, 24, meta=False)
            pe.wait_ge(s["tables_loaded"], 16)
            rope = slice(NOPE, QK)
            filled(pe.matmul(open_bank("krs")[rope, 0:KEYS], cst("swap", ROPE, slice(0, ROPE)), kr_z[0:ROPE, :],
                             start=True, stop=True), "krs")
            filled(pe.matmul(open_bank("krc")[rope, 0:KEYS], ident[0:ROPE, 0:ROPE], kr_z[0:ROPE, :],
                             start=True, stop=True), "krc")
            z(24, 26, meta=False)

            def y_slot(b, i, u_hi, u_lo):
                sl = Slot(FIRST["y_%s%d" % (b, i)], 0, None)
                ready(sl)
                hi = w_hi[:, sl.ring(), :].rearrange("p (c n) -> p c n", c=2)
                lo = w_lo[:, sl.ring(), :].rearrange("p (c n) -> p c n", c=2)
                for q in range(4):
                    name = "y_%s%d" % (b, 2 * i + q // 2)
                    if q % 2 == 0:
                        open_out(name)
                    for c in range(2):
                        cols = slice(q * P, q * P + P)
                        mm = exact(acc[:, pair(name), q % 2, 0:ROWS], hi[:, c, cols], lo[:, c, cols],
                                   u_hi[:, c, :], u_lo[:, c, :], start=c == 0, stop=c == 1)
                    if q == 1:
                        mm.then_inc(s["y_first"], 1)
                mm.then_inc(weights_used, 1)

            t_stage(FIRST["gate_sc"], 8, OUT["gate_sc0"], xm_hi, xm_lo)
            pe.wait_ge(s["sc_split"], 1)
            for h in range(2):
                y_slot("sc", h, u_sc_hi, u_sc_lo)
                t_stage(FIRST["gate_pool%d" % h], 4, OUT["gate_pool%d" % (2 * h)], xm_hi, xm_lo)
                if h == 0:
                    pe.wait_ge(s["conv_done"], 1)
                    b = open_bank("conf_mean")
                    src = conv
                else:
                    pe.wait_ge(s["conf_squared"], 1)
                    b = open_bank("conf_var")
                    src = conf_sq
                pe.matmul(b[:, 0:ROWS], ones, src[:, 0, :], start=True, stop=False)
                filled(pe.matmul(b[:, 0:ROWS], ones, src[:, 1, :], start=False, stop=True), "conf_var" if h else "conf_mean")
            pe.wait_ge(s["pool_split"], 1)
            for h in range(2):
                y_slot("pool", h, u_pool_hi, u_pool_lo)
                t_stage(FIRST["gate_conf%d" % h], 4, OUT["gate_conf%d" % (2 * h)], xm_hi, xm_lo)
            pe.wait_ge(s["conf_split"], 1)

            pe.wait_ge(s["q_roped"], 4)
            pe.wait_ge(s["k_spread"], 1)

            def mla_scores(i):
                b = open_bank("s%d" % i)
                pe.matmul(b[:, 0:S0], qT[0:QK, i, 0:P], kT[0:QK, i, 0:S0], start=True, stop=True)
                filled(pe.matmul(b[:, S0:S0 + S1], qT[0:QK, i, P:ROWS], kT[0:QK, i, :], start=True, stop=True), "s%d" % i)

            def mla_turn(i):
                pe.wait_ge(s["probs_ready"], i + 1)
                pr = probs[:, i % 2, :]
                b = open_bank("pt%d" % i)
                pe.transpose(b[:, 0:P], pr[:, META:S0], ident)
                pe.transpose(b[:, P:2 * P], pr[:, S0 + META:S0 + S0], ident)
                filled(pe.transpose(b[:, 2 * P:3 * P], pr[:, S0 + S0:S0 + S1], ident), "pt%d" % i)
                b = open_bank("pm%d" % i)
                pe.transpose(b[0:META, 0:P], pr[:, 0:META], ident)
                filled(pe.transpose(b[0:META, P:2 * P], pr[:, S0:S0 + META], ident), "pm%d" % i)

            def mla_heads(i):
                name = "heads%d" % (i // 2)
                if i % 2 == 0:
                    open_out(name)
                await_read(pe, "pt%d" % i)
                await_read(pe, "pm%d" % i)
                dst = acc[i % 2 * VD:i % 2 * VD + VD, pair(name), 0, :]
                cols = slice(i * VD, i * VD + VD)
                pe.matmul(dst[:, 0:ROWS], vt[:, 0, cols], metaT[:, i % 2, :], start=True, stop=False)
                pe.matmul(dst[:, 0:ROWS], vt[:, 1, cols], probsT[:, i % 2, 0:ROWS], start=False, stop=False)
                pe.matmul(dst[:, P:ROWS], vt[:, 2, cols], probsT[:, i % 2, ROWS:ROWS + P], start=False,
                          stop=True).then_inc(s["heads_done"], 1)

            for n in range(HEADS + 2):
                if n % 5 == 0:
                    y_slot("conf", n // 5, u_conf_hi, u_conf_lo)
                else:
                    g = n - 1 - n // 5
                    name = "gate_mla%d" % (g // 2)
                    if g % 2 == 0:
                        open_out(name)
                    t_slot(Slot(FIRST["gate_mla%d" % (g // 4)] + g % 4, g % 4, None), pair(name), g % 2, xm_hi, xm_lo,
                           first=g % 2 == 0, last=g % 2 == 1)
                if n < HEADS:
                    mla_scores(n)
                if n >= 2:
                    mla_turn(n - 2)
                if n >= 3:
                    mla_heads(n - 3)
            mla_heads(HEADS - 1)
            for i in range(4):
                open_out("y_mla%d" % i)
                sl = Slot(FIRST["y_mla"] + i, i, None)
                ready(sl)
                hi = w_hi[:, sl.ring(), :].rearrange("p (c n) -> p c n", c=4)
                lo = w_lo[:, sl.ring(), :].rearrange("p (c n) -> p c n", c=4)
                for c in range(4):
                    if i == 0:
                        pe.wait_ge(s["u_mla_split"], c + 1)
                    for b in range(2):
                        cols = slice(b * P, b * P + P)
                        mm = exact(acc[:, pair("y_mla%d" % i), b, 0:ROWS], hi[:, c, cols], lo[:, c, cols],
                                   u_mla_hi[:, c, :], u_mla_lo[:, c, :], start=c == 0, stop=c == 3)
                mm.then_inc(weights_used, 1)
            n_product("w_o", m_hi, m_lo, lambda q: pe.wait_ge(s["m_split"], q + 1))

            t_first(FIRST["gla_gk"], "gla_gk", "x1", 0, halves=1)
            t_stage(FIRST["gla_q"], 4, OUT["gla_q0"], xt_hi, xt_lo)
            pe.wait_ge(s["gk_loaded"], 32)
            await_out(pe, "gla_gk")
            for j in range(2):
                b = open_bank("la%d" % j)
                for i in range(2):
                    c = 2 * j + i
                    mm = pe.matmul(b[:, i * ROWS:(i + 1) * ROWS], w_gk[0:16, c * DK:(c + 1) * DK], gk_low[0:16, :],
                                   start=True, stop=True)
                filled(mm, "la%d" % j)
            t_stage(FIRST["gla_k"], 4, OUT["gla_k0"], xt_hi, xt_lo)
            n_slots("gla_v", ["gla_v0", "gla_v1"], xt_hi, xt_lo)
            pe.wait_ge(s["qd_ready"], 1)
            pe.wait_ge(s["ki_ready"], 1)
            for j in range(2):
                b = open_bank("sg%d" % j)
                for i in range(4):
                    hd, t = 2 * j + i // 2, i % 2
                    rows = slice(t * P, t * P + P)
                    mm = pe.matmul(b[:, i * P:(i + 1) * P], ki[:, hd, rows], qd[:, hd, rows], start=True, stop=True)
                filled(mm, "sg%d" % j)
            pe.wait_ge(s["ke_ready"], 1)
            for j in range(2):
                b = open_bank("ke%d" % j)
                for i in range(4):
                    hd, t = 2 * j + i // 2, i % 2
                    tr = pe.transpose(b[:, i * P:(i + 1) * P], ke[:, hd, t * P:t * P + P], ident)
                filled(tr, "ke%d" % j)
            n_slots("gla_g", ["gla_g0", "gla_g1"], xt_hi, xt_lo, 0, 2)
            await_read(pe, "ke0")
            await_read(pe, "ke1")
            await_out(pe, "gla_v0")
            await_out(pe, "gla_v1")
            for hd in range(GLA_H):
                for half, chunks in (("a", (0, 1)), ("b", (2,))):
                    b = open_bank("upd%d%s" % (hd, half))
                    for n in chunks:
                        mm = pe.matmul(b[:, n % 2 * DV:n % 2 * DV + DV], ke_half[:, n % 2, hd * TILES + n // 2, :],
                                       gv[:, n // 2, hd * DV:(hd + 1) * DV], start=True, stop=True)
                    filled(mm, "upd%d%s" % (hd, half))
            n_slots("gla_g", ["gla_g0", "gla_g1"], xt_hi, xt_lo, 2, 4)
            pe.wait_ge(s["intra_ready"], 2)
            pe.wait_ge(s["half_ready"], 2)
            for hd in range(GLA_H - 2, GLA_H):
                await_read(pe, "upd%da" % hd)
                await_read(pe, "upd%db" % hd)
            for j in range(4):
                b = open_bank("o%d" % j)
                t = j // 2
                for i in range(2):
                    hd = j % 2 * 2 + i
                    dst = b[:, i * DV:(i + 1) * DV]
                    rows = slice(t * P, t * P + P)
                    pe.matmul(dst, intra[:, hd * TILES + t, :], gv[:, t, hd * DV:(hd + 1) * DV], start=True, stop=False)
                    if t == 1:
                        pe.matmul(dst, qd_half[:, 0, hd, rows], state[:, hd, 1, :], start=False, stop=False)
                    mm = pe.matmul(dst, qd_half[:, 1, hd, rows], state[:, hd, 2 * t, :], start=False, stop=True)
                filled(mm, "o%d" % j)
            n_slots("gla_g", ["gla_g0", "gla_g1"], xt_hi, xt_lo, 4, 7)

            def turn_gated(hf):
                for j in (2 * hf, 2 * hf + 1):
                    if hf == 0:
                        await_read(pe, "o0")
                        await_read(pe, "o2")
                    else:
                        pe.wait_ge(s["o_gated"], j - 1)
                    b = open_bank("ot%d" % j)
                    for c in range(2):
                        for t in range(TILES):
                            tr = pe.transpose(b[:, c * ROWS + t * P:c * ROWS + t * P + P],
                                              gg[:, t, (2 * j + c) * P:(2 * j + c) * P + P], ident)
                    filled(tr, "ot%d" % j)

            turn_gated(0)
            n_slots("gla_g", ["gla_g0", "gla_g1"], xt_hi, xt_lo, 7, 8)

            def gated_ready(q):
                if q == 1:
                    turn_gated(1)
                await_read(pe, "ot%d" % q)

            n_product("gla_out", o_hi, o_lo, gated_ready)

            def swiglu(layer):
                tag = "gu%d" % layer
                t_first(FIRST[tag], tag + "_0", "x2" if layer == 0 else "x4", 2 + 4 * layer)
                t_stage(FIRST[tag] + 2, COUNT[tag] - 2, OUT[tag + "_1"], xt_hi, xt_lo, body=2 * RING)
                tag = "down%d" % layer
                names = [tag + "_0", tag + "_1"]

                def down_half(k, t, hf):
                    sl = Slot(FIRST[tag] + k, k, None)
                    rows, cols = slice(t * P, t * P + P), slice(hf * 512, hf * 512 + 512)
                    return exact(acc[:, pair(names[hf]), t, :], h_hi[:, k, rows], h_lo[:, k, rows],
                                 w_hi[:, sl.ring(), cols], w_lo[:, sl.ring(), cols], start=k == 0, stop=k == FCH - 1)

                def down_ready(k):
                    if k % 2 == 0:
                        pe.wait_ge(s["h_split"], layer * FCH // 2 + k // 2 + 1)
                    ready(Slot(FIRST[tag] + k, k, None))

                for k in range(FCH - RING):
                    down_ready(k)
                    for hf in range(2):
                        if k == 0:
                            open_out(names[hf])
                        for t in range(TILES):
                            mm = down_half(k, t, hf)
                    mm.then_inc(weights_used, 1)
                for k in range(FCH - RING, FCH):
                    down_ready(k)
                    for hf in range(2):
                        mm = down_half(k, 0, hf)
                        if k == FCH - 1:
                            mm.then_inc(s["down_part"], 1)
                for hf in range(2):
                    for k in range(FCH - RING, FCH):
                        mm = down_half(k, 1, hf)
                        if hf == 1:
                            mm.then_inc(weights_used, 1)
                    if hf == 0:
                        mm.then_inc(s["down_part"], 1)

            swiglu(0)

            t_first(FIRST["moba_q"], "moba_q0", "x3", 4)
            t_stage(FIRST["moba_q"] + 2, 6, OUT["moba_q1"], xt_hi, xt_lo)
            t_stage(FIRST["moba_k"], 8, OUT["moba_k0"], xt_hi, xt_lo)

            def moba_scores(i):
                b = open_bank("ms%d" % i)
                pe.matmul(b[:, 0:P], mq[:, i, 0:P], mk[:, i, 0:P], start=True, stop=True)
                filled(pe.matmul(b[:, P:P + ROWS], mq[:, i, P:ROWS], mk[:, i, :], start=True, stop=True), "ms%d" % i)

            def moba_turn(i):
                pe.wait_ge(s["m_probs"], i + 1)
                b = open_bank("mt%d" % i)
                for c in range(3):
                    tr = pe.transpose(b[:, c * P:(c + 1) * P], mprobs[:, i % 2, c * P:(c + 1) * P], ident)
                filled(tr, "mt%d" % i)

            def moba_pv(i):
                name = "moba_heads%d" % (i // 4)
                if i % 4 == 0:
                    await_out(pe, "moba_v%d" % (i // 4))
                    open_out(name)
                await_read(pe, "mt%d" % i)
                dst = acc[:, pair(name), i % 4 // 2, i % 2 * ROWS:(i % 2 + 1) * ROWS]
                cols = slice(i * HD, (i + 1) * HD)
                pe.matmul(dst[:, 0:ROWS], mv[:, 0, cols], mprobsT[:, i, 0:ROWS], start=True, stop=False)
                pe.matmul(dst[:, P:ROWS], mv[:, 1, cols], mprobsT[:, i, ROWS:ROWS + P], start=False,
                          stop=True).then_inc(s["m_heads_done"], 1)

            for i in range(HEADS):
                n_slots("moba_v", ["moba_v0", "moba_v1"], xt_hi, xt_lo, i, i + 1)
                if i % 2 == 0:
                    by, n = ("", i // 2 + 1) if i < 4 else ("_pool", i // 2 - 1)
                    pe.wait_ge(s["mq_roped" + by], n)
                    pe.wait_ge(s["mk_roped" + by], n)
                moba_scores(i)
                if i >= 2:
                    moba_turn(i - 2)
                if i in (5, 6):
                    moba_pv(2 * i - 10)
                    moba_pv(2 * i - 9)
            moba_turn(HEADS - 2)

            def heads_ready(q):
                if q == 1:
                    moba_turn(HEADS - 1)
                if q in (1, 2):
                    moba_pv(2 * q + 2)
                    moba_pv(2 * q + 3)
                if q % 2 == 0:
                    pe.wait_ge(s["mo_split"], q // 2 + 1)
                else:
                    await_out(pe, "moba_heads%d" % (q // 2))

            n_product("moba_out", mo_hi, mo_lo, heads_ready)
            swiglu(1)

        @block.scalar
        def _(act):
            chained = [0]

            def link(ins):
                chained[0] += 1
                ins.then_inc(act_chain, 1)
                act.wait_ge(act_chain, chained[0])

            def round_slot(sl, ahead):
                k = sl.ring(ahead)
                act.wait_ge(landed[k], (sl.uses(ahead) + 1) * 16)
                if sl.loop is not None or sl.at + ahead >= RING:
                    act.wait_ge(weights_used, sl.number(ahead + 1 - RING))
                nc.scalar.copy(w_hi[:, k, :], staged[:, k, :]).then_inc(rounded, 1)

            def lead(sl):
                if sl.loop is not None or sl.at + LEAD < TOTAL:
                    round_slot(sl, LEAD)

            def copy_out(dst, src, name, func=ACT.Copy, **kw):
                nc.scalar.activation(dst, src, func, **kw).then_inc(evacuated[OUT[name] % 2], 1)

            def out_t(name, n=ROWS, lo=0):
                return acc[:, pair(name), :, lo:lo + n]

            def halves(dst, i):
                return dst[:, 2 * i:2 * i + 2, :]

            act.wait_ge(s["x_loaded"], 16)
            act.wait_ge(s["cleared"], 1)
            nc.scalar.activation(y[:, 0, :], x[:, 0, :], ACT.Square, accum_out=ssq[:, 0:1])
            act.wait_ge(s["meta_loaded"], 16)
            nc.scalar.activation(meta_h, m_rows, ACT.Square, accum_out=ssq[0:META, 1:2]).then_inc(s["ssq0"], 1)
            act.wait_ge(s["rstd0"], 1)
            nc.scalar.activation(y[:, 0, :], x[:, 0, :], ACT.Copy, scale=rs[:, 1, 0:1]).then_inc(s["normed"], 1)
            round_slot(Slot(0, 0, None), 0)
            await_read(act, "vec")
            for c in range(KC):
                if c == KC // 2:
                    round_slot(Slot(1, 1, None), 0)
                await_full(act, "x0_%d" % c)
                nc.scalar.activation(x_hi[:, c, :], bank("x0_%d" % c)[:, 0:KEYS], ACT.Copy,
                                     scale=col("pre_norm_g", c)).then_inc(s["x0_rounded"], 1)
            round_slot(Slot(2, 2, None), 0)

            for sl in over_slots(act, 0, COUNT["z"], loops=0):
                lead(sl)
                if sl.at % 2 == 0:
                    continue
                name = "z%d" % (sl.at // 2)
                what = Z_BLOCKS[sl.at // 2][0]
                slot_done(act, "z", sl.at)
                if what == "ckv_kr":
                    nc.scalar.copy(kv_z[:], acc[:, pair(name), 0, 0:KEYS])
                    nc.scalar.copy(kr_z[0:ROPE, :], acc[0:ROPE, pair(name), 1, 0:KEYS])
                    copy_out(sq_kv[:], acc[:, pair(name), 0, 0:KEYS], name, ACT.Square)
                elif what == "cq":
                    nc.scalar.copy(cq_z[:], out_t(name))
                    copy_out(sq_cq[:], out_t(name), name, ACT.Square)
                elif what in ("pool_v", "conf_a", "sc_c", "sc_x"):
                    dst = {"pool_v": pool_v, "conf_a": glu, "sc_c": sc_c, "sc_x": sc_x}[what]
                    copy_out(dst[:], out_t(name, KEYS), name)
                elif what == "conf_g":
                    copy_out(glu_g[:], out_t(name, KEYS), name, ACT.Sigmoid)
                elif what == "sc_b":
                    copy_out(sc_b[:], out_t(name), name)
                else:
                    dst = {"sc_gate": sc_gate[:], "pool_gate": pool_gate[:], "conf_gate": conf_gate[:],
                           "mla_gate0": halves(mla_gate, 0), "mla_gate1": halves(mla_gate, 1)}[what]
                    copy_out(dst, out_t(name), name, ACT.Silu)
                if what == "sc_gate":
                    act.wait_ge(s["trig_args"], 1)
                    act.wait_ge(s["cleared"], 3)
                    nc.scalar.activation(trig[0:ROPE, 0, :], trig_abs, ACT.Sin, bias=half_pi[0:ROPE, :], scale=-1.0)
                    nc.scalar.activation(trig[0:ROPE, 1, :], trig_r, ACT.Sin,
                                         scale=cst("sign", 1, slice(0, ROPE))).then_inc(s["trig_ready"], 1)
                    for j in range(4):
                        await_full(act, "uq%d" % j)
                        nc.scalar.copy(qT[0:QK, 2 * j:2 * j + 2, :], bank("uq%d" % j)[0:QK, :]
                                       .rearrange("p (h r) -> p h r", h=2)).then_inc(read_sem("uq%d" % j), 1)
                    for i in range(HEADS):
                        await_full(act, "kn%d" % i)
                        nc.scalar.copy(kT[0:NOPE, i, :], bank("kn%d" % i)[0:NOPE, 0:KEYS]).then_inc(read_sem("kn%d" % i), 1)
                    act.wait_ge(s["cleared"], 4)
                    for i, n in enumerate((META, P, P)):
                        await_full(act, "vt%d" % i)
                        nc.scalar.copy(vt[0:n, i, :], bank("vt%d" % i)[0:n, :]).then_inc(read_sem("vt%d" % i), 1)
                if sl.at == 23:
                    act.wait_ge(s["sc_u"], 1)
                    nc.scalar.copy(u_sc_hi[:], sc_acc[:]).then_inc(s["sc_rounded"], 1)
                if sl.at == 25:
                    await_read(act, "pool")
                    nc.scalar.copy(u_pool_hi[:], pool_gate[:]).then_inc(s["pool_rounded"], 1)

            def gate_bias(b, c):
                return col("gate_bias", BRANCH[b] * KC + c)

            def take_gates(b, before, i):
                name = "gate_%s%d" % (b, i)
                if before:
                    await_out(act, "y_%s%d" % (before, i))
                nc.scalar.activation(gates[:, 2 * i, :], acc[:, pair(name), 0, 0:ROWS], ACT.Sigmoid,
                                     bias=gate_bias(b, 2 * i))
                copy_out(gates[:, 2 * i + 1, :], acc[:, pair(name), 1, 0:ROWS], name, ACT.Sigmoid,
                         bias=gate_bias(b, 2 * i + 1))

            for sl in over_slots(act, FIRST["gate_sc"], 8, loops=0):
                lead(sl)
                if sl.index % 2 == 1:
                    slot_done(act, "gate_sc", sl.index)
                    take_gates("sc", None, sl.index // 2)
            for before, b in (("sc", "pool"), ("pool", "conf")):
                for h in range(2):
                    lead(Slot(FIRST["y_%s%d" % (before, h)], 0, None))
                    stage = "gate_%s%d" % (b, h)
                    for sl in over_slots(act, FIRST[stage], 4, loops=0):
                        lead(sl)
                        if sl.index % 2 == 1:
                            slot_done(act, stage, sl.index)
                            take_gates(b, before, 2 * h + sl.index // 2)
                        if stage == "gate_pool1" and sl.index == 1:
                            await_read(act, "conf_mean")
                            nc.scalar.square(conf_sq[:], conv[:]).then_inc(s["conf_squared"], 1)
                        if stage == "gate_conf0" and sl.index == 3:
                            act.wait_ge(s["conf_zn"], 1)
                            nc.scalar.activation(conf_sq[:, 0, :], conv[:, 0, :], ACT.Sigmoid, bias=col("conf_ln_b", 0))
                            nc.scalar.activation(conf_sq[:, 1, :], conv[:, 1, :], ACT.Sigmoid,
                                                 bias=col("conf_ln_b", 1)).then_inc(s["conf_sig"], 1)
                        if stage == "gate_conf1" and sl.index == 1:
                            act.wait_ge(s["conf_u"], 1)
                            nc.scalar.copy(u_conf_hi[:], conv[:]).then_inc(s["conf_rounded"], 1)

            def mla_probsT(i):
                await_full(act, "pt%d" % i)
                nc.scalar.copy(probsT[:, i % 2, :], bank("pt%d" % i)[:, 0:3 * P]).then_inc(read_sem("pt%d" % i), 1)
                await_full(act, "pm%d" % i)
                nc.scalar.copy(metaT[0:META, i % 2, :], bank("pm%d" % i)[0:META, 0:ROWS]).then_inc(read_sem("pm%d" % i), 1)

            def mla_u_hi(i):
                await_out(act, "heads%d" % i)
                nc.scalar.copy(u_mla_hi[:, i, :], u_mla[:, i, :]).then_inc(s["u_mla_rounded"], 1)

            act.wait_ge(s["meta_cleared"], 1)
            for n in range(HEADS + 2):
                g = n - 1 - n // 5
                lead(Slot(FIRST["y_conf0"] + n, n, None))
                if n == HEADS:
                    for b in (1, 2):
                        await_out(act, "gate_mla%d" % b)
                    for b in range(3):
                        nc.scalar.activation(halves(gates, b), halves(gates, b), ACT.Sigmoid).then_inc(s["mla_gates"], 1)
                if n % 5 and g % 2 == 1:
                    b, name = g // 2, "gate_mla%d" % (g // 2)
                    slot_done(act, "gate_mla%d" % (g // 4), g % 4)
                    await_out(act, "y_conf%d" % b)
                    func = ACT.Identity if b < 3 else ACT.Sigmoid
                    nc.scalar.activation(gates[:, 2 * b, :], acc[:, pair(name), 0, 0:ROWS], func, bias=gate_bias("mla", 2 * b))
                    copy_out(gates[:, 2 * b + 1, :], acc[:, pair(name), 1, 0:ROWS], name, func,
                             bias=gate_bias("mla", 2 * b + 1))
                if n >= 2:
                    mla_probsT(n - 2)
                if n < HEADS:
                    act.wait_ge(s["max_ready"], n + 1)
                    nc.scalar.activation(probs[:, n % 2, 0:S0], scores[:, n % 2, 0:S0], ACT.Exp, bias=neg_max[:, n % 2, 0:1],
                                         accum_out=sums[:, n % 2, 0:1])
                    nc.scalar.activation(probs[:, n % 2, S0:], scores[:, n % 2, S0:], ACT.Exp, bias=neg_max[:, n % 2, 1:2],
                                         accum_out=sums[:, n % 2, 1:2]).then_inc(s["exp_done"], 1)
                if n in (6, 8):
                    mla_u_hi((n - 6) // 2)
            mla_u_hi(2)
            mla_u_hi(3)
            for i in range(4):
                lead(Slot(FIRST["y_mla"] + i, i, None))
                act.wait_ge(s["m_ready"], i + 1)
                nc.scalar.copy(halves(m_hi, i), halves(m, i)).then_inc(s["m_rounded"], 1)
            junk = m[:].rearrange("p c r -> p (c r)")
            def squares(t, hf):
                k = 2 * t + hf
                return nc.scalar.activation(junk[:, k * 512:(k + 1) * 512], acc[:, pair("w_o%d" % hf), t, :], ACT.Square,
                                            accum_out=ssq[:, k:k + 1])

            for sl in over_slots(act, FIRST["w_o"], 8, loops=0):
                lead(sl)
                if sl.index == 3:
                    slot_done(act, "w_o", 3)
                    act.wait_ge(s["m_split"], 4)
                    squares(0, 0)
                    squares(1, 0).then_inc(s["wo_ssq"], 1)
                if sl.index == 4:
                    act.wait_ge(s["tile0_done"], TAILS["w_o"])
                    squares(0, 1).then_inc(s["wo_ssq"], 1)
            slot_done(act, "w_o", 7)
            squares(1, 1).then_inc(s["wo_ssq"], 1)

            def scale_tile0(k):
                act.wait_ge(s["rstd_tile0"], k + 1)
                for hf in range(2):
                    cols = slice(hf * 512, hf * 512 + 512)
                    nc.scalar.activation(y[:, 0, cols], y[:, 0, cols], ACT.Identity, bias=rs[:, 2, 0:1],
                                         scale=rs[:, 1, 0:1]).then_inc(s["scaled0"], 1)

            def round_rows(tag):
                for u in TURN_ORDER:
                    t, j = u // 2, u % 2
                    await_full(act, "%s_%d" % (tag, u))
                    nc.scalar.copy(x_hi[:, 4 * j:4 * j + 4, t * P:t * P + P], bank("%s_%d" % (tag, u))
                                   .rearrange("p (c r) -> p c r", c=4)).then_inc(s["x_rounded"], 1)

            round_rows("x1")
            for sl in over_slots(act, FIRST["gla_gk"], 2):
                lead(sl)
            slot_done(act, "gla_gk", 1)
            copy_out(gk_low[0:16, :], acc[0:16, pair("gla_gk"), 0, 0:ROWS], "gla_gk")
            for sl in over_slots(act, FIRST["gla_q"], 4, loops=0):
                lead(sl)
                if sl.index % 2 == 1:
                    slot_done(act, "gla_q", sl.index)
                    name = "gla_q%d" % (sl.index // 2)
                    copy_out(halves(gq, sl.index // 2), out_t(name), name, scale=float(DK) ** -0.5)
            for sl in over_slots(act, FIRST["gla_k"], 4, loops=0):
                lead(sl)
                if sl.index == 0:
                    for j in range(2):
                        await_full(act, "la%d" % j)
                        for i in range(2):
                            c = 2 * j + i
                            ab = nc.scalar.activation(la_e[:, c, :], bank("la%d" % j)[:, i * ROWS:(i + 1) * ROWS], ACT.Abs,
                                                      bias=col("gla_b_gk_2", c))
                        ab.then_inc(s["la_abs"], 1)
                    act.wait_ge(s["la_abs"], 2)
                    link(nc.scalar.activation(la_e[:], la_e[:], ACT.Exp, scale=-1.0))
                    nc.scalar.activation(la_e[:], la_e[:], ACT.Ln, bias=1.0).then_inc(s["la_log"], 1)
                if sl.index % 2 == 1:
                    slot_done(act, "gla_k", sl.index)
                    name = "gla_k%d" % (sl.index // 2)
                    copy_out(halves(gk, sl.index // 2), out_t(name), name)
                if sl.index == 2:
                    act.wait_ge(s["cum_ready"], 1)
                    nc.scalar.activation(e_cum[:], la_e[:], ACT.Exp, scale=1.0 / 16.0).then_inc(s["e_ready"], 1)
                    nc.scalar.activation(e_inv[:], la_e[:], ACT.Exp, scale=-1.0 / 16.0).then_inc(s["e_ready"], 1)
                    act.wait_ge(s["end_ready"], 1)
                    nc.scalar.activation(e_end[:], la[:], ACT.Exp, scale=1.0 / 16.0).then_inc(s["e_ready"], 1)
            for sl in over_slots(act, FIRST["gla_v"], 8, loops=0):
                lead(sl)
                if sl.index % 4 == 3:
                    hf = sl.index // 4
                    slot_done(act, "gla_v", sl.index)
                    copy_out(gv[:, :, hf * 512:(hf + 1) * 512], acc[:, pair("gla_v%d" % hf), :, :], "gla_v%d" % hf)
            def round_gated(hf):
                for j in (2 * hf, 2 * hf + 1):
                    await_full(act, "ot%d" % j)
                    nc.scalar.copy(halves(o_hi, j), bank("ot%d" % j).rearrange("p (c r) -> p c r", c=2)).then_inc(s["o_rounded"], 1)

            for sl in over_slots(act, FIRST["gla_g"], 8, loops=0):
                lead(sl)
                if sl.index == 0:
                    act.wait_ge(s["zeroed"], 4)
                    for j in range(2):
                        await_full(act, "sg%d" % j)
                        b = bank("sg%d" % j).rearrange("p (g r) -> p g r", g=4)
                        nc.scalar.copy(intra[0:CH, 4 * j:4 * j + 4, 0:CH], b[0:CH, :, 0:CH])
                        nc.scalar.copy(intra[CH:P, 4 * j:4 * j + 4, CH:P], b[CH:P, :, CH:P]).then_inc(read_sem("sg%d" % j), 1)
                    for j in range(2):
                        await_full(act, "ke%d" % j)
                        b = bank("ke%d" % j).rearrange("p (g r) -> p g r", g=4)
                        nc.scalar.copy(ke_half[0:CH, 0, 4 * j:4 * j + 4, :], b[0:CH])
                        nc.scalar.copy(ke_half[CH:P, 1, 4 * j:4 * j + 4, :], b[CH:P]).then_inc(read_sem("ke%d" % j), 1)
                if sl.index == 4:
                    junk1 = e_inv[:].rearrange("p h r -> p (h r)")
                    junk2 = e_end[:].rearrange("p h r -> p (h r)")
                    for j in range(4):
                        await_full(act, "o%d" % j)
                        for i in range(2):
                            k = 2 * j + i
                            dst = (junk1 if k < 4 else junk2)[:, k % 4 * DV:(k % 4 + 1) * DV]
                            nc.scalar.activation(dst, bank("o%d" % j)[:, i * DV:(i + 1) * DV], ACT.Square,
                                                 accum_out=ssq[:, k:k + 1]).then_inc(s["o_ssq"], 1)
                if sl.index == 7:
                    round_gated(0)
                if sl.index % 4 == 3:
                    hf = sl.index // 4
                    slot_done(act, "gla_g", sl.index)
                    if hf == 0:
                        copy_out(gg[:, :, 0:512], acc[:, pair("gla_g0"), :, :], "gla_g0", ACT.Silu)
                    else:
                        nc.scalar.activation(gg[:, :, 512:768], acc[:, pair("gla_g1"), :, 0:256], ACT.Silu).then_inc(s["gg1_ready"], 1)
                        copy_out(gg[:, :, 768:1024], acc[:, pair("gla_g1"), :, 256:512], "gla_g1", ACT.Silu)
            for sl in over_slots(act, FIRST["gla_out"], 8, loops=0):
                lead(sl)
                if sl.index == 1:
                    round_gated(1)

            def swiglu(layer):
                tag = "gu%d" % layer
                for sl in over_slots(act, FIRST[tag], COUNT[tag]):
                    lead(sl)
                    og = OUT[tag + "_0"]
                    if sl.index == 1:
                        act.wait_ge(weights_used, sl.number(1))
                        nc.scalar.activation(h_gate[:], acc[:, og % 2, :, 0:ROWS], ACT.Silu).then_inc(evacuated[og % 2], 1)
                    if sl.index == 3:
                        act.wait_ge(evacuated[(og + 1) % 2], sl.loop + ((og + 1) // 2 + 1))
                        nc.scalar.copy(h_hi[:, bass.ds(sl.loop * 2, 2), :], hidden[:]).then_inc(s["h_rounded"], 1)
                tag = "down%d" % layer
                for sl in over_slots(act, FIRST[tag], COUNT[tag], loops=4):
                    lead(sl)

            scale_tile0(0)
            round_rows("x2")
            swiglu(0)
            scale_tile0(1)
            round_rows("x3")
            for tag, dst in (("moba_q", mq), ("moba_k", mk)):
                for sl in over_slots(act, FIRST[tag], 8, loops=0):
                    lead(sl)
                    if sl.index % 2 == 1:
                        slot_done(act, tag, sl.index)
                        name = "%s%d" % (tag, sl.index // 2)
                        copy_out(halves(dst, sl.index // 2), out_t(name), name)

            def moba_probsT(i):
                await_full(act, "mt%d" % i)
                nc.scalar.copy(mprobsT[:, i, :], bank("mt%d" % i)[:, 0:P + ROWS]).then_inc(read_sem("mt%d" % i), 1)

            def moba_exp(i):
                act.wait_ge(s["m_max"], i + 1)
                nc.scalar.activation(mprobs[:, i % 2, 0:P], mscores[:, i % 2, 0:P], ACT.Exp, bias=neg_max[:, i % 2, 0:1],
                                     accum_out=sums[:, i % 2, 0:1])
                nc.scalar.activation(mprobs[:, i % 2, P:], mscores[:, i % 2, P:], ACT.Exp, bias=neg_max[:, i % 2, 1:2],
                                     accum_out=sums[:, i % 2, 1:2]).then_inc(s["m_exp"], 1)

            def moba_v_out(hf):
                slot_done(act, "moba_v", 4 * hf + 3)
                copy_out(mv[:, :, hf * 512:(hf + 1) * 512], acc[:, pair("moba_v%d" % hf), :, :], "moba_v%d" % hf)

            def moba_round(i):
                act.wait_ge(s["m_heads_done"], 2 * i + 2)
                nc.scalar.copy(halves(mo_hi, i), acc[:, pair("moba_heads%d" % (i // 2)), i % 2, :]
                               .rearrange("p (h r) -> p h r", h=2)).then_inc(s["mo_rounded"], 1)

            for i in range(HEADS):
                lead(Slot(FIRST["moba_v"] + i, i, None))
                if i == HEADS - 1:
                    moba_round(0)
                    moba_round(1)
                if i >= 2:
                    moba_probsT(i - 2)
                moba_exp(i)
                if i % 4 == 3:
                    moba_v_out(i // 4)
            moba_probsT(HEADS - 2)
            for i in range(8):
                lead(Slot(FIRST["moba_out"] + i, i, None))
                if i == 0:
                    moba_probsT(HEADS - 1)
                    moba_round(2)
                if i == 1:
                    moba_round(3)
            scale_tile0(2)
            round_rows("x4")
            swiglu(1)
            scale_tile0(3)

        @block.vector
        def _(dve):
            chained = [0]

            def count(ins):
                chained[0] += 1
                ins.then_inc(dve_chain, 1)
                return chained[0]

            def link(ins):
                dve.wait_ge(dve_chain, count(ins))

            def split_slot(sl, ahead):
                k = sl.ring(ahead)
                dve.wait_ge(rounded, sl.number(ahead + 1))
                nc.vector.tensor_tensor(w_lo[:, k, :], staged[:, k, :], w_hi[:, k, :].bitcast(F32),
                                        ALU.subtract).then_inc(split, 1)

            def lead(sl):
                if sl.loop is not None or sl.at + LEAD < TOTAL:
                    split_slot(sl, LEAD)

            def rest(dst, src, hi):
                return nc.vector.tensor_tensor(dst, src, hi.bitcast(F32), ALU.subtract)

            def newton(v, r, t, steps=range(3)):
                if 0 in steps:
                    link(nc.vector.tensor_scalar(r.bitcast(I32), v.bitcast(I32), 1, None, ALU.logical_shift_right))
                    link(nc.vector.tensor_scalar(r.bitcast(I32), r.bitcast(I32), -1.0, float(0x5F3759DF), ALU.mult, ALU.add))
                for step in steps:
                    link(nc.vector.tensor_tensor(t, r, r, ALU.mult))
                    link(nc.vector.scalar_tensor_tensor(t, t, -0.5, v, ALU.mult, ALU.mult))
                    last = nc.vector.scalar_tensor_tensor(r, t, 1.5, r, ALU.add, ALU.mult)
                    if step < steps[-1]:
                        link(last)
                return last

            def newton_col(v, r, t, beside):
                n = count(nc.vector.tensor_scalar(r.bitcast(I32), v.bitcast(I32), 1, None, ALU.logical_shift_right))
                beside(0)
                dve.wait_ge(dve_chain, n)
                n = count(nc.vector.tensor_scalar(r.bitcast(I32), r.bitcast(I32), -1.0, float(0x5F3759DF), ALU.mult, ALU.add))
                beside(1)
                dve.wait_ge(dve_chain, n)
                for step, three in enumerate((3.0, 12.0, 768.0)):
                    n = count(nc.vector.scalar_tensor_tensor(t, r, v, r, ALU.mult, ALU.mult))
                    if step == 0:
                        beside(2)
                    dve.wait_ge(dve_chain, n)
                    n = count(nc.vector.scalar_tensor_tensor(r, t, -three, r, ALU.add, ALU.mult))
                    if step == 0:
                        beside(3)
                    dve.wait_ge(dve_chain, n)
                link(nc.vector.tensor_scalar(r, r, -1.0 / 8192, None, ALU.mult))

            def handed_back(stage):
                dve.wait_ge(split, FIRST[stage] + LEAD)

            def mean_eps(dst, src, n, eps):
                return nc.vector.tensor_scalar(dst, src, 1.0 / n, eps, ALU.mult, ALU.add)

            def halves(dst, i):
                return dst[:, 2 * i:2 * i + 2, :]

            def out_t(name):
                return acc[:, pair(name), :, 0:ROWS]

            def taken(ins, name):
                ins.then_inc(evacuated[pair(name)], 1)

            def read(ins, name):
                ins.then_inc(read_sem(name), 1)

            dve.wait_ge(s["x1_loaded"], 16)
            for hf in range(2):
                last = nc.vector.bn_stats(stats[:, 1, hf, :], x[:, 1, hf * 512:hf * 512 + 512])
            link(last)
            link(nc.vector.bn_aggr(mu_var[:, 1, :], stats[:, 1].rearrange("p h e -> p (h e)")))
            link(nc.vector.scalar_tensor_tensor(rs[:, 0, 2:3], mu_var[:, 1, 0:1], mu_var[:, 1, 0:1], mu_var[:, 1, 1:2],
                                                ALU.mult, ALU.add))
            nc.vector.tensor_scalar(rs[:, 0, 2:3], rs[:, 0, 2:3], EPS, None, ALU.add)
            dve.wait_ge(s["ssq0"], 1)
            link(mean_eps(rs[:, 0, 0:2], ssq[:, 0:2], DM, EPS))
            newton(rs[:, 0, 0:3], rs[:, 1, 0:3], rs[:, 2, 0:3]).then_inc(s["rstd0"], 1)
            dve.wait_ge(s["rstd0"], 1)
            nc.vector.tensor_scalar(y[:, 1, :], x[:, 1, :], rs[:, 1, 2:3], None, ALU.mult).then_inc(s["normed"], 1)
            nc.vector.tensor_scalar(meta_h, m_rows, rs[0:META, 1, 1:2], None, ALU.mult).then_inc(s["normed"], 1)
            await_full(dve, "vec")
            read(nc.vector.tensor_copy(vec[:, 0:VEC_N], bank("vec")[:, 0:VEC_N]), "vec")
            await_read(dve, "vec")
            for c in range(KC):
                if c % 4 == 0:
                    split_slot(Slot(c // 4, c // 4, None), 0)
                dve.wait_ge(s["x0_rounded"], c + 1)
                read(nc.vector.scalar_tensor_tensor(x_lo[:, c, :], bank("x0_%d" % c)[:, 0:KEYS], col("pre_norm_g", c),
                                                    x_hi[:, c, :].bitcast(F32), ALU.mult, ALU.subtract), "x0_%d" % c)
            split_slot(Slot(2, 2, None), 0)

            def trig_multiple():
                dve.wait_ge(s["pos_loaded"], 16)
                dve.wait_ge(s["tables_loaded"], 16)
                link(nc.vector.tensor_scalar(trig_r, pos_i, cst("inv_freq", 1, slice(0, ROPE)), None, ALU.mult))
                magic = 1.5 * 2.0 ** 23
                link(nc.vector.tensor_scalar(trig_k, trig_r, float(1 / (2 * np.pi)), magic, ALU.mult, ALU.add))
                link(nc.vector.tensor_scalar(trig_k, trig_k, -magic, None, ALU.add))
                link(nc.vector.tensor_scalar(trig_kh, trig_k, 1.0 / 2048, magic, ALU.mult, ALU.add))
                link(nc.vector.tensor_scalar(trig_kh, trig_kh, -magic, 2048.0, ALU.add, ALU.mult))
                link(nc.vector.tensor_tensor(trig_k, trig_k, trig_kh, ALU.subtract))

            def trig_reduce(of):
                rest_2pi, parts = 2 * np.pi, []
                for bits in (11, 11, 11):
                    e = np.floor(np.log2(rest_2pi))
                    unit = 2.0 ** (e - bits + 1)
                    parts.append(np.floor(rest_2pi / unit) * unit)
                    rest_2pi -= parts[-1]
                parts = (parts + [rest_2pi])[of]
                for part in parts:
                    for k in (trig_kh, trig_k):
                        link(nc.vector.scalar_tensor_tensor(trig_r, k, -float(part), trig_r, ALU.mult, ALU.add))
                if of.stop is not None:
                    return
                link(nc.vector.tensor_scalar(trig_r, trig_r, 3.1415925, -3.1415925, ALU.min, ALU.max))
                nc.vector.scalar_tensor_tensor(trig_abs, trig_r, -1.0, trig_r, ALU.mult, ALU.max).then_inc(s["trig_args"], 1)

            def kvq_norm(step):
                v, r, t = kvq_rs
                if step == 0:
                    await_full(dve, "ssq_kv")
                    read(mean_eps(v[:, 0:KEYS], bank("ssq_kv")[:, 0:KEYS], P, EPS), "ssq_kv")
                    await_full(dve, "ssq_cq")
                    read(mean_eps(v[:, KEYS:], bank("ssq_cq")[:, 0:ROWS], 2 * P, EPS), "ssq_cq")
                    await_read(dve, "ssq_kv")
                    await_read(dve, "ssq_cq")
                if step < 3:
                    link(newton(v, r, t, [step]))
                    return
                nc.vector.scalar_tensor_tensor(kv_z[:], kv_z[:], col("kv_norm_g"), r[:, 0:KEYS], ALU.mult, ALU.mult)
                for c in range(2):
                    last = nc.vector.scalar_tensor_tensor(cq_z[:, c, :], cq_z[:, c, :], col("q_norm_g", c), r[:, KEYS:],
                                                          ALU.mult, ALU.mult)
                last.then_inc(s["kv_normed"], 1)

            conv_last = [0, 0]

            def conv_taps(lo, hi):
                for j in range(lo, hi):
                    k = CONF_K - 1 - j
                    for c in range(2):
                        w = col("conf_dw_w", 2 * k + c)
                        if j == 0:
                            ins = nc.vector.tensor_scalar(conv[:, c, :], glu[:, c, META:KEYS], w, col("conf_dw_b", c),
                                                          ALU.mult, ALU.add)
                        else:
                            r0 = max(0, j - META)
                            dve.wait_ge(dve_chain, conv_last[c])
                            ins = nc.vector.scalar_tensor_tensor(conv[:, c, r0:], glu[:, c, META + r0 - j:KEYS - j], w,
                                                                 conv[:, c, r0:], ALU.mult, ALU.add)
                        if j == CONF_K - 1 and c == 1:
                            dve.wait_ge(dve_chain, conv_last[0])
                            ins.then_inc(s["conv_done"], 1)
                        else:
                            conv_last[c] = count(ins)

            def short_conv():
                dve.wait_ge(s["sc_ready"], 1)
                last = [0, 0]
                for k in range(SC_K):
                    for c in range(2):
                        w = col("sc_dw_w", 2 * k + c)
                        src = sc_x[:, c, META - SC_K + 1 + k:KEYS - SC_K + 1 + k]
                        if k == 0:
                            last[c] = count(nc.vector.tensor_scalar(sc_acc[:, c, :], src, w, None, ALU.mult))
                        else:
                            dve.wait_ge(dve_chain, last[c])
                            last[c] = count(nc.vector.scalar_tensor_tensor(sc_acc[:, c, :], src, w, sc_acc[:, c, :],
                                                                           ALU.mult, ALU.add))
                await_out(dve, "z7")
                dve.wait_ge(dve_chain, last[1])
                link(nc.vector.tensor_tensor(sc_acc[:], sc_acc[:], sc_b[:], ALU.mult))
                await_out(dve, "z8")
                nc.vector.tensor_tensor(sc_acc[:], sc_acc[:], sc_gate[:], ALU.mult).then_inc(s["sc_u"], 1)

            rope = slice(NOPE, QK)

            def two_heads(a):
                return a.unsqueeze(1).to_broadcast([ROPE, 2, ROWS])

            def rotate_keys():
                dve.wait_ge(s["q_roped"], 4)
                await_full(dve, "krs")
                read(nc.vector.tensor_tensor(rope_t[rope, 0:KEYS], bank("krs")[rope, 0:KEYS], cst("sin", KEYS, rope), ALU.mult),
                     "krs")
                await_full(dve, "krc")
                read(nc.vector.tensor_tensor(kr_t[rope, :], bank("krc")[rope, 0:KEYS], cst("cos", KEYS, rope), ALU.mult), "krc")
                await_read(dve, "krs")
                await_read(dve, "krc")
                nc.vector.tensor_tensor(kr_t[rope, :], kr_t[rope, :], rope_t[rope, 0:KEYS], ALU.add).then_inc(s["kr_roped"], 1)

            for sl in over_slots(dve, 0, COUNT["z"], loops=0):
                lead(sl)
                if sl.at == 3:
                    trig_multiple()
                if sl.at == 4:
                    trig_reduce(slice(0, 2))
                if sl.at == 5:
                    trig_reduce(slice(2, None))
                if sl.at in (6, 7, 9, 10):
                    kvq_norm((6, 7, 9, 10).index(sl.at))
                if sl.at == 11:
                    dve.wait_ge(s["glu_ready"], 1)
                conv_taps(*Z_TAPS.get(sl.at, (0, 0)))
                if sl.at == 19:
                    short_conv()
                if sl.at == 22:
                    await_full(dve, "pool")
                    await_out(dve, "z9")
                    for c in range(2):
                        last = nc.vector.scalar_tensor_tensor(pool_gate[:, c, :], bank("pool")[:, c * ROWS:(c + 1) * ROWS],
                                                              col("pool_scale", c), pool_gate[:, c, :], ALU.mult, ALU.mult)
                    read(last, "pool")
                if sl.at == 24:
                    dve.wait_ge(s["sc_rounded"], 1)
                    rest(u_sc_lo[:], sc_acc[:], u_sc_hi[:]).then_inc(s["sc_split"], 1)
                    rotate_keys()

            gated = [0]

            def gate_out(b, i):
                name = "y_%s%d" % (b, i)
                if b == "sc":
                    taken(nc.vector.tensor_tensor(halves(m, i), out_t(name), halves(gates, i), ALU.mult), name)
                    return
                if b == "mla" and i >= 2:
                    dve.wait_ge(s["m_ready"], i - 1)
                elif b != "mla" and gated[0] >= 2:
                    dve.wait_ge(s["m_added"], gated[0] - 1)
                taken(nc.vector.tensor_tensor(y_gated[:, gated[0] % 2], out_t(name), halves(gates, i), ALU.mult), name)
                gated[0] += 1

            def conf_centre():
                await_full(dve, "conf_mean")
                for c in range(2):
                    last = nc.vector.scalar_tensor_tensor(conv[:, c, :], bank("conf_mean")[:, 0:ROWS], -1.0 / (2 * P),
                                                          conv[:, c, :], ALU.mult, ALU.add)
                read(last, "conf_mean")

            def conf_norm(step):
                v, r, t = [a[:, 0:ROWS] for a in kvq_rs]
                if step == 0:
                    await_full(dve, "conf_var")
                    read(mean_eps(v, bank("conf_var")[:, 0:ROWS], 2 * P, EPS), "conf_var")
                    await_read(dve, "conf_var")
                link(newton(v, r, t, [step]))
                if step < 2:
                    return
                for c in range(2):
                    last = nc.vector.scalar_tensor_tensor(conv[:, c, :], conv[:, c, :], col("conf_ln_g", c), r, ALU.mult, ALU.mult)
                last.then_inc(s["conf_zn"], 1)

            def conf_operand():
                dve.wait_ge(s["conf_sig"], 1)
                for c in range(2):
                    last = nc.vector.scalar_tensor_tensor(conv[:, c, :], conv[:, c, :], col("conf_ln_b", c), conf_sq[:, c, :],
                                                          ALU.add, ALU.mult)
                link(last)
                nc.vector.tensor_tensor(conv[:], conv[:], conf_gate[:], ALU.mult).then_inc(s["conf_u"], 1)

            halves_taken = [0]

            def take_out(b, h):
                halves_taken[0] += 1
                dve.wait_ge(s["y_first"], halves_taken[0])
                gate_out(b, 2 * h)
                slot_done(dve, "y_%s%d" % (b, h), 0)
                gate_out(b, 2 * h + 1)

            for sl in over_slots(dve, FIRST["gate_sc"], 8, loops=0):
                lead(sl)
                if sl.index == 0:
                    dve.wait_ge(s["pool_rounded"], 1)
                    rest(u_pool_lo[:], pool_gate[:], u_pool_hi[:]).then_inc(s["pool_split"], 1)
                elif sl.index <= 6:
                    conv_taps(17 + 2 * sl.index, 19 + 2 * sl.index)
            for before, b in (("sc", "pool"), ("pool", "conf")):
                for h in range(2):
                    take_out(before, h)
                    lead(Slot(FIRST["y_%s%d" % (before, h)], 0, None))
                    stage = "gate_%s%d" % (b, h)
                    for sl in over_slots(dve, FIRST[stage], 4, loops=0):
                        lead(sl)
                        if stage == "gate_pool1" and sl.index == 0:
                            conf_centre()
                        if stage == "gate_conf0" and sl.index < 3:
                            conf_norm(sl.index)
                        if stage == "gate_conf1" and sl.index == 0:
                            conf_operand()
                        if stage == "gate_conf1" and sl.index == 2:
                            dve.wait_ge(s["conf_rounded"], 1)
                            rest(u_conf_lo[:], conv[:], u_conf_hi[:]).then_inc(s["conf_split"], 1)

            def masked_max(i, name, n0, sc, scale, mask, done):
                n = sc.shape[-1]
                await_full(dve, name)
                read(nc.vector.scalar_tensor_tensor(sc, bank(name)[:, 0:n], scale, cst(mask, n), ALU.mult, ALU.add), name)
                await_read(dve, name)
                nc.vector.tensor_reduce(neg_max[:, i % 2, 0:1], sc[:, 0:n0], AX.X, ALU.max, negate=True)
                nc.vector.tensor_reduce(neg_max[:, i % 2, 1:2], sc[:, n0:], AX.X, ALU.max, negate=True).then_inc(done, 1)

            def normalise(i, pr, n0, exp_done, done):
                dve.wait_ge(exp_done, i + 1)
                link(nc.vector.reciprocal(inv_sum[:, i % 2, :], sums[:, i % 2, :]))
                nc.vector.tensor_scalar(pr[:, 0:n0], pr[:, 0:n0], inv_sum[:, i % 2, 0:1], None, ALU.mult)
                nc.vector.tensor_scalar(pr[:, n0:], pr[:, n0:], inv_sum[:, i % 2, 1:2], None, ALU.mult).then_inc(done, 1)

            def mla_norm(i):
                normalise(i, probs[:, i % 2, :], S0, s["exp_done"], s["probs_ready"])

            def mla_gated(i):
                dve.wait_ge(s["heads_done"], 2 * i + 2)
                taken(nc.vector.tensor_tensor(u_mla[:, i, :], acc[:, pair("heads%d" % i), 0, 0:ROWS], mla_gate[:, i, :],
                                              ALU.mult), "heads%d" % i)

            def mla_rest(i):
                dve.wait_ge(s["u_mla_rounded"], i + 1)
                rest(u_mla_lo[:, i, :], u_mla[:, i, :], u_mla_hi[:, i, :]).then_inc(s["u_mla_split"], 1)

            for n in range(HEADS + 2):
                if n in (5, 7, 9):
                    mla_gated((n - 5) // 2)
                if 1 <= n <= HEADS:
                    mla_norm(n - 1)
                if n % 5 == 0:
                    take_out("conf", n // 5)
                if n < HEADS:
                    masked_max(n, "s%d" % n, S0, scores[:, n % 2, :], float(QK) ** -0.5, "mask_mla", s["max_ready"])
                lead(Slot(FIRST["y_conf0"] + n, n, None))
                if n in (7, 9):
                    mla_rest((n - 7) // 2)
            mla_gated(3)
            mla_rest(2)
            mla_rest(3)
            dve.wait_ge(s["m_added"], 8)
            dve.wait_ge(s["mla_gates"], 3)
            for i in range(5):
                if i < 4:
                    slot_done(dve, "y_mla", i)
                    gate_out("mla", i)
                    await_out(dve, "y_mla%d" % i)
                    nc.vector.tensor_tensor(halves(m, i), halves(m, i), y_gated[:, (gated[0] - 1) % 2],
                                            ALU.add).then_inc(s["m_ready"], 1)
                if i >= 1:
                    dve.wait_ge(s["m_rounded"], i)
                    rest(halves(m_lo, i - 1), halves(m, i - 1), halves(m_hi, i - 1)).then_inc(s["m_split"], 1)
            handed_back("w_o")
            def post_gain(t, hf):
                name = "w_o%d" % hf
                cols = slice(hf * 512, hf * 512 + 512)
                ins = nc.vector.tensor_tensor(y[:, t, cols], acc[:, pair(name), t, :], gain[:, cols], ALU.mult)
                if t == TILES - 1:
                    taken(ins, name)
                else:
                    count(ins)

            def rest_rows(tag, us):
                for u in us:
                    t, j = u // 2, u % 2
                    dve.wait_ge(s["x_rounded"], 4 * (int(tag[1]) - 1) + TURN_ORDER.index(u) + 1)
                    read(rest(x_lo[:, 4 * j:4 * j + 4, t * P:t * P + P], bank("%s_%d" % (tag, u))
                              .rearrange("p (c r) -> p c r", c=4), x_hi[:, 4 * j:4 * j + 4, t * P:t * P + P]), "%s_%d" % (tag, u))

            dve.wait_ge(s["gain_loaded"], 16)
            for sl in over_slots(dve, FIRST["w_o"], 5, loops=0):
                lead(sl)
                if sl.index == 3:
                    dve.wait_ge(s["wo_ssq"], 1)
                    for t in range(TILES):
                        post_gain(t, 0)
            for t in range(TILES):
                dve.wait_ge(s["wo_ssq"], t + 2)
                v, r, u = [rs[:, i, t:t + 1] for i in range(3)]
                link(nc.vector.tensor_tensor(u, ssq[:, 2 * t:2 * t + 1], ssq[:, 2 * t + 1:2 * t + 2], ALU.add))
                link(mean_eps(v, u, DM, EPS))
                newton_col(v, r, u, lambda step: post_gain(t, 1) if step == 0 else None)
                if t == TILES - 1:
                    await_out(dve, "w_o0")
                    await_out(dve, "w_o1")
                for hf in range(2):
                    cols = slice(hf * 512, hf * 512 + 512)
                    nc.vector.scalar_tensor_tensor(x[:, t, cols], y[:, t, cols], r, x[:, t, cols], ALU.mult,
                                                   ALU.add).then_inc(s["x_ready%d" % t], 1)
                    if t == 1 and hf == 0:
                        rest_rows("x1", [0])

            def residual(t, name, hf):
                cols = slice(hf * 512, hf * 512 + 512)
                ins = nc.vector.scalar_tensor_tensor(y[:, t, cols], x[:, t, cols], ALPHA, acc[:, pair(name), t, :], ALU.mult, ALU.add)
                if t == TILES - 1:
                    taken(ins, name)
                    return None
                return count(ins)

            def moments(t, name, hf, written):
                if t == TILES - 1:
                    await_out(dve, name)
                else:
                    dve.wait_ge(dve_chain, written)
                return nc.vector.bn_stats(stats[:, t, hf, :], y[:, t, hf * 512:hf * 512 + 512])

            def residual_moments(t, name, hf):
                link(moments(t, name, hf, residual(t, name, hf)))

            def norm_tile(k, t, beside=lambda step: None):
                mean, var = mu_var[:, t, 0:1], mu_var[:, t, 1:2]
                v, r, u = [rs[:, i, t:t + 1] for i in range(3)]

                def centre(q):
                    cols = slice(q * 256, q * 256 + 256)
                    nc.vector.scalar_tensor_tensor(y[:, t, cols], y[:, t, cols], mean, gain[:, cols], ALU.subtract, ALU.mult)

                link(nc.vector.bn_aggr(mu_var[:, t, :], stats[:, t].rearrange("p h e -> p (h e)")))
                link(nc.vector.tensor_scalar(v, var, LN_EPS, None, ALU.add))
                if t == 0:
                    newton_col(v, r, u, beside)
                    nc.vector.scalar_tensor_tensor(u, mean, -1.0, r, ALU.mult, ALU.mult).then_inc(s["rstd_tile0"], 1)
                    return
                dve.wait_ge(s["norm_loaded"], 32 * (k + 1))
                newton_col(v, r, u, centre)
                for hf in range(2):
                    cols = slice(hf * 512, hf * 512 + 512)
                    nc.vector.scalar_tensor_tensor(x[:, t, cols], y[:, t, cols], r, shift[:, cols], ALU.mult,
                                                   ALU.add).then_inc(s["x_ready1"], 1)
                    if hf == 0 and k < 3:
                        rest_rows("x%d" % (k + 2), [0])

            rest_rows("x1", [2, 1, 3])
            handed_back("gla_gk")
            for stage in ("gla_gk", "gla_q"):
                for sl in over_slots(dve, FIRST[stage], COUNT[stage]):
                    lead(sl)
            for sl in over_slots(dve, FIRST["gla_k"], 4, loops=0):
                lead(sl)
                if sl.index == 0:
                    for j in range(2):
                        dve.wait_ge(s["la_abs"], j + 1)
                        for i in range(2):
                            c = 2 * j + i
                            last = nc.vector.tensor_scalar(la[:, c, :], bank("la%d" % j)[:, i * ROWS:(i + 1) * ROWS],
                                                           col("gla_b_gk_2", c), 0.0, ALU.add, ALU.min)
                        read(last, "la%d" % j)
                    dve.wait_ge(s["la_log"], 1)
                    await_read(dve, "la0")
                    await_read(dve, "la1")
                    link(nc.vector.tensor_tensor(la[:], la[:], la_e[:], ALU.subtract))
                    dve.wait_ge(s["zeroed"], 1)
                    flat = "p h r -> p (h r)"
                    nc.vector.tensor_tensor_scan(la_e[:].rearrange(flat), reset[:].rearrange(flat), la[:].rearrange(flat), 0.0,
                                                 ALU.mult, ALU.add).then_inc(s["cum_ready"], 1)
                    dve.wait_ge(s["cum_ready"], 1)
                    chunks = la_e[:].rearrange("p h (n i) -> p (h n) i", i=CH)
                    nc.vector.tensor_tensor(la[:].rearrange("p h (n i) -> p (h n) i", i=CH),
                                            chunks[:, :, CH - 1:CH].to_broadcast([P, GLA_H * NCH, CH]), chunks,
                                            ALU.subtract).then_inc(s["end_ready"], 1)
            for sl in over_slots(dve, FIRST["gla_v"], 8, loops=0):
                lead(sl)
                if sl.index == 0:
                    await_out(dve, "gla_q0")
                    await_out(dve, "gla_q1")
                    dve.wait_ge(s["e_ready"], 3)
                    nc.vector.tensor_tensor(qd[:], gq[:], e_cum[:], ALU.mult).then_inc(s["qd_ready"], 1)
                if sl.index == 1:
                    await_out(dve, "gla_k0")
                    await_out(dve, "gla_k1")
                    nc.vector.tensor_tensor(ki[:], gk[:], e_inv[:], ALU.mult).then_inc(s["ki_ready"], 1)
                if sl.index == 2:
                    nc.vector.tensor_tensor(ke[:], gk[:], e_end[:], ALU.mult).then_inc(s["ke_ready"], 1)
            def gate_head(hd):
                if hd == 2:
                    dve.wait_ge(s["gg1_ready"], 1)
                else:
                    await_out(dve, "gla_g1")
                cols = slice(hd * DV, (hd + 1) * DV)
                nc.vector.tensor_tensor(gg[:, :, cols], gg[:, :, cols], y[:, :, cols], ALU.mult).then_inc(s["o_gated"], 1)

            def rest_gated(hf):
                for j in (2 * hf, 2 * hf + 1):
                    dve.wait_ge(s["o_rounded"], j + 1)
                    read(rest(halves(o_lo, j), bank("ot%d" % j).rearrange("p (c r) -> p c r", c=2), halves(o_hi, j)), "ot%d" % j)

            def states(hd):
                a, b = "upd%da" % hd, "upd%db" % hd
                await_full(dve, a)
                nc.vector.tensor_copy(state[:, hd, 0, :], bank(a)[:, 0:DV]).then_inc(s["state_ready"], 1)
                dve.wait_ge(s["state_ready"], hd + 1)
                read(nc.vector.scalar_tensor_tensor(state[:, hd, 1, :], state[:, hd, 0, :], e_cum[:, hd, 2 * CH - 1:2 * CH],
                                                    bank(a)[:, DV:2 * DV], ALU.mult, ALU.add), a)
                await_full(dve, b)
                await_read(dve, a)
                read(nc.vector.scalar_tensor_tensor(state[:, hd, 2, :], state[:, hd, 1, :], e_cum[:, hd, 3 * CH - 1:3 * CH],
                                                    bank(b)[:, 0:DV], ALU.mult, ALU.add), b)

            for sl in over_slots(dve, FIRST["gla_g"], 8, loops=0):
                if sl.index == 2:
                    states(0)
                    states(1)
                lead(sl)
                if sl.index == 2:
                    states(2)
                    states(3)
                if sl.index == 4:
                    dve.wait_ge(s["o_ssq"], 8)
                    link(mean_eps(rs[:, 0, :], ssq[:], DV, EPS))
                    link(newton(rs[:, 0, :], rs[:, 1, :], rs[:, 2, :]))
                    dve.wait_ge(s["gg0_ready"], 1)
                    for j in (0, 2, 1, 3):
                        for i in range(2):
                            hd = j % 2 * 2 + i
                            cols = slice(hd * DV, (hd + 1) * DV)
                            dst, by = (gg, gg[:, j // 2, cols]) if hd < 2 else (y, head_gain[:])
                            last = nc.vector.scalar_tensor_tensor(dst[:, j // 2, cols], bank("o%d" % j)[:, i * DV:(i + 1) * DV],
                                                                  rs[:, 1, 2 * j + i:2 * j + i + 1], by, ALU.mult, ALU.mult)
                        read(last, "o%d" % j)
                if sl.index == 7:
                    rest_gated(0)
            for j in (1, 3):
                await_read(dve, "o%d" % j)
            gate_head(2)
            gate_head(3)

            def out_stage(stage, k):
                lent = 0
                if stage == "gla_out":
                    rest_gated(1)
                    lent = 3
                    dve.wait_ge(split, FIRST[stage] + LEAD + lent)
                for sl in over_slots(dve, FIRST[stage], 5, loops=0):
                    if sl.index >= lent:
                        lead(sl)
                    if stage == "moba_out" and sl.index < 2:
                        moba_rest(2 + sl.index)
                    if sl.index == 3:
                        slot_done(dve, stage, 3)
                        for t in range(TILES):
                            residual_moments(t, stage + "0", 0)
                dve.wait_ge(s["tile0_done"], TAILS[stage])
                for t in range(TILES):
                    if t == 1:
                        slot_done(dve, stage, 7)
                    residual_moments(t, stage + "1", 1)
                    norm_tile(k, t)

            out_stage("gla_out", 0)

            def swiglu(layer):
                tag = "gu%d" % layer
                og = OUT[tag + "_0"]
                for sl in over_slots(dve, FIRST[tag], COUNT[tag]):
                    lead(sl)
                    if sl.index == 3:
                        dve.wait_ge(weights_used, sl.number(1))
                        dve.wait_ge(evacuated[og % 2], sl.loop + (og // 2 + 1))
                        nc.vector.tensor_tensor(hidden[:], h_gate[:], acc[:, (og + 1) % 2, :, 0:ROWS],
                                                ALU.mult).then_inc(evacuated[(og + 1) % 2], 1)
                        dve.wait_ge(s["h_rounded"], sl.loop + (layer * (FCH // 2) + 1))
                        rest(h_lo[:, bass.ds(sl.loop * 2, 2), :], hidden[:],
                             h_hi[:, bass.ds(sl.loop * 2, 2), :]).then_inc(s["h_split"], 1)
                stage = "down%d" % layer
                for sl in over_slots(dve, FIRST[stage], COUNT[stage] - 3, loops=4):
                    lead(sl)
                names = ["%s_%d" % (stage, hf) for hf in range(2)]
                for hf in range(2):
                    dve.wait_ge(s["down_part"], 3 * layer + hf + 1)
                    residual_moments(0, names[hf], hf)

                def tile1_half0(step):
                    if step == 0:
                        dve.wait_ge(s["down_part"], 3 * layer + 3)
                        residual(1, names[0], 0)
                    if step == 1:
                        count(moments(1, names[0], 0, None))

                norm_tile(2 * layer + 1, 0, tile1_half0)
                slot_done(dve, stage, COUNT[stage] - 1)
                residual_moments(1, names[1], 1)
                norm_tile(2 * layer + 1, 1)

            rest_rows("x2", [2, 1, 3])
            handed_back("gu0")
            swiglu(0)
            rest_rows("x3", [2, 1, 3])
            handed_back("moba_q")
            r32 = slice(0, ROPE)

            def moba_rotate(src, swap, swapped, done, pairs):
                t = mrope[r32, :].rearrange("p (h r) -> p h r", h=2)
                for j in pairs:
                    hs = slice(2 * j, 2 * j + 2)
                    dve.wait_ge(s["swapped_%s%d" % (swapped, j // 2)], 32)
                    nc.vector.tensor_tensor(t, swap[r32, hs, :], two_heads(trig[r32, 1, :]), ALU.mult)
                    link(nc.vector.tensor_tensor(src[r32, hs, :], src[r32, hs, :], two_heads(trig[r32, 0, :]), ALU.mult))
                    nc.vector.tensor_tensor(src[r32, hs, :], src[r32, hs, :], t, ALU.add).then_inc(done, 1)
                    dve.wait_ge(done, j + 1)

            for sl in over_slots(dve, FIRST["moba_q"], 8):
                lead(sl)
            dve.wait_ge(s["trig_ready"], 1)
            for sl in over_slots(dve, FIRST["moba_k"], 8, loops=0):
                lead(sl)
                if sl.index < 2:
                    moba_rotate(mq, mq_swap, "q", s["mq_roped"], [sl.index])
                if sl.index >= 6:
                    moba_rotate(mk, mk_swap, "k", s["mk_roped"], [sl.index - 6])

            def moba_norm(i):
                normalise(i, mprobs[:, i % 2, :], P, s["m_exp"], s["m_probs"])

            def moba_rest(i):
                name = "moba_heads%d" % (i // 2)
                dve.wait_ge(s["mo_rounded"], i + 1)
                rest(halves(mo_lo, i), acc[:, pair(name), i % 2, :].rearrange("p (h r) -> p h r", h=2),
                     halves(mo_hi, i)).then_inc(evacuated[pair(name)] if i % 2 else s["mo_split"], 1)

            for i in range(HEADS):
                if i >= 1:
                    moba_norm(i - 1)
                if i == HEADS - 1:
                    moba_rest(0)
                    moba_rest(1)
                masked_max(i, "ms%d" % i, P, mscores[:, i % 2, :], float(HD) ** -0.5, "mask_moba", s["m_max"])
                lead(Slot(FIRST["moba_v"] + i, i, None))
            moba_norm(HEADS - 1)
            out_stage("moba_out", 2)
            rest_rows("x4", [2, 1, 3])
            handed_back("gu1")
            swiglu(1)

        @block.gpsimd
        def _(pool):
            chained = [0]

            def link(ins):
                chained[0] += 1
                ins.then_inc(pool_chain, 1)
                pool.wait_ge(pool_chain, chained[0])

            def rotate(dst, swap, rows, j, tmp, cos, sin, done, number):
                hs = slice(2 * j, 2 * j + 2)
                t = tmp[rows, :].rearrange("p (h r) -> p h r", h=2)
                nc.gpsimd.tensor_tensor(t, swap[rows, hs, :], sin.unsqueeze(1).to_broadcast([ROPE, 2, ROWS]), ALU.mult)
                link(nc.gpsimd.tensor_tensor(dst[rows, hs, :], dst[rows, hs, :], cos.unsqueeze(1).to_broadcast([ROPE, 2, ROWS]),
                                             ALU.mult))
                nc.gpsimd.tensor_tensor(dst[rows, hs, :], dst[rows, hs, :], t, ALU.add).then_inc(done, 1)
                pool.wait_ge(done, number)

            nc.gpsimd.memset(ssq[:], 0.0).then_inc(s["cleared"], 1)
            nc.gpsimd.memset(w_pool[:], 0.0).then_inc(s["cleared"], 1)
            nc.gpsimd.memset(half_pi[:], float(np.pi / 2)).then_inc(s["cleared"], 1)
            nc.gpsimd.memset(vt[:, 0, :], 0.0).then_inc(s["cleared"], 1)
            await_out(pool, "z2")
            src, reach = pool_v, 1
            for g, dst in enumerate((pool_a, pool_b, pool_a, pool_b)):
                w = 2 * reach
                lo = w - 1
                link(nc.gpsimd.tensor_tensor(dst[:, :, lo:], src[:, :, lo:], src[:, :, lo - reach:KEYS - reach], ALU.add))
                r = slice(g % 2 * 64, g % 2 * 64 + 64)
                link(nc.gpsimd.tensor_scalar(pooled[r, g // 2, :], dst[r, g // 2, META:], 1.0 / w, None, ALU.mult))
                ins = nc.gpsimd.tensor_tensor(pooled[r, g // 2, :], pooled[r, g // 2, :], pool_v[r, g // 2, META:], ALU.subtract)
                if g < 3:
                    link(ins)
                else:
                    ins.then_inc(s["pooled_ready"], 1)
                src, reach = dst, w
            pool.wait_ge(s["pooled_ready"], 1)
            await_out(pool, "z3")
            await_out(pool, "z4")
            nc.gpsimd.tensor_tensor(glu[:], glu[:], glu_g[:], ALU.mult).then_inc(s["glu_ready"], 1)
            await_out(pool, "z5")
            await_out(pool, "z6")
            nc.gpsimd.tensor_tensor(sc_x[:], sc_c[:], sc_x[:], ALU.mult).then_inc(s["sc_ready"], 1)
            for j in range(4):
                await_read(pool, "uq%d" % j)
            a, b = slice(NOPE, NOPE + ROPE // 2), slice(NOPE + ROPE // 2, QK)
            pool.dma_start(q_swap[a, :, :], qT[b, :, :]).then_inc(s["q_swapped"], 16)
            pool.dma_start(q_swap[b, :, :], qT[a, :, :]).then_inc(s["q_swapped"], 16)
            pool.wait_ge(s["sc_ready"], 1)
            pool.wait_ge(s["tables_loaded"], 16)
            rope = slice(NOPE, QK)
            pool.wait_ge(s["q_swapped"], 32)
            for j in range(4):
                rotate(qT, q_swap, rope, j, rope_t, cst("cos", KEYS, rope)[:, META:], cst("sin", KEYS, rope)[:, META:],
                       s["q_roped"], j + 1)
            pool.wait_ge(s["kr_roped"], 1)
            for i in range(HEADS):
                last = nc.gpsimd.tensor_copy(kT[NOPE:QK, i, :], kr_t[NOPE:QK, :])
            last.then_inc(s["k_spread"], 1)
            pool.wait_ge(s["k_spread"], 1)
            pool.wait_ge(s["sc_split"], 1)
            pool.wait_ge(s["pool_split"], 1)
            nc.gpsimd.memset(metaT[:], 0.0).then_inc(s["meta_cleared"], 1)
            n = 0
            for b in ("pool", "conf"):
                for i in range(4):
                    await_out(pool, "y_%s%d" % (b, i))
                    if n >= 4:
                        pool.wait_ge(s["m_added"], n - 3)
                    nc.gpsimd.tensor_tensor(m[:, 2 * i:2 * i + 2, :], m[:, 2 * i:2 * i + 2, :], y_gated[:, n % 2],
                                            ALU.add).then_inc(s["m_added"], 1)
                    n += 1

            def lend(first, count):
                for at in range(first, min(first + count, TOTAL)):
                    k = at % RING
                    pool.wait_ge(rounded, at + 1)
                    pool.wait_ge(split, at)
                    nc.gpsimd.tensor_tensor(w_lo[:, k, :], staged[:, k, :], w_hi[:, k, :].bitcast(F32),
                                            ALU.subtract).then_inc(split, 1)

            def load_norm(k):
                pool.wait_ge(s["x_ready0"], 2 * k + 2)
                pool.wait_ge(s["x_ready1"], 2 * k + 2)
                pool.dma_start(gain[:], d["ln_g_2"][k // 2, k % 2].partition_broadcast(P)).then_inc(s["norm_loaded"], 16)
                pool.dma_start(shift[:], d["ln_b_2"][k // 2, k % 2].partition_broadcast(P)).then_inc(s["norm_loaded"], 16)

            lend(FIRST["y_mla"] + LEAD, 4)
            lend(FIRST["gla_gk"], LEAD)
            load_norm(0)
            link(nc.gpsimd.memset(reset[:], 1.0))
            nc.gpsimd.memset(reset[:].rearrange("p h (n i) -> p (h n) i", i=CH)[:, :, 0:1], 0.0).then_inc(s["zeroed"], 1)
            nc.gpsimd.memset(intra[:], 0.0).then_inc(s["zeroed"], 1)
            nc.gpsimd.memset(ke_half[:], 0.0).then_inc(s["zeroed"], 1)
            nc.gpsimd.memset(qd_half[:], 0.0).then_inc(s["zeroed"], 1)
            pool.wait_ge(s["qd_ready"], 1)
            pool.wait_ge(s["zeroed"], 4)
            for c in range(2):
                view = "p h (t c i) -> p (h t) c i"
                nc.gpsimd.tensor_copy(qd_half[:, c].rearrange(view, t=TILES, c=2)[:, :, c, :],
                                      qd[:].rearrange(view, t=TILES, c=2)[:, :, c, :]).then_inc(s["half_ready"], 1)
            await_read(pool, "sg0")
            await_read(pool, "sg1")
            pool.wait_ge(s["half_ready"], 2)
            for c in range(2):
                if c == 1:
                    pool.wait_ge(s["intra_ready"], 1)
                blk = intra[c * CH:c * CH + CH, :, c * CH:c * CH + CH]
                nc.gpsimd.affine_select(out=blk, in_=blk, pattern=[[0, GLA_H * TILES], [1, CH]], compare_op=ALU.is_ge, fill=0.0,
                                        base=0, channel_multiplier=-1).then_inc(s["intra_ready"], 1)
            pool.wait_ge(s["gk_loaded"], 32)
            pool.wait_ge(s["intra_ready"], 2)
            await_out(pool, "gla_g0")
            for t in range(TILES):
                g = gg[:, t, 0:512].rearrange("p (h e) -> p h e", h=2)
                last = nc.gpsimd.tensor_tensor(g, g, head_gain[:].unsqueeze(1).to_broadcast([P, 2, DV]), ALU.mult)
            last.then_inc(s["gg0_ready"], 1)
            lend(FIRST["gla_out"] + LEAD, 3)
            def norm_tile0(k, halves=range(2)):
                pool.wait_ge(s["norm_loaded"], 32 * (k + 1))
                for hf in halves:
                    cols = slice(hf * 512, hf * 512 + 512)
                    pool.wait_ge(s["scaled0"], 2 * k + hf + 1)
                    link(nc.gpsimd.tensor_tensor(y[:, 0, cols], y[:, 0, cols], gain[:, cols], ALU.mult))
                    nc.gpsimd.tensor_tensor(x[:, 0, cols], y[:, 0, cols], shift[:, cols], ALU.add).then_inc(s["x_ready0"], 1)

            for k, stage in enumerate(("gu0", "moba_q", "gu1")):
                lend(FIRST[stage], 1)
                norm_tile0(k)
                lend(FIRST[stage] + 1, LEAD - 1)
                load_norm(k + 1)
                if stage == "moba_q":
                    def swap_halves(name, src, swap, j):
                        hs = slice(4 * j, 4 * j + 4)
                        for i in (2 * j, 2 * j + 1):
                            await_out(pool, "moba_%s%d" % (name, i))
                        for i in range(2):
                            to, of = slice(i * ROPE // 2, (i + 1) * ROPE // 2), slice((1 - i) * ROPE // 2, (2 - i) * ROPE // 2)
                            pool.dma_start(swap[to, hs, :], src[of, hs, :]).then_inc(s["swapped_%s%d" % (name, j)], 16)

                    r32 = slice(0, ROPE)

                    def rotate_heads(name, src, swap, j):
                        pool.wait_ge(s["swapped_%s1" % name], 32)
                        rotate(src, swap, r32, j, mrope_pool, trig[r32, 0, :], trig[r32, 1, :], s["m%s_roped_pool" % name], j - 1)

                    swap_halves("q", mq, mq_swap, 0)
                    swap_halves("q", mq, mq_swap, 1)
                    rotate_heads("q", mq, mq_swap, 2)
                    swap_halves("k", mk, mk_swap, 0)
                    rotate_heads("q", mq, mq_swap, 3)
                    swap_halves("k", mk, mk_swap, 1)
                    rotate_heads("k", mk, mk_swap, 2)
                    rotate_heads("k", mk, mk_swap, 3)
            norm_tile0(3)


_NAMES = ["x", "meta_tokens", "pre_norm_g", "w_in", "gate_bias", "pool_w", "pool_scale", "w_out_pool", "q_norm_g", "w_uq",
          "kv_norm_g", "w_ukv", "w_out_mla", "conf_dw_w", "conf_dw_b", "conf_ln_g", "conf_ln_b", "w_out_conf", "sc_dw_w",
          "w_out_sc", "w_o", "post_norm_g", "positions_2", "gla_w_in_2", "gla_w_gk_2", "gla_b_gk_2", "gla_norm_g_2",
          "gla_w_out_2", "moba_w_in_2", "moba_w_out_2", "ffn_w_gu_2", "ffn_w_down_2", "ln_g_2", "ln_b_2"]


def kernel(**inputs):
    import concourse.bacc as bacc
    from concourse.bass_utils import run_bass_kernel_spmd

    nc = bacc.Bacc("TRN2", target_bir_lowering=False, num_devices=1)
    arrays = {n: np.ascontiguousarray(inputs[n]) for n in _NAMES}
    arrays["constants"] = constants()
    d = {n: nc.dram_tensor("in_" + n, a.shape, mybir.dt.from_np(a.dtype), kind="ExternalInput").ap()
         for n, a in arrays.items()}
    out = nc.dram_tensor("out", (1, ROWS, DM), F32, kind="ExternalOutput").ap()
    hybrid_stack(nc, d, out)
    r = run_bass_kernel_spmd(nc, [{"in_" + n: a for n, a in arrays.items()}], core_ids=[0])
    return r.results[0]["out"]
```
